# Optimizing a Trainium2 kernel written in Bass

```python
import math
import jax, jax.numpy as jnp
from jax import lax
import numpy as np

D_MODEL = 1024
BATCH = 1
SEQ = 128
DEPTH = 2
DEC_BATCH = 1
DEC_SEQ = 512
PAST_LEN = 128

GRID_W = 64
HY_W = 256
HY_ORDER = 2
N_BANDS = 8
POS_EMB = 1 + 2 * N_BANDS
FILT_HID = 64
N_HEADS = 8
Q_LORA = 256
KV_LORA = 128
NOPE_DIM = 64
ROPE_DIM = 32
V_DIM = 64
ROPE_BASE = 10000.0
Q_BLOCK = 128
FN_GROUPS = 4
FN_GROUP_W = 64
FN_W = FN_GROUPS * FN_GROUP_W
N_BRANCH = 3
D_FF = 2816
EPS = 1e-6
IN_COLS = 3 * HY_W + Q_LORA + KV_LORA + ROPE_DIM + FN_W + N_BRANCH * D_MODEL

kernel_name = 'hybrid_hyena_mla_fnet_diffusion_step'

def rmsnorm(x, g):
    x32 = x.astype(jnp.float32)
    y = x32 * lax.rsqrt(jnp.mean(x32 * x32, axis=-1, keepdims=True) + EPS)
    return (y * g.astype(jnp.float32)).astype(x.dtype)

def swiglu(x, w_up, w_down):
    g, u = jnp.split(x @ w_up, 2, axis=-1)
    return (jax.nn.silu(g) * u) @ w_down

def short_conv(u, w, b):
    up = jnp.pad(u, ((0, 0), (1, 1), (0, 0)))
    return up[:, :-2] * w[0] + up[:, 1:-1] * w[1] + up[:, 2:] * w[2] + b

def hyena_filters(L, w1, b1, w2, b2, w3):
    f32 = jnp.float32
    t_idx = jnp.arange(L, dtype=f32)
    t_norm = t_idx / (L - 1)
    w = 2.0 * math.pi * t_idx / L
    bands = jnp.linspace(1e-4, N_BANDS - 1, N_BANDS, dtype=f32)
    ang = w[:, None] * bands[None, :]
    feats = jnp.concatenate([t_norm[:, None], jnp.cos(ang), -jnp.sin(ang)], axis=-1)
    h = jnp.sin(feats @ w1.astype(f32) + b1.astype(f32))
    h = jnp.sin(h @ w2.astype(f32) + b2.astype(f32))
    h = (h @ w3.astype(f32)).reshape(L, 2, HY_ORDER, HY_W)
    deltas = jnp.linspace(math.log(1e-2) / 1.5, math.log(1e-2) / 0.3, HY_W, dtype=f32)
    decay = jnp.exp(-t_norm[:, None] * jnp.abs(deltas)[None, :])
    h = h * decay[:, None, None, :]
    h_fwd, h_bwd = h[:, 0], h[:, 1]
    filt = jnp.concatenate([h_fwd, jnp.zeros((1, HY_ORDER, HY_W), f32), h_bwd[1:][::-1]], axis=0)
    filt = filt / (jnp.sum(jnp.abs(filt), axis=0, keepdims=True) + EPS)
    return jnp.fft.rfft(filt, axis=0)

def fftconv(u, filt_f, skip):
    L = u.shape[1]
    u32 = u.astype(jnp.float32)
    U = jnp.fft.rfft(u32, n=2 * L, axis=1)
    y = jnp.fft.irfft(U * filt_f[None], n=2 * L, axis=1)[:, :L]
    return (y + u32 * skip.astype(jnp.float32)).astype(u.dtype)

def hyena_mixer(u, conv_w, conv_b, w1, b1, w2, b2, w3, skip):
    L = u.shape[1]
    u = short_conv(u, conv_w, conv_b)
    x1, x2, v = jnp.split(u, 3, axis=-1)
    filt_f = hyena_filters(L, w1, b1, w2, b2, w3)
    z = x1 * fftconv(v, filt_f[:, 0], skip[0])
    z = x2 * fftconv(z, filt_f[:, 1], skip[1])
    return z

def axial_angles(rows_n):
    f32 = jnp.float32
    rows = jnp.repeat(jnp.arange(rows_n, dtype=f32), GRID_W)
    cols = jnp.tile(jnp.arange(GRID_W, dtype=f32), rows_n)
    n_freq = ROPE_DIM // 4
    inv = ROPE_BASE ** (-jnp.arange(n_freq, dtype=f32) / n_freq)
    return rows[:, None] * inv[None, :], cols[:, None] * inv[None, :]

def rotate_block(x, ang):
    c = jnp.cos(ang)[:, None, :]
    s = jnp.sin(ang)[:, None, :]
    x1, x2 = jnp.split(x, 2, axis=-1)
    return jnp.concatenate([x1 * c - x2 * s, x2 * c + x1 * s], axis=-1)

def axial_rope(x, ang_r, ang_c):
    xr, xc = jnp.split(x, 2, axis=-1)
    return jnp.concatenate([rotate_block(xr, ang_r), rotate_block(xc, ang_c)], axis=-1).astype(x.dtype)

def blocked_attention(q, k, v):
    B, Lq, H, dq = q.shape
    nb = Lq // Q_BLOCK
    scale = 1.0 / math.sqrt(dq)
    qb = q.reshape(B, nb, Q_BLOCK, H, dq).transpose(1, 0, 2, 3, 4)

    def one_block(qi):
        s = jnp.einsum('bqhd,bkhd->bhqk', qi, k).astype(jnp.float32) * scale
        p = jax.nn.softmax(s, axis=-1).astype(v.dtype)
        return jnp.einsum('bhqk,bkhd->bqhd', p, v)

    o = lax.map(one_block, qb)
    return o.transpose(1, 0, 2, 3, 4).reshape(B, Lq, H * v.shape[-1])

def token_mix(n, l, P, rope_ang, ctx_ckv, ctx_krope):
    B, L, _ = n.shape
    proj = n @ P['w_in'][l]
    i0 = 3 * HY_W
    i1 = i0 + Q_LORA
    i2 = i1 + KV_LORA
    i3 = i2 + ROPE_DIM
    i4 = i3 + FN_W
    hy, q_a, kv_a, k_r, fn, gates = jnp.split(proj, [i0, i1, i2, i3, i4], axis=-1)

    y_a = hyena_mixer(hy, P['hy_conv_w'][l], P['hy_conv_b'][l], P['hy_filt_w1'][l], P['hy_filt_b1'][l],
                      P['hy_filt_w2'][l], P['hy_filt_b2'][l], P['hy_filt_w3'][l], P['hy_skip'][l]) @ P['w_hy_out'][l]

    q = (rmsnorm(q_a, P['q_norm_g'][l]) @ P['w_qb'][l]).reshape(B, L, N_HEADS, NOPE_DIM + ROPE_DIM)
    q_nope, q_rope = jnp.split(q, [NOPE_DIM], axis=-1)
    ckv = rmsnorm(kv_a, P['kv_norm_g'][l])
    k_rope = k_r[:, :, None, :]
    if rope_ang is not None:
        q_rope = axial_rope(q_rope, rope_ang[0], rope_ang[1])
        k_rope = axial_rope(k_rope, rope_ang[0], rope_ang[1])
    kv = (ckv @ P['w_kvb'][l]).reshape(B, L, N_HEADS, NOPE_DIM + V_DIM)
    k_nope, v = jnp.split(kv, [NOPE_DIM], axis=-1)
    if ctx_ckv is not None:
        Lc = ctx_ckv.shape[1]
        kv_c = (ctx_ckv @ P['w_kvb'][l]).reshape(B, Lc, N_HEADS, NOPE_DIM + V_DIM)
        k_nope = jnp.concatenate([k_nope, kv_c[..., :NOPE_DIM]], axis=1)
        v = jnp.concatenate([v, kv_c[..., NOPE_DIM:]], axis=1)
        k_rope = jnp.concatenate([k_rope, ctx_krope[:, :, None, :]], axis=1)
    k = jnp.concatenate([k_nope, jnp.broadcast_to(k_rope, k_nope.shape[:-1] + (ROPE_DIM,))], axis=-1)
    q = jnp.concatenate([q_nope, q_rope], axis=-1)
    y_b = blocked_attention(q, k, v) @ P['w_mla_o'][l]

    f = fn.reshape(B, L, FN_GROUPS, FN_GROUP_W).astype(jnp.float32)
    f = jnp.fft.fft2(f, axes=(1, 3), norm='ortho').real.reshape(B, L, FN_W).astype(n.dtype)
    y_c = f @ P['w_fnet'][l]

    g_a, g_b, g_c = jnp.split(jax.nn.sigmoid(gates), N_BRANCH, axis=-1)
    y = (g_a * y_a + g_b * y_b + g_c * y_c) @ P['w_out'][l]
    return y, ckv, k_r

def trunk_layer(h, ada, l, P, rope_ang, ctx_ckv, ctx_krope):
    s0, sc0, g0, s1, sc1, g1, s2, sc2, g2 = [m[:, None, :] for m in jnp.split(ada, 9, axis=-1)]
    n = rmsnorm(h, P['norm_g'][l, 0]) * (1 + sc0) + s0
    h = h + 0.5 * g0 * swiglu(n, P['w_ffn_up'][l, 0], P['w_ffn_down'][l, 0])
    n = rmsnorm(h, P['norm_g'][l, 1]) * (1 + sc1) + s1
    y, ckv, k_r = token_mix(n, l, P, rope_ang, ctx_ckv, ctx_krope)
    h = h + g1 * y
    n = rmsnorm(h, P['norm_g'][l, 2]) * (1 + sc2) + s2
    h = h + 0.5 * g2 * swiglu(n, P['w_ffn_up'][l, 1], P['w_ffn_down'][l, 1])
    return h, ckv, k_r

def setup_inputs(seed: int = 0) -> dict:
    key = jax.random.key(seed)
    ks = jax.random.split(key, 32)
    f32 = jnp.float32

    def nrm(k, shape, scale=1.0):
        return jax.random.normal(k, shape, f32) * scale

    D = D_MODEL
    return {
        'x_prompt': nrm(ks[0], (BATCH, SEQ, D)),
        'x_sample': nrm(ks[1], (DEC_BATCH, DEC_SEQ, D)),
        'cache_ckv': nrm(ks[2], (DEC_BATCH, DEPTH, PAST_LEN, KV_LORA)),
        'cache_krope': nrm(ks[3], (DEC_BATCH, DEPTH, PAST_LEN, ROPE_DIM)),
        'c': nrm(ks[4], (DEC_BATCH, D)),
        'c_ctx': nrm(ks[5], (D,)),
        'w_ada': nrm(ks[6], (DEPTH, D, 9 * D), 0.5 * D ** -0.5),
        'b_ada': nrm(ks[7], (DEPTH, 9 * D), 0.01),
        'norm_g': 1.0 + nrm(ks[8], (DEPTH, 3, D), 0.05),
        'w_ffn_up': nrm(ks[9], (DEPTH, 2, D, 2 * D_FF), D ** -0.5),
        'w_ffn_down': nrm(ks[10], (DEPTH, 2, D_FF, D), D_FF ** -0.5),
        'w_in': nrm(ks[11], (DEPTH, D, IN_COLS), D ** -0.5),
        'hy_conv_w': nrm(ks[12], (DEPTH, 3, 3 * HY_W), 3 ** -0.5),
        'hy_conv_b': nrm(ks[13], (DEPTH, 3 * HY_W), 0.01),
        'hy_filt_w1': nrm(ks[14], (DEPTH, POS_EMB, FILT_HID), POS_EMB ** -0.5),
        'hy_filt_b1': nrm(ks[15], (DEPTH, FILT_HID), 0.1),
        'hy_filt_w2': nrm(ks[16], (DEPTH, FILT_HID, FILT_HID), FILT_HID ** -0.5),
        'hy_filt_b2': nrm(ks[17], (DEPTH, FILT_HID), 0.1),
        'hy_filt_w3': nrm(ks[18], (DEPTH, FILT_HID, 2 * HY_ORDER * HY_W), FILT_HID ** -0.5),
        'hy_skip': nrm(ks[19], (DEPTH, HY_ORDER, HY_W), 0.5),
        'w_hy_out': nrm(ks[20], (DEPTH, HY_W, D), HY_W ** -0.5),
        'q_norm_g': 1.0 + nrm(ks[21], (DEPTH, Q_LORA), 0.05),
        'w_qb': nrm(ks[22], (DEPTH, Q_LORA, N_HEADS * (NOPE_DIM + ROPE_DIM)), Q_LORA ** -0.5),
        'kv_norm_g': 1.0 + nrm(ks[23], (DEPTH, KV_LORA), 0.05),
        'w_kvb': nrm(ks[24], (DEPTH, KV_LORA, N_HEADS * (NOPE_DIM + V_DIM)), KV_LORA ** -0.5),
        'w_mla_o': nrm(ks[25], (DEPTH, N_HEADS * V_DIM, D), (N_HEADS * V_DIM) ** -0.5),
        'w_fnet': nrm(ks[26], (DEPTH, FN_W, D), FN_W ** -0.5),
        'w_out': nrm(ks[27], (DEPTH, D, D), D ** -0.5),
        'final_g': 1.0 + nrm(ks[28], (D,), 0.05),
    }

def reference(x_prompt, x_sample, cache_ckv, cache_krope, c, c_ctx, w_ada, b_ada, norm_g, w_ffn_up, w_ffn_down,
              w_in, hy_conv_w, hy_conv_b, hy_filt_w1, hy_filt_b1, hy_filt_w2, hy_filt_b2, hy_filt_w3, hy_skip,
              w_hy_out, q_norm_g, w_qb, kv_norm_g, w_kvb, w_mla_o, w_fnet, w_out, final_g):
    P = {
        'norm_g': norm_g, 'w_ffn_up': w_ffn_up, 'w_ffn_down': w_ffn_down, 'w_in': w_in,
        'hy_conv_w': hy_conv_w, 'hy_conv_b': hy_conv_b, 'hy_filt_w1': hy_filt_w1, 'hy_filt_b1': hy_filt_b1,
        'hy_filt_w2': hy_filt_w2, 'hy_filt_b2': hy_filt_b2, 'hy_filt_w3': hy_filt_w3, 'hy_skip': hy_skip,
        'w_hy_out': w_hy_out, 'q_norm_g': q_norm_g, 'w_qb': w_qb, 'kv_norm_g': kv_norm_g, 'w_kvb': w_kvb,
        'w_mla_o': w_mla_o, 'w_fnet': w_fnet, 'w_out': w_out,
    }
    rows_n = x_sample.shape[1] // GRID_W
    rope_ang = axial_angles(rows_n)
    silu_ctx = jax.nn.silu(c_ctx)[None, :]
    silu_c = jax.nn.silu(c)
    hp = x_prompt
    hs = x_sample
    ckv_list = []
    kr_list = []
    for l in range(DEPTH):
        ada_ctx = silu_ctx @ w_ada[l] + b_ada[l]
        hp, ckv, kr = trunk_layer(hp, ada_ctx, l, P, None, None, None)
        ckv_list.append(ckv)
        kr_list.append(kr)
        ada_lat = silu_c @ w_ada[l] + b_ada[l]
        hs, _, _ = trunk_layer(hs, ada_lat, l, P, rope_ang, cache_ckv[:, l], cache_krope[:, l])
    y_prompt = rmsnorm(hp, final_g)
    y_sample = rmsnorm(hs, final_g)
    new_ckv = jnp.stack(ckv_list, axis=1)
    new_krope = jnp.stack(kr_list, axis=1)
    return (y_prompt, y_sample, new_ckv, new_krope)


_drawn_inputs = setup_inputs


def setup_inputs(seed=0):
    import zlib

    import numpy as np

    out = dict(_drawn_inputs(seed))
    spreads = {}
    factors = {'cache_ckv': 8.0,
     'cache_krope': 8.0,
     'b_ada': 3.813,
     'hy_conv_b': 23.735,
     'hy_filt_b1': 6.957,
     'hy_filt_b2': 5.897,
     'q_norm_g': 8.0}
    for name, (base, spread) in spreads.items():
        noise = np.random.default_rng([zlib.crc32(name.encode()), seed]).standard_normal(out[name].shape)
        drawn = base * np.exp(spread * noise) if base else spread * noise
        out[name] = __import__('jax').numpy.asarray(drawn.astype(out[name].dtype))
    for name, factor in factors.items():
        out[name] = (out[name] * factor).astype(out[name].dtype)
    return out
```

```python
import math
from contextlib import ExitStack, contextmanager

import numpy as np
import concourse.bass as bass
import concourse.mybir as mybir

F32 = mybir.dt.float32
F32R = mybir.dt.float32r
ALU = mybir.AluOpType
ACT = mybir.ActivationFunctionType
AX = mybir.AxisListType

P = 128
D = 1024
KT = D // P
TL, TC = 512, 128
T = TL + TC
TH = T // 2
DEPTH = 2
PAST = 128
HYW = 256
FW = 256
NB = 8
FHID = 64
HEADS = 8
NOPE, ROPE, VD = 64, 32, 64
QK = NOPE + ROPE
KEYS = T + PAST
DFF = 2816
HT = DFF // P
CHUNKS = [8, 8, 6]
EPS = 1e-6
PANEL = 2048
FQ = TL // P
GRID_W = 64

PAR = {}
_at = 0
for _n, _w in [("b_ada", 144), ("norm_g", 48), ("conv", 24), ("skip", 4), ("q_g", 2), ("kv_g", 1), ("b1", 1), ("b2", 1),
               ("w1", FHID), ("w2", 2 * FHID), ("ckv", PAST), ("krope", PAST), ("w3", 4 * HYW)]:
    PAR[_n] = (_at, _at + _w)
    _at += _w
NPAR = _at
CST = {}
_at = 0
for _n, _w in [("decay", 5 * HYW), ("rope", TL), ("ident", P), ("ones", P), ("sel", 2), ("eps", 1), ("final_g", KT)]:
    CST[_n] = (_at, _at + _w)
    _at += _w
NCST = _at
SM_C, SM_S, SM_CI, SM_SI, SM_BD, SM_FC, SM_FS, NSM = 0, 128, 256, 384, 512, 768, 896, 1024

SEGMENTS = [(0, 0, TH, 0, TH, 0), (1, 0, TL - TH, TH, TL, 0), (1, TL - TH, TH, TL, T, 1)]
GROUPS = [(0, 0, TL), (1, TL, T)]
FFN_PANELS = sum(c + 4 for c in CHUNKS)
LAYER_PANELS = 36 + 2 * FFN_PANELS + 6 + 2 + 8 + 4 + 16 + 4


class Due:

    entered = None

    def __init__(self, engine, eng, per_pass, start):
        self.engine, self.eng, self.per_pass, self.n, self.loops = engine, eng, per_pass, dict(start), []

    def __call__(self, sem, k=1):
        name = sem.name
        self.n[name] = self.n.get(name, 0) + k
        value = self.n[name]
        for key, reg in self.loops:
            step = self.per_pass.get(key, {}).get(name, 0)
            if step:
                value = reg * step + value
        return value

    def now(self, sem):
        return self(sem, 0)

    @contextmanager
    def loop(self, label, count):
        key, before = (self.engine, label), dict(self.n)
        self.eng.sem_inc(self.entered, 1)
        with self.eng.Fori(0, count) as reg:
            self.loops.append((key, reg))
            yield reg
            self.loops.pop()
        step = {s: v - before.get(s, 0) for s, v in self.n.items()}
        self.per_pass[key] = step
        for s, v in step.items():
            self.n[s] += (count - 1) * v


def program(nc, per_pass, x, w_ada, w_up, w_down, w_mix, w_qkv, w_gate, w_out, tables, small, cst_in, cvec, feats, par,
            y_out, ckv_out, krope_out):
    ctx = ExitStack()
    with ctx:
        def sem(name):
            return ctx.enter_context(nc.semaphore(name))

        base = (nc.sbuf_base + 63) // 64 * 64

        def place(at, *specs):
            out = []
            for name, shape, dt in specs:
                out.append(nc.alloc_sbuf_tensor_at(name, shape, dt, offset=at))
                at += 4 * int(np.prod(shape[1:]))
                at = (at + 31) // 32 * 32
            return out, at

        (h, raw, whi, wlo), at = place(base, ("h", [P, KT, T], F32), ("raw", [P, 2, PANEL], F32),
                                       ("whi", [P, 2, PANEL], F32R), ("wlo", [P, 2, PANEL], F32R))
        (smh, sml, cs_t, pr, ada, gm), at = place(
            at, ("small_hi", [P, NSM], F32R), ("small_lo", [P, NSM], F32R), ("constants", [P, NCST], F32),
            ("params", [P, NPAR], F32), ("ada_t", [P, 72, 2], F32), ("norm_scale", [P, 24, 2], F32))
        (stat,), at = place(at, ("softmax_stats", [P, 16], F32))
        X0 = at
        (xh, xl), at = place(X0, ("x_hi", [P, 8, T], F32R), ("x_lo", [P, 8, T], F32R))
        N0 = at
        (nh, nl), at = place(N0, ("n_hi", [P, KT, T], F32R), ("n_lo", [P, KT, T], F32R))
        W0 = at
        (sg, hf, acc, sq, rs, rr, tn, un), end1 = place(
            W0, ("gate_act", [P, 2, T], F32), ("hidden", [P, 2, T], F32), ("sq_sum", [P, T], F32),
            ("squares", [P, 2, T], F32), ("rms", [P, T], F32), ("inv_rms", [P, T], F32), ("scaled", [P, 2, T], F32),
            ("modulated", [P, 2, T], F32))
        (csil, cvt, csr, row), _ = place(
            W0, ("c_silu", [P, KT, 2], F32), ("c_raw", [P, KT, 2], F32), ("c_split", [P, KT, P], F32R),
            ("ada_rows", [P, 2, 256], F32))
        (smraw,), _ = place(N0, ("small_raw", [P, NSM], F32))
        (qa, kvr, krr), A0 = place(W0, ("q_low", [P, 2, T], F32), ("kv_low", [P, T], F32), ("k_rope_h2", [P, T], F32))
        (qnh, qnl), _ = place(W0, ("qn_hi", [P, 2, T], F32R), ("qn_lo", [P, 2, T], F32R))
        (hyx,), wt = place(A0, ("hyena_x", [P, 6, T], F32))
        UP = T + 4
        (upad, ft), end2 = place(wt, ("conv_pad", [P, 2, UP], F32), ("features", [P, T], F32))
        (mz, mz2, mk, mr), _ = place(N0, ("sin_h", [P, T], F32), ("sin_z", [P, T], F32), ("sin_k", [P, T], F32),
                                     ("sin_r", [P, T], F32))
        (reb, hbb, pp, yf, ab, inv), end3 = place(
            wt, ("re_part", [P, 2 * HYW], F32), ("im_part", [P, HYW], F32), ("products", [P, 2, HYW], F32),
            ("y_freq", [P, 2 * HYW], F32), ("abs_filter", [P, 2 * HYW], F32), ("inv_l1", [P, 2, HYW], F32))
        XT = 4 * T
        (fnh,), _ = place(X0, ("fnet_in_hi", [P, 2, T], F32R))
        (fah, ), _ = place(X0 + 2 * XT, ("fnet_mid_hi", [P, 5, 512], F32R))
        (fnl,), _ = place(X0 + 8 * XT, ("fnet_in_lo", [P, 2, T], F32R))
        (fal, ), _ = place(X0 + 10 * XT, ("fnet_mid_lo", [P, 5, 512], F32R))
        (tmh, tml, hd), _ = place(N0, ("tok_hi", [P, 5, 3 * HYW], F32R), ("tok_lo", [P, 5, 3 * HYW], F32R),
                                  ("taps", [P, 5, 2 * HYW], F32))
        (yh,), _ = place(X0 + 2 * XT, ("spec_hi", [P, 10, HYW], F32R))
        (yl,), _ = place(X0 + 10 * XT, ("spec_lo", [P, 10, HYW], F32R))
        NPT = 5 * TL + TC
        (pth, ptl, qh, ql, qf), _ = place(
            N0, ("probs_t_hi", [P, NPT], F32R), ("probs_t_lo", [P, NPT], F32R), ("q_hi", [P, 2, T], F32R),
            ("q_lo", [P, 2, T], F32R), ("q_f32", [P, 2, T], F32))
        (asq, ars, art), _ = place(N0, ("att_sq", [P, 3, T], F32), ("att_rms", [P, 2, T], F32), ("att_scaled", [P, 3, T], F32))
        (kh, kl, vh, vl, pm, ckh, ckl), _ = place(
            A0, ("k_hi", [P, KEYS], F32R), ("k_lo", [P, KEYS], F32R), ("v_hi", [P, KEYS], F32R), ("v_lo", [P, KEYS], F32R),
            ("probs", [P, 2, T], F32), ("ckv_hi", [P, KEYS], F32R), ("ckv_lo", [P, KEYS], F32R))
        (kro, krt), _ = place(A0 + 4 * 4 * KEYS, ("k_roped", [P, T], F32), ("rope_tmp", [P, T], F32))
        (yc, sgm, prod), _ = place(W0, ("mixed", [P, KT, T], F32), ("branch_gate", [P, 3, T], F32), ("branch", [P, T], F32))

        tps = ctx.enter_context(nc.psum_tensor("tile_psum", [P, 2, 2, 512], F32))
        mps = ctx.enter_context(nc.psum_tensor("misc_psum", [P, 2, 2, 512], F32))

        def flat(ps, s):
            return ps[:, s].rearrange("p a b -> p (a b)")

        def halves(ap):
            return ap.rearrange("p (a b) -> p a b", a=2)

        def cst(name):
            return cs_t[:, CST[name][0]:CST[name][1]]

        def prm(name, a=0, b=None):
            lo, hi = PAR[name]
            return pr[:, lo + a:(hi if b is None else lo + b)]

        ident, ones, eps, sel = cst("ident"), cst("ones"), cst("eps"), cst("sel")

        def smat(ap, at, n=P):
            return ap[:, at:at + n]

        loaded = [sem(f"panel_loaded{s}") for s in range(2)]
        hi_ready = sem("panel_hi_ready")
        lo_ready = sem("panel_lo_ready")
        tile_done = [sem(f"tile_done{s}") for s in range(2)]
        tile_free = [sem(f"tile_free{s}") for s in range(2)]
        misc_done = [sem(f"misc_done{s}") for s in range(2)]
        misc_free = [sem(f"misc_free{s}") for s in range(2)]
        dve_own = sem("dve_own")
        consts_in, small_in, par_in = sem("constants_in"), sem("small_in"), sem("params_in")
        x_in, c_in, feat_in = sem("x_in"), sem("c_in"), sem("features_in")
        small_hi, small_split = sem("small_hi"), sem("small_split")
        c_clear, silu_out, c_hi, c_split = sem("c_split_clear"), sem("silu_c_out"), sem("c_hi"), sem("c_split_ready")
        sin_in, sin_out = sem("sin_in"), sem("sin_out")
        rows_out, layer_end, mod_ready = sem("ada_rows_out"), sem("layer_end"), sem("modulation_ready")
        h_new, sq_out, sq_used, sum_ready = sem("h_new"), sem("squares_out"), sem("squares_used"), sem("sq_sum_ready")
        rms_out, t_ready, hi_out, n_ready = sem("rms_out"), sem("scaled_ready"), sem("n_hi_out"), sem("n_ready")
        hid_hi, hid_ready = sem("hidden_hi"), sem("hidden_ready")
        spilled, back = sem("n_spilled"), sem("n_back")
        conv_in, conv_used, v_ready = sem("conv_in"), sem("conv_used"), sem("v_ready")
        taps_ready, abs_ready, abs_used, bwd_sum = sem("taps_ready"), sem("abs_ready"), sem("abs_used"), sem("bwd_sum_out")
        parts_out, parts_used, spec_ready = sem("spectrum_parts"), sem("spectrum_parts_used"), sem("spectrum_ready")
        op_hi, z_new, z_split, y_done = sem("operand_hi"), sem("z_new"), sem("z_split"), sem("y_done")
        asq_ready, low_ready, low_hi, low_split = sem("low_squares"), sem("low_scaled"), sem("low_hi"), sem("low_split")
        krope_ready, q_copy, q_roped, q_split = sem("k_roped_ready"), sem("q_copied"), sem("q_roped_ready"), sem("q_split")
        prob_in, prob_ready = sem("neg_max_ready"), sem("probs_ready")
        y_ready, stored = sem("y_ready"), sem("outputs_stored")
        Due.entered = sem("loop_entered")
        credit = {lo_ready.name: 2}

        n_keep = [nc.dram_tensor(f"n_keep{i}", [P, KT, T], F32).ap() for i in range(2)]

        class Slot:

            def __init__(self, s, done, free, due):
                self.s, self.done, self.free = s, done, free
                self.done_at = due(done)
                self.reusable_at = due(free)
                self.free_at = self.reusable_at + 1

        class Slots:

            def __init__(self, due):
                self.due, self.tiles, self.miscs = due, 0, 0

            def tile(self):
                s, self.tiles = self.tiles % 2, self.tiles + 1
                return Slot(s, tile_done[s], tile_free[s], self.due)

            def misc(self):
                s, self.miscs = self.miscs % 2, self.miscs + 1
                return Slot(s, misc_done[s], misc_free[s], self.due)

        block = ctx.enter_context(nc.Block())

        @block.sync
        def _(sp):
            due = Due("sp", sp, per_pass, {})
            slot = [0]

            def load(src, cols):
                s = slot[0] % 2
                slot[0] += 1
                sp.wait_ge(lo_ready, due(lo_ready))
                sp.dma_start(raw[:, s, 0:cols], src).then_inc(loaded[s], 16)

            def pairs(label, src, first, count, cols=PANEL):
                with due.loop(label, count // 2) as i:
                    for k in range(2):
                        load(src(i, first + k), cols)

            sp.dma_start(cs_t[:, :], cst_in).then_inc(consts_in, 16)
            sp.dma_start(smraw[:, :], small).then_inc(small_in, 16)
            sp.dma_start(h[:, :, :], x).then_inc(x_in, 16)
            with due.loop("layer", DEPTH) as l:
                pairs("ada", lambda i, k: w_ada[bass.ds(l * 36 + i * 2 + k, 1)].rearrange("a p n -> (a p) n"), 0, 36)

                def ffn(f):
                    at = 0
                    for c, n in enumerate(CHUNKS):
                        pairs(f"up{f}{c}", lambda i, k: w_up[bass.ds((l * 2 + f) * HT + i * 2 + k, 1)]
                              .rearrange("a p n -> (a p) n"), at, n)
                        wd = w_down[0] if n == 8 else w_down[1]
                        base_row = (l * 2 + f) * 8 + 4 * c if n == 8 else (l * 2 + f) * 4
                        pairs(f"down{f}{c}", lambda i, k: wd[bass.ds(base_row + i * 2 + k, 1)]
                              .rearrange("a p n -> (a p) n"), 0, 4, 2 * n * P)
                        at += n

                ffn(0)
                pairs("mix", lambda i, k: w_mix[bass.ds(l * 6 + i * 2 + k, 1)].rearrange("a p n -> (a p) n"), 0, 6)
                for t in (4, 5) + (0, 1, 2, 3) * 2:
                    load(tables[t], PANEL)
                pairs("qkv", lambda i, k: w_qkv[bass.ds(l * 4 + i * 2 + k, 1)].rearrange("a p n -> (a p) n"), 0, 4, 7 * P)
                pairs("gate", lambda i, k: w_gate[bass.ds(l * 16 + i * 2 + k, 1)].rearrange("a p n -> (a p) n"), 0, 16)
                pairs("out", lambda i, k: w_out[bass.ds(l * 4 + i * 2 + k, 1)].rearrange("a p n -> (a p) n"), 0, 4)
                ffn(1)
            for k in range(2):
                load(tables[0][:, 0:P], P)
            sp.wait_ge(y_ready, due(y_ready, 8))
            sp.dma_start(y_out, h[:, :, :]).then_inc(stored, 16)
            sp.wait_ge(stored, 16 + DEPTH * 32)

        @block.gpsimd
        def _(pool):
            due = Due("pool", pool, per_pass, {})
            with due.loop("panels", DEPTH * LAYER_PANELS // 2 + 1):
                for s in range(2):
                    pool.wait_ge(hi_ready, due(hi_ready))
                    pool.tensor_tensor(wlo[:, s, :], raw[:, s, :], whi[:, s, :].bitcast(F32), ALU.subtract)\
                        .then_inc(lo_ready, 1)

        @block.tensor
        def _(pe):
            due = Due("pe", pe, per_pass, credit)
            slots = Slots(due)
            at = [0]

            def panel():
                s = at[0] % 2
                at[0] += 1
                pe.wait_ge(lo_ready, due(lo_ready))
                return s

            def blk(s, b, n=P):
                return whi[:, s, b * P:b * P + n], wlo[:, s, b * P:b * P + n]

            def mm3(outs, w, xs, first, last):
                for n, (a, b) in enumerate(((0, 0), (0, 1), (1, 0))):
                    for o, x_ in zip(outs, xs):
                        ins = pe.matmul(o, w[a], x_[b], start=first and n == 0, stop=last and n == 2)
                return ins

            def tile():
                t = slots.tile()
                pe.wait_ge(t.free, t.reusable_at)
                return t.s

            def misc():
                m = slots.misc()
                pe.wait_ge(m.free, m.reusable_at)
                return m.s

            def all_read(frees):
                for f in frees:
                    pe.wait_ge(f, due.now(f) + 1)

            def xs_of(hi, lo, k):
                return [(hi[:, k, j * TH:(j + 1) * TH], lo[:, k, j * TH:(j + 1) * TH]) for j in range(2)]

            def gemm(s, b0, hi, lo, k0, n, wait=None):
                t = tile()
                for k in range(n):
                    if wait is not None:
                        pe.wait_ge(wait, due(wait))
                    ins = mm3([tps[:, t, j, 0:TH] for j in range(2)], blk(s, b0 + k), xs_of(hi, lo, k0 + k),
                              k == 0, k == n - 1)
                ins.then_inc(tile_done[t], 1)

            def column_sums(ready, rhs, n=1):
                m = misc()
                pe.wait_ge(ready, due(ready))
                for k in range(n):
                    for j in range(2):
                        ins = pe.matmul(mps[:, m, j, 0:TH], ones, rhs[k][:, j * TH:(j + 1) * TH],
                                        start=k == 0, stop=k == n - 1)
                ins.then_inc(misc_done[m], 1)

            def ffn(f):
                column_sums(sum_ready, [acc])
                first = True
                for c, n in enumerate(CHUNKS):
                    if c == 0:
                        pe.wait_ge(n_ready, due(n_ready, KT))
                    with due.loop(f"up{f}{c}", n // 2):
                        for k in range(2):
                            s = panel()
                            gemm(s, 0, nh, nl, 0, KT)
                            gemm(s, KT, nh, nl, 0, KT)
                    pe.wait_ge(hid_ready, due(hid_ready, n))
                    with due.loop(f"down{f}{c}", 2):
                        for k in range(2):
                            s = panel()
                            gemm(s, 0, xh, xl, 0, n)
                            gemm(s, n, xh, xl, 0, n)

            def transposes(src, tiles):
                m = misc()
                for c in range(2):
                    ins = pe.transpose(mps[:, m, 0, c * P:(c + 1) * P], src[:, 4 + c, tiles * P:(tiles + 1) * P], ident)
                ins.then_inc(misc_done[m], 1)

            pe.wait_ge(consts_in, due(consts_in, 16))
            pe.wait_ge(small_split, due(small_split))
            with due.loop("layer", DEPTH):
                def filter_mlp(w, src, kk, mm=FHID):
                    m = misc()
                    for j in range(2):
                        ins = pe.matmul(mps[0:mm, m, j, 0:TH], w[0:kk, :], src[0:kk, j * TH:(j + 1) * TH],
                                        start=True, stop=True)
                    ins.then_inc(misc_done[m], 1)

                pe.wait_ge(c_split, due(c_split))
                with due.loop("ada", 18):
                    for k in range(2):
                        s = panel()
                        m = misc()
                        for kt in range(KT):
                            for n, w in enumerate((whi, wlo)):
                                ins = pe.matmul(mps[:, m, 0, 0:256], csr[:, kt, :], w[:, s, kt * 256:(kt + 1) * 256],
                                                start=kt == 0 and n == 0, stop=kt == KT - 1 and n == 1)
                        ins.then_inc(misc_done[m], 1)
                        m2 = misc()
                        pe.wait_ge(rows_out, due(rows_out))
                        for j in range(2):
                            ins = pe.matmul(mps[:, m2, 0, 2 * j:2 * j + 2], row[0:4, k, j * P:(j + 1) * P], sel[0:4, :],
                                            start=True, stop=True)
                        ins.then_inc(misc_done[m2], 1)
                ffn(0)

                column_sums(sum_ready, [acc])
                pe.wait_ge(n_ready, due(n_ready, KT))
                with due.loop("mix", 3):
                    for k in range(2):
                        s = panel()
                        gemm(s, 0, nh, nl, 0, KT)
                        gemm(s, KT, nh, nl, 0, KT)

                bdm = [(smat(smh, SM_BD, 256), smat(sml, SM_BD, 256))]
                pe.wait_ge(feat_in, due(feat_in, 16))
                pe.wait_ge(par_in, due(par_in, 16))
                filter_mlp(prm("w1"), ft, 17)
                all_read(tile_free)
                for t in range(5):
                    m = misc()
                    for c in range(2):
                        tk = slice(t * P, (t + 1) * P)
                        ins = mm3([mps[:, m, 0, c * 256:(c + 1) * 256]], (fnh[:, c, tk], fnl[:, c, tk]), bdm, True, True)
                    ins.then_inc(misc_done[m], 1)
                pe.wait_ge(sin_out, due(sin_out))
                filter_mlp(prm("w2"), mz, FHID, P)
                sc, ss = panel(), panel()
                all_read(misc_free)
                for c in range(2):
                    t = tile()
                    for part, s in ((0, sc), (1, ss)):
                        lo_c = c * 256 + part * P
                        for tt in range(4):
                            w = (fah[:, tt, lo_c:lo_c + P], fal[:, tt, lo_c:lo_c + P])
                            mm3([tps[:, t, 0, :]], w, [blk(s, 4 * tt, 512)], part == 0 and tt == 0, part == 1 and tt == 3)
                        at_ = SM_FC if part == 0 else SM_FS
                        w = (fah[:, 4, lo_c:lo_c + P], fal[:, 4, lo_c:lo_c + P])
                        ins = mm3([tps[:, t, 1, 0:TC]], w, [(smat(smh, at_), smat(sml, at_))], part == 0, part == 1)
                    ins.then_inc(tile_done[t], 1)

                pe.wait_ge(sin_out, due(sin_out))
                for o in range(2):
                    for t in range(5):
                        m = misc()
                        pe.matmul(mps[:, m, 0, :], krr[0:FHID, t * P:(t + 1) * P],
                                  prm("w3", o * 512, (o + 1) * 512)[0:FHID, :], start=True, stop=True)\
                            .then_inc(misc_done[m], 1)
                    for g, ts in ((0, range(4)), (1, range(4, 5))):
                        m = misc()
                        for t in ts:
                            pe.wait_ge(abs_ready, due(abs_ready))
                            pe.matmul(mps[:, m, 0, :], ones, (ab if t % 2 == 0 else yf)[:, :], start=t == ts[0], stop=t == ts[-1])\
                                .then_inc(misc_done[m] if t == ts[-1] else abs_used, 1)
                    pe.wait_ge(v_ready, due(v_ready, 2))
                    for t in range(5):
                        transposes(hyx, t)
                    sc, ss = panel(), panel()
                    all_read(misc_free)
                    for f in range(5):
                        m = misc()
                        for part, (s, col, sm) in enumerate(((sc, 0, SM_C), (ss, HYW, SM_S))):
                            out = [mps[:, m, part, :]]
                            if f < 4:
                                for t in range(4):
                                    w = (whi[:, s, t * 512 + f * P:t * 512 + (f + 1) * P],
                                         wlo[:, s, t * 512 + f * P:t * 512 + (f + 1) * P])
                                    ins = mm3(out, w, [(tmh[:, t, col:col + 512], tml[:, t, col:col + 512])], t == 0, t == 3)
                            else:
                                ins = mm3(out, (smat(smh, sm), smat(sml, sm)),
                                          [(tmh[:, 4, col:col + 512], tml[:, 4, col:col + 512])], True, True)
                        ins.then_inc(misc_done[m], 1)
                    sc, ss = panel(), panel()
                    pe.wait_ge(spec_ready, due(spec_ready, 5))
                    for c in range(2):
                        t = tile()
                        cc = slice(c * P, (c + 1) * P)
                        for part, s in ((0, sc), (1, ss)):
                            for f in range(4):
                                w = (yh[:, 2 * f + part, cc], yl[:, 2 * f + part, cc])
                                mm3([tps[:, t, 0, :]], w, [blk(s, 4 * f, 512)], part == 0 and f == 0, part == 1 and f == 3)
                            w = (yh[:, 8 + part, cc], yl[:, 8 + part, cc])
                            sm = SM_CI if part == 0 else SM_SI
                            ins = mm3([tps[:, t, 1, 0:TC]], w, [(smat(smh, sm), smat(sml, sm))], part == 0, part == 1)
                        ins.then_inc(tile_done[t], 1)

                column_sums(asq_ready, [asq[:, k, :] for k in range(2)], 2)
                column_sums(asq_ready, [asq[:, 2, :]])
                pe.wait_ge(low_split, due(low_split, 4))
                with due.loop("heads", 2):
                    for pair in range(2):
                        s = panel()
                        for j in range(2):
                            q = j
                            t = tile()
                            for k in range(2):
                                ins = mm3([tps[:, t, i, 0:TH] for i in range(2)], blk(s, 2 * j + k), xs_of(qnh, qnl, k), k == 0, k == 1)
                            ins.then_inc(tile_done[t], 1)
                            m = misc()
                            ks = [slice(0, KEYS // 2), slice(KEYS // 2, KEYS)]
                            mm3([mps[:, m, i, 0:KEYS // 2] for i in range(2)], blk(s, 4 + j),
                                [(ckh[:, i], ckl[:, i]) for i in ks], True, True).then_inc(misc_done[m], 1)
                            if j == 0:
                                m = misc()
                                for kt in range(6):
                                    kk = slice(kt * P, (kt + 1) * P)
                                    ins = mm3([mps[:, m, kt // 3, (kt % 3) * P:(kt % 3 + 1) * P]], (ckh[:, kk], ckl[:, kk]),
                                              [blk(s, 6)], True, True)
                                ins.then_inc(misc_done[m], 1)
                            all_read(misc_free)
                            pe.wait_ge(q_split, due(q_split))

                            def scores(qt):
                                m = misc()
                                w = (qh[0:QK, q, qt * P:(qt + 1) * P], ql[0:QK, q, qt * P:(qt + 1) * P])
                                if qt < 4:
                                    mm3([mps[:, m, 0, :]], w, [(kh[0:QK, 0:TL], kl[0:QK, 0:TL])], True, True)
                                    ins = mm3([mps[:, m, 1, 0:P]], w, [(kh[0:QK, T:KEYS], kl[0:QK, T:KEYS])], True, True)
                                else:
                                    ins = mm3([mps[:, m, 0, 0:P]], w, [(kh[0:QK, TL:T], kl[0:QK, TL:T])], True, True)
                                ins.then_inc(misc_done[m], 1)

                            def turn(qt):
                                t = tile()
                                pe.wait_ge(prob_ready, due(prob_ready))
                                for kt in range(5 if qt < 4 else 1):
                                    ins = pe.transpose(flat(tps, t)[:, kt * P:(kt + 1) * P], pm[:, qt % 2, kt * P:(kt + 1) * P], ident)
                                ins.then_inc(tile_done[t], 1)

                            scores(0)
                            for qt in range(1, 5):
                                scores(qt)
                                turn(qt - 1)
                            turn(4)
                            t = tile()
                            for f in tile_free:
                                pe.wait_ge(f, due.now(f) + (0 if f is tile_free[t] else 1))
                            for kt in range(5):
                                vt = kt if kt < 4 else 5
                                kk = slice(vt * P, (vt + 1) * P)
                                mm3([tps[:, t, 0, :]], (vh[:, kk], vl[:, kk]),
                                    [(pth[:, kt * TL:(kt + 1) * TL], ptl[:, kt * TL:(kt + 1) * TL])], kt == 0, kt == 4)
                            mm3([tps[:, t, 1, 0:TC]], (vh[:, TL:T], vl[:, TL:T]), [(pth[:, 5 * TL:], ptl[:, 5 * TL:])], True, True)\
                                .then_inc(tile_done[t], 1)

                all_read(tile_free)
                pe.wait_ge(z_split, due(z_split, 2))
                pe.wait_ge(back, due(back, 32))
                with due.loop("gate", KT):
                    s = panel()
                    gemm(s, 0, nh, nl, 0, KT)
                    gemm(s, KT, nh, nl, 0, KT)
                    s = panel()
                    gemm(s, 0, nh, nl, 0, KT)
                    gemm(s, 8, xh, xl, 0, 2)
                    gemm(s, 10, xh, xl, 2, 4)
                    gemm(s, 14, xh, xl, 6, 2)
                pe.wait_ge(n_ready, due(n_ready, KT))
                with due.loop("out", 2):
                    for k in range(2):
                        s = panel()
                        gemm(s, 0, nh, nl, 0, KT)
                        gemm(s, KT, nh, nl, 0, KT)
                ffn(1)
            column_sums(sum_ready, [acc])


        @block.scalar
        def _(act):
            due = Due("act", act, per_pass, {})
            slots = Slots(due)
            at = [0]

            def round_panel():
                s = at[0] % 2
                at[0] += 1
                act.wait_ge(loaded[s], due(loaded[s], 16))
                act.activation(whi[:, s, :], raw[:, s, :], ACT.Copy).then_inc(hi_ready, 1)

            def seen(slot):
                act.wait_ge(slot.done, slot.done_at)
                return slot

            def tile():
                return seen(slots.tile())

            def misc():
                return seen(slots.misc())

            def tile2(t, g=False):
                return tps[:, t.s, :, 0:TH]

            def squares():
                act.wait_ge(h_new, due(h_new))
                for k in range(KT):
                    if k >= 3:
                        act.wait_ge(sq_used, due(sq_used))
                    act.activation(acc[:, :] if k == 0 else sq[:, k % 2, :], h[:, k, :], ACT.Square).then_inc(sq_out, 1)
                due(sq_used)

            def root(out, width, m, ready):
                act.activation(halves(out), mps[:, m.s, :, 0:TH], ACT.Sqrt, bias=eps, scale=1.0 / width).then_inc(ready, 1)

            def norm(i):
                squares()
                root(rs[:, :], D, misc(), rms_out)
                for k in range(KT):
                    act.wait_ge(t_ready, due(t_ready))
                    for _, a, b in GROUPS:
                        g = 0 if a == 0 else 1
                        ins = act.activation(nh[:, k, a:b], tn[:, k % 2, a:b], ACT.Identity,
                                             bias=ada[:, 24 * i + k, g:g + 1], scale=gm[:, 8 * i + k, g:g + 1])
                    ins.then_inc(hi_out, 1)
                due(n_ready, KT)

            def ffn(f):
                norm(2 * f)
                for c, n in enumerate(CHUNKS):
                    with due.loop(f"up{f}{c}", n // 2) as i:
                        for k in range(2):
                            t = tile()
                            act.activation(halves(sg[:, k, :]), tile2(t), ACT.Silu).then_inc(t.free, 1)
                            t = tile()
                            round_panel()
                            act.wait_ge(t.free, t.free_at)
                            act.activation(xh[:, bass.ds(i * 2 + k, 1), :].rearrange("p a t -> p (a t)"), hf[:, k, :], ACT.Copy)\
                                .then_inc(hid_hi, 1)
                    with due.loop(f"down{f}{c}", 2):
                        for k in range(2):
                            slots.tile()
                            tile()
                            round_panel()

            def split_hi(out, src, ready=op_hi):
                act.activation(out, src, ACT.Copy).then_inc(ready, 1)

            act.wait_ge(small_in, due(small_in, 16))
            split_hi(smh[:, :], smraw[:, :], small_hi)
            act.wait_ge(consts_in, due(consts_in, 16))
            round_panel()
            round_panel()
            with due.loop("layer", DEPTH) as l:
                act.wait_ge(layer_end, due(layer_end))
                act.dma_start(pr[:, :], par[bass.ds(l, 1)].rearrange("a p n -> (a p) n")).then_inc(par_in, 16)
                act.dma_start(cvt[:, :, :], cvec).then_inc(c_in, 16)
                act.wait_ge(c_in, due(c_in, 16))
                act.activation(csil[:, :, :], cvt[:, :, :], ACT.Silu).then_inc(silu_out, 1)
                act.wait_ge(silu_out, due(silu_out))
                act.wait_ge(c_clear, due(c_clear))
                act.activation(csr[:, :, 0:2], csil[:, :, :], ACT.Copy).then_inc(c_hi, 1)
                with due.loop("ada", 18):
                    for k in range(2):
                        m = misc()
                        act.activation(row[0:4, k, :], mps[0:4, m.s, 0, 0:256], ACT.Copy).then_inc(rows_out, 1)
                        round_panel()
                        act.wait_ge(rows_out, due(rows_out))
                        act.sem_inc(m.free, 1)
                        misc()
                act.wait_ge(mod_ready, due(mod_ready))
                ffn(0)

                norm(1)
                act.wait_ge(n_ready, due.now(n_ready))
                act.dma_start(n_keep[0], nh[:, :, :].bitcast(F32)).then_inc(spilled, 16)
                act.dma_start(n_keep[1], nl[:, :, :].bitcast(F32)).then_inc(spilled, 16)
                act.dma_start(ft[:, :], feats).then_inc(feat_in, 16)
                for c in range(2):
                    t = tile()
                    split_hi(halves(fnh[:, c, :]), tile2(t))
                round_panel()
                for c in range(6):
                    t = tile()
                    if c >= 2:
                        act.wait_ge(conv_used, due(conv_used))
                    for bank, c0, c1, t0, t1, g in SEGMENTS:
                        ins = act.activation(upad[:, c % 2, t0 + 1 + 2 * g:t1 + 1 + 2 * g], tps[:, t.s, bank, c0:c1], ACT.Copy)
                        ins.then_inc(t.free if g else conv_in, 1)
                    if c % 2:
                        round_panel()
                due(conv_used, 2)
                for c in range(2):
                    t = tile()
                    act.activation(halves(qa[:, c, :]), tile2(t), ACT.Copy).then_inc(t.free, 1)
                round_panel()
                t = tile()
                act.activation(halves(kvr[:, :]), tile2(t), ACT.Copy).then_inc(t.free, 1)
                t = tile()
                act.activation(halves(krr[FHID:P, :]), tps[FHID:P, t.s, :, 0:TH], ACT.Copy).then_inc(t.free, 1)
                round_panel()
                act.wait_ge(t.free, t.free_at)
                act.dma_start(krope_out[bass.ds(l, 1)].rearrange("a p n -> (a p) n"), krr[FHID:FHID + ROPE, TL:T]).then_inc(stored, 16)

                act.wait_ge(spilled, due(spilled, 32))
                def sine(out):
                    misc_ = slots.misc()
                    act.wait_ge(sin_in, due(sin_in))
                    act.activation(out, mr[0:FHID, :], ACT.Sin).then_inc(sin_out, 1)

                sine(mz[0:FHID, :])
                for t in range(5):
                    m = misc()
                    split_hi(fah[:, t, :], mps[:, m.s, 0, :])
                sine(krr[0:FHID, :])
                for c in range(2):
                    t = tile()
                    split_hi(xh[:, 6 + c, :], flat(tps, t.s)[:, 0:T])
                round_panel()
                round_panel()

                for o in range(2):
                    for t in range(5):
                        slots.misc()
                    for t in range(5):
                        act.wait_ge(taps_ready, due(taps_ready))
                        if t in (2, 3):
                            act.wait_ge(abs_used, due(abs_used))
                        if t == 4:
                            act.wait_ge(abs_used, due(abs_used))
                            m = misc()
                            split_hi(inv[:, 0, :], mps[:, m.s, 0, HYW:2 * HYW], bwd_sum)
                        act.activation((ab if t % 2 == 0 else yf)[:, :], hd[:, t, :], ACT.Abs).then_inc(abs_ready, 1)
                    m = misc()
                    split_hi(inv[:, 1, :], mps[:, m.s, 0, HYW:2 * HYW], bwd_sum)
                    for t in range(5):
                        m = misc()
                        split_hi(tmh[:, t, HYW:2 * HYW], mps[:, m.s, 0, 0:HYW])
                    for f in range(5):
                        m = misc()
                        act.wait_ge(parts_used, due(parts_used))
                        act.activation(reb[:, :], mps[:, m.s, 0, :], ACT.Copy)
                        act.activation(hbb[:, :], mps[:, m.s, 1, HYW:2 * HYW], ACT.Copy).then_inc(parts_out, 1)
                    round_panel()
                    round_panel()
                    slots.tile()
                    tile()
                    round_panel()
                    round_panel()
                for c in range(2):
                    act.wait_ge(z_new, due(z_new))
                    split_hi(xh[:, c, :], hyx[:, 4 + c, :])

                for k in range(2):
                    ins = act.activation(asq[:, k, :], qa[:, k, :], ACT.Square)
                ins.then_inc(asq_ready, 1)
                act.activation(asq[:, 2, :], kvr[:, :], ACT.Square).then_inc(asq_ready, 1)
                m = misc()
                root(ars[:, 0, :], 2 * P, m, rms_out)
                m = misc()
                root(ars[:, 1, :], P, m, rms_out)
                act.wait_ge(low_ready, due(low_ready))
                split_hi(ckh[:, 0:T], art[:, 2, :], low_hi)
                split_hi(ckh[:, T:KEYS], prm("ckv"), low_hi)
                act.dma_start(ckv_out[bass.ds(l, 1)].rearrange("a p n -> (a p) n"), art[:, 2, TL:T]).then_inc(stored, 16)
                act.wait_ge(krope_ready, due(krope_ready))
                R = slice(NOPE, QK)
                split_hi(kh[R, 0:TL], kro[R, 0:TL], low_hi)
                split_hi(kh[R, TL:T], krr[R, TL:T], low_hi)
                split_hi(kh[R, T:KEYS], prm("krope")[R, :], low_hi)
                act.wait_ge(low_ready, due(low_ready, 3))
                for k in range(2):
                    split_hi(qnh[:, k, :], art[:, k, :], low_hi)
                act.wait_ge(stored, due(stored, 32))
                with due.loop("heads", 2) as i:
                    for pair in range(2):
                        for j in range(2):
                            t = tile()
                            act.activation(halves(qf[0:QK, j, :]), tps[0:QK, t.s, :, 0:TH], ACT.Copy).then_inc(q_copy, 1)
                            m = misc()
                            split_hi(halves(kh[0:NOPE, :]), mps[0:NOPE, m.s, :, 0:KEYS // 2])
                            if j == 1:
                                round_panel()
                            if j == 0:
                                m = misc()
                                split_hi(halves(vh[:, :]), mps[:, m.s, :, 0:KEYS // 2])
                            act.wait_ge(q_roped, due(q_roped))
                            split_hi(qh[0:QK, j, :], qf[0:QK, j, :])

                            def softmax(qt):
                                m = misc()
                                n = TL + PAST if qt < 4 else TC
                                act.wait_ge(prob_in, due(prob_in))
                                act.activation(pm[:, qt % 2, 0:n], flat(mps, m.s)[:, 0:n], ACT.Exp, bias=stat[:, 5 + qt:6 + qt],
                                               scale=QK ** -0.5, accum_out=stat[:, 10 + qt:11 + qt]).then_inc(m.free, 1)

                            def turned(qt):
                                t = tile()
                                if qt < 4:
                                    split_hi(pth[:, 0:5 * TL].rearrange("p (a t) -> p a t", a=5)[:, :, qt * P:(qt + 1) * P],
                                             flat(tps, t.s)[:, 0:T].rearrange("p (a t) -> p a t", a=5))
                                else:
                                    split_hi(pth[:, 5 * TL:], tps[:, t.s, 0, 0:TC])

                            softmax(0)
                            for qt in range(1, 5):
                                softmax(qt)
                                turned(qt - 1)
                            turned(4)
                            t = tile()
                            rows = slice(j * VD, (j + 1) * VD)
                            split_hi(xh[rows, bass.ds(i * 2 + (2 + pair), 1), :].rearrange("p a t -> p (a t)"), flat(tps, t.s)[rows, 0:T])
                act.wait_ge(t.free, t.free_at)
                act.dma_start(nh[:, :, :].bitcast(F32), n_keep[0]).then_inc(back, 16)
                act.dma_start(nl[:, :, :].bitcast(F32), n_keep[1]).then_inc(back, 16)

                with due.loop("gate", KT):
                    for b in range(3):
                        t = tile()
                        act.activation(halves(sgm[:, b, :]), tile2(t), ACT.Sigmoid).then_inc(t.free, 1)
                        if b == 1:
                            round_panel()
                    slots.tile()
                    slots.tile()
                    tile()
                    round_panel()
                act.wait_ge(y_done, due(y_done))
                for k in range(KT):
                    split_hi(nh[:, k, :], yc[:, k, :], hi_out)
                due(n_ready, KT)
                with due.loop("out", 2):
                    for k in range(2):
                        slots.tile()
                        tile()
                        round_panel()
                ffn(1)
            squares()
            root(rs[:, :], D, misc(), rms_out)

        @block.vector
        def _(dve):
            due = Due("dve", dve, per_pass, {})
            slots = Slots(due)

            def own(ins):
                ins.then_inc(dve_own, 1)
                dve.wait_ge(dve_own, due(dve_own))

            def seen(slot):
                dve.wait_ge(slot.done, slot.done_at)
                return slot

            def tile():
                return seen(slots.tile())

            def misc():
                return seen(slots.misc())

            def tile2(t):
                return tps[:, t.s, :, 0:TH]

            def lo_part(out, src, hi, ready, after=None):
                after = op_hi if after is None else after
                dve.wait_ge(after, due(after))
                dve.tensor_tensor(out, src, hi.bitcast(F32), ALU.subtract).then_inc(ready, 1)

            def sum_squares():
                dve.wait_ge(sq_out, due(sq_out))
                for k in range(1, KT):
                    dve.wait_ge(sq_out, due(sq_out))
                    if k > 1:
                        dve.wait_ge(sq_used, due(sq_used))
                    dve.tensor_tensor(acc[:, :], acc[:, :], sq[:, k % 2, :], ALU.add)\
                        .then_inc(sq_used if k < KT - 1 else sum_ready, 1)

            def norm(i):
                sum_squares()
                m = slots.misc()
                dve.wait_ge(rms_out, due(rms_out))
                dve.reciprocal(rr[:, :], rs[:, :]).then_inc(m.free, 1)
                dve.wait_ge(m.free, m.free_at)
                def scaled(k):
                    dve.tensor_tensor(tn[:, k % 2, :], h[:, k, :], rr[:, :], ALU.mult).then_inc(t_ready, 1)

                scaled(0)
                for k in range(KT):
                    if k + 1 < KT:
                        scaled(k + 1)
                    dve.wait_ge(t_ready, due(t_ready))
                    for _, a, b in GROUPS:
                        g = 0 if a == 0 else 1
                        ins = dve.tensor_scalar(un[:, k % 2, a:b], tn[:, k % 2, a:b], gm[:, 8 * i + k, g:g + 1],
                                                ada[:, 24 * i + k, g:g + 1], ALU.mult, ALU.add)
                    own(ins)
                    lo_part(nl[:, k, :], un[:, k % 2, :], nh[:, k, :], n_ready, hi_out)

            def into_h(section, m):
                t = tile()
                for bank, c0, c1, t0, t1, g in SEGMENTS:
                    hs = h[:, bass.ds(m, 1), t0:t1].rearrange("p a t -> p (a t)")
                    gate = ada[:, bass.ds(m + 8 * section, 1), g:g + 1].rearrange("p a t -> p (a t)")
                    ins = dve.scalar_tensor_tensor(out=hs, in0=tps[:, t.s, bank, c0:c1], scalar=gate, in1=hs,
                                                   op0=ALU.mult, op1=ALU.add)
                ins.then_inc(t.free, 1)
                return t

            def ffn(f):
                norm(2 * f)
                for c, n in enumerate(CHUNKS):
                    with due.loop(f"up{f}{c}", n // 2) as i:
                        for k in range(2):
                            tg = slots.tile()
                            t = tile()
                            dve.wait_ge(tg.free, tg.free_at)
                            dve.tensor_tensor(halves(hf[:, k, :]), halves(sg[:, k, :]), tile2(t), ALU.mult).then_inc(t.free, 1)
                            dve.wait_ge(t.free, t.free_at)
                            kk = bass.ds(i * 2 + k, 1)
                            lo_part(xl[:, kk, :].rearrange("p a t -> p (a t)"), hf[:, k, :],
                                    xh[:, kk, :].rearrange("p a t -> p (a t)"), hid_ready, hid_hi)
                    with due.loop(f"down{f}{c}", 2) as i:
                        for k in range(4):
                            t = into_h(2 if f == 0 else 8, i * 4 + k)
                    dve.wait_ge(t.free, t.free_at)
                dve.sem_inc(h_new, 1)

            dve.sem_inc(lo_ready, 2)
            for f in tile_free + misc_free + [layer_end, parts_used]:
                dve.sem_inc(f, 1)
            dve.wait_ge(small_hi, due(small_hi))
            dve.tensor_tensor(sml[:, :], smraw[:, :], smh[:, :].bitcast(F32), ALU.subtract).then_inc(small_split, 1)
            dve.wait_ge(x_in, due(x_in, 16))
            dve.wait_ge(consts_in, due(consts_in, 16))
            dve.sem_inc(h_new, 1)
            with due.loop("layer", DEPTH):
                dve.memset(csr[:, :, :].bitcast(F32), 0.0).then_inc(c_clear, 1)
                dve.wait_ge(c_hi, due(c_hi))
                dve.tensor_tensor(csr[:, :, 2:4], csil[:, :, :], csr[:, :, 0:2].bitcast(F32), ALU.subtract).then_inc(c_split, 1)
                dve.wait_ge(par_in, due(par_in, 16))
                bada = prm("b_ada").rearrange("p (a b) -> p a b", b=2)
                with due.loop("ada", 18) as i:
                    for k in range(2):
                        slots.misc()
                        m = misc()
                        at_ = bass.ds(i * 4 + 2 * k, 2)
                        dve.tensor_tensor(ada[:, at_, :], mps[:, m.s, 0, 0:4].rearrange("p (a b) -> p a b", b=2),
                                          bada[:, at_, :], ALU.add).then_inc(m.free, 1)
                dve.wait_ge(m.free, m.free_at)
                ng = prm("norm_g").rearrange("p (a b) -> p a b", b=2)
                for i in range(3):
                    sc = slice(24 * i + 8, 24 * i + 16)
                    ins = dve.scalar_tensor_tensor(out=gm[:, 8 * i:8 * i + 8, :], in0=ada[:, sc, :], scalar=1.0,
                                                   in1=ng[:, 8 * i:8 * i + 8, :], op0=ALU.add, op1=ALU.mult)
                    if i != 1:
                        gs = slice(24 * i + 16, 24 * i + 24)
                        ins = dve.tensor_scalar(ada[:, gs, :], ada[:, gs, :], 0.5, None, ALU.mult)
                own(ins)
                dve.sem_inc(mod_ready, 1)
                ffn(0)

                norm(1)
                for c in range(2):
                    t = tile()
                    lo_part(halves(fnl[:, c, :]), tile2(t), halves(fnh[:, c, :]), t.free)
                for c in (0, UP - 1, TL + 1, TL + 2):
                    ins = dve.memset(upad[:, :, c:c + 1], 0.0)
                own(ins)
                for c in range(6):
                    t = slots.tile()
                    dve.wait_ge(conv_in, due(conv_in, 2))
                    dve.wait_ge(t.free, t.free_at)
                    w = prm("conv", 4 * c, 4 * c + 4)
                    for tap, shift in ((1, 1), (0, 0), (2, 2)):
                        for g, a, b in GROUPS:
                            gg = 0 if a == 0 else 1
                            src = upad[:, c % 2, a + shift + 2 * gg:b + shift + 2 * gg]
                            if tap == 1:
                                ins = dve.tensor_scalar(hyx[:, c, a:b], src, w[:, 1:2], w[:, 3:4], ALU.mult, ALU.add)
                            else:
                                ins = dve.scalar_tensor_tensor(out=hyx[:, c, a:b], in0=src, scalar=w[:, tap:tap + 1],
                                                               in1=hyx[:, c, a:b], op0=ALU.mult, op1=ALU.add)
                        if tap != 2:
                            own(ins)
                    ins.then_inc(conv_used, 1)
                    dve.wait_ge(conv_used, due(conv_used))
                for _ in range(4):
                    t = slots.tile()
                dve.sem_inc(v_ready, 1)
                dve.sem_inc(v_ready, 1)

                def sine(bias):
                    m = misc()
                    magic, c1 = 1.5 * 2 ** 23, 6.28125
                    F = slice(0, FHID)
                    dve.tensor_scalar(halves(mz2[F, :]), mps[F, m.s, :, 0:TH], bias[F, :], None, ALU.add).then_inc(m.free, 1)
                    dve.wait_ge(m.free, m.free_at)
                    own(dve.tensor_scalar(mk[F, :], mz2[F, :], 1 / (2 * math.pi), magic, ALU.mult, ALU.add))
                    own(dve.tensor_scalar(mk[F, :], mk[F, :], magic, None, ALU.subtract))
                    own(dve.scalar_tensor_tensor(out=mr[F, :], in0=mk[F, :], scalar=-c1, in1=mz2[F, :], op0=ALU.mult, op1=ALU.add))
                    own(dve.scalar_tensor_tensor(out=mr[F, :], in0=mk[F, :], scalar=-(2 * math.pi - c1), in1=mr[F, :],
                                                 op0=ALU.mult, op1=ALU.add))
                    dve.tensor_scalar(mr[F, :], mr[F, :], 3.1415925, -3.1415925, ALU.min, ALU.max).then_inc(sin_in, 1)

                dve.wait_ge(spilled, due(spilled, 32))
                sine(prm("b1"))
                for t in range(5):
                    m = misc()
                    lo_part(fal[:, t, :], mps[:, m.s, 0, :], fah[:, t, :], m.free)
                sine(prm("b2"))
                for c in range(2):
                    t = tile()
                    lo_part(xl[:, 6 + c, :], flat(tps, t.s)[:, 0:T], xh[:, 6 + c, :], t.free)

                decay = cst("decay")
                for o in range(2):
                    for t in range(5):
                        m = misc()
                        dc = decay[:, t * HYW:(t + 1) * HYW]
                        dve.tensor_tensor(hd[:, t, 0:HYW], mps[:, m.s, 0, 0:HYW], dc, ALU.mult)
                        dve.tensor_tensor(hd[:, t, HYW:], mps[:, m.s, 0, HYW:], dc, ALU.mult).then_inc(m.free, 1)
                        dve.wait_ge(m.free, m.free_at)
                        if t in (0, 4):
                            own(dve.memset(hd[0:1, t, HYW:], 0.0))
                        dve.sem_inc(taps_ready, 1)
                    for g in range(2):
                        m = misc()
                        dve.wait_ge(bwd_sum, due(bwd_sum))
                        dve.tensor_tensor(inv[:, g, :], mps[:, m.s, 0, 0:HYW], inv[:, g, :], ALU.add).then_inc(m.free, 1)
                        dve.wait_ge(m.free, m.free_at)
                        own(dve.tensor_scalar(inv[:, g, :], inv[:, g, :], EPS, None, ALU.add))
                        own(dve.reciprocal(inv[:, g, :], inv[:, g, :]))
                    for t in range(5):
                        dve.tensor_tensor(pp[:, 0, :], hd[:, t, 0:HYW], hd[:, t, HYW:], ALU.add)
                        own(dve.tensor_tensor(pp[:, 1, :], hd[:, t, 0:HYW], hd[:, t, HYW:], ALU.subtract))
                        iv = inv[:, t // 4, :]
                        dve.tensor_tensor(pp[:, 0, :], pp[:, 0, :], iv, ALU.mult)
                        own(dve.tensor_tensor(pp[:, 1, :], pp[:, 1, :], iv, ALU.mult))
                        hi2 = tmh[:, t, :].rearrange("p (a c) -> p a c", a=3)[:, 0:3:2, :]
                        lo2 = tml[:, t, :].rearrange("p (a c) -> p a c", a=3)[:, 0:3:2, :]
                        own(dve.tensor_copy(hi2, pp[:, :, :]))
                        own(dve.tensor_tensor(lo2, pp[:, :, :], hi2.bitcast(F32), ALU.subtract))
                    for t in range(5):
                        m = misc()
                        lo_part(tml[:, t, HYW:2 * HYW], mps[:, m.s, 0, 0:HYW], tmh[:, t, HYW:2 * HYW], m.free)
                    for f in range(5):
                        m = misc()
                        dve.wait_ge(parts_out, due(parts_out))
                        ha, ur, us = reb[:, 0:HYW], reb[:, HYW:], mps[:, m.s, 1, 0:HYW]
                        dve.tensor_tensor(pp[:, 0, :], ur, ha, ALU.mult)
                        own(dve.tensor_tensor(pp[:, 1, :], us, hbb[:, :], ALU.mult))
                        own(dve.tensor_tensor(yf[:, 0:HYW], pp[:, 0, :], pp[:, 1, :], ALU.subtract))
                        dve.tensor_tensor(pp[:, 0, :], ur, hbb[:, :], ALU.mult)
                        dve.tensor_tensor(pp[:, 1, :], us, ha, ALU.mult).then_inc(m.free, 1)
                        dve.wait_ge(m.free, m.free_at)
                        dve.tensor_tensor(yf[:, HYW:], pp[:, 0, :], pp[:, 1, :], ALU.add).then_inc(parts_used, 1)
                        dve.wait_ge(parts_used, due(parts_used) + 1)
                        ysl = slice(2 * f, 2 * f + 2)
                        own(dve.tensor_copy(yh[:, ysl, :].rearrange("p a c -> p (a c)"), yf[:, :]))
                        dve.tensor_tensor(yl[:, ysl, :].rearrange("p a c -> p (a c)"), yf[:, :],
                                          yh[:, ysl, :].rearrange("p a c -> p (a c)").bitcast(F32), ALU.subtract)\
                            .then_inc(spec_ready, 1)
                    for c in range(2):
                        t = tile()
                        v = hyx[:, 4 + c, :]
                        dve.scalar_tensor_tensor(out=v, in0=v, scalar=prm("skip", 2 * o + c, 2 * o + c + 1),
                                                 in1=flat(tps, t.s)[:, 0:T], op0=ALU.mult, op1=ALU.add).then_inc(t.free, 1)
                        dve.wait_ge(t.free, t.free_at)
                        dve.tensor_tensor(v, v, hyx[:, 2 * o + c, :], ALU.mult).then_inc(v_ready if o == 0 else z_new, 1)
                    if o == 0:
                        dve.wait_ge(v_ready, due(v_ready, 4))
                for c in range(2):
                    dve.wait_ge(z_new, due(z_new))
                    lo_part(xl[:, c, :], hyx[:, 4 + c, :], xh[:, c, :], z_split)

                for k in range(2):
                    m = slots.misc()
                    dve.wait_ge(rms_out, due(rms_out))
                    dve.reciprocal(ars[:, k, :], ars[:, k, :]).then_inc(m.free, 1)
                    dve.wait_ge(m.free, m.free_at)
                for k, (src, g) in ((2, (kvr[:, :], prm("kv_g"))), (0, (qa[:, 0, :], prm("q_g", 0, 1))),
                                    (1, (qa[:, 1, :], prm("q_g", 1, 2)))):
                    own(dve.tensor_tensor(art[:, k, :], src, ars[:, 1 if k == 2 else 0, :], ALU.mult))
                    dve.tensor_scalar(art[:, k, :], art[:, k, :], g, None, ALU.mult).then_inc(low_ready, 1)
                    dve.wait_ge(low_ready, due(low_ready))
                R, R2 = slice(NOPE, QK), slice(QK, P)
                rope = cst("rope")
                dve.tensor_tensor(krt[R, 0:TL], krr[R2, 0:TL], rope[R2, :], ALU.mult)
                own(dve.tensor_tensor(kro[R, 0:TL], krr[R, 0:TL], rope[R, :], ALU.mult))
                dve.tensor_tensor(kro[R, 0:TL], kro[R, 0:TL], krt[R, 0:TL], ALU.add).then_inc(krope_ready, 1)
                dve.wait_ge(krope_ready, due(krope_ready))
                dve.wait_ge(low_hi, due(low_hi, 5))
                for n, (out, src, hi) in enumerate((
                        (ckl[:, 0:T], art[:, 2, :], ckh[:, 0:T]), (ckl[:, T:KEYS], prm("ckv"), ckh[:, T:KEYS]),
                        (kl[R, 0:TL], kro[R, 0:TL], kh[R, 0:TL]), (kl[R, TL:T], krr[R, TL:T], kh[R, TL:T]),
                        (kl[R, T:KEYS], prm("krope")[R, :], kh[R, T:KEYS]))):
                    ins = dve.tensor_tensor(out, src, hi.bitcast(F32), ALU.subtract)
                    if n == 1:
                        ins.then_inc(low_split, 1)
                ins.then_inc(low_split, 1)
                dve.wait_ge(low_split, due(low_split, 2))
                dve.sem_inc(low_ready, 1)
                due(low_ready)
                due(low_split, 2)
                dve.wait_ge(stored, due(stored, 32))
                for k in range(2):
                    dve.wait_ge(low_hi, due(low_hi))
                    dve.tensor_tensor(qnl[:, k, :], art[:, k, :], qnh[:, k, :].bitcast(F32), ALU.subtract).then_inc(low_split, 1)
                with due.loop("heads", 2) as i:
                    for pair in range(2):
                        for j in range(2):
                            t = tile()
                            dve.wait_ge(q_copy, due(q_copy))
                            for bank, c0, c1, t0, t1, g in SEGMENTS[:2]:
                                dve.tensor_tensor(krt[R, t0:t1], tps[R2, t.s, bank, c0:c1], rope[R2, t0:t1], ALU.mult)
                                ins = dve.tensor_tensor(kro[R, t0:t1], tps[R, t.s, bank, c0:c1], rope[R, t0:t1], ALU.mult)
                            own(ins)
                            dve.tensor_tensor(qf[R, j, 0:TL], kro[R, 0:TL], krt[R, 0:TL], ALU.add).then_inc(t.free, 1)
                            dve.wait_ge(t.free, t.free_at)
                            dve.sem_inc(q_roped, 1)
                            m = misc()
                            lo_part(halves(kl[0:NOPE, :]), mps[0:NOPE, m.s, :, 0:KEYS // 2], halves(kh[0:NOPE, :]), m.free)
                            if j == 0:
                                m = misc()
                                lo_part(halves(vl[:, :]), mps[:, m.s, :, 0:KEYS // 2], halves(vh[:, :]), m.free)
                            lo_part(ql[0:QK, j, :], qf[0:QK, j, :], qh[0:QK, j, :], q_split)

                            def softmax(qt):
                                m = misc()
                                n = TL + PAST if qt < 4 else TC
                                own(dve.tensor_reduce(stat[:, qt:qt + 1], flat(mps, m.s)[:, 0:n], AX.X, ALU.max))
                                dve.tensor_scalar(stat[:, 5 + qt:6 + qt], stat[:, qt:qt + 1], -QK ** -0.5, None, ALU.mult)\
                                    .then_inc(prob_in, 1)
                                dve.wait_ge(m.free, m.free_at)
                                own(dve.reciprocal(stat[:, qt:qt + 1], stat[:, 10 + qt:11 + qt]))
                                p = pm[:, qt % 2, 0:n]
                                dve.tensor_scalar(p, p, stat[:, qt:qt + 1], None, ALU.mult).then_inc(prob_ready, 1)

                            def turned(qt):
                                t = tile()
                                if qt < 4:
                                    out, hi = [x_[:, 0:5 * TL].rearrange("p (a t) -> p a t", a=5)[:, :, qt * P:(qt + 1) * P]
                                               for x_ in (ptl, pth)]
                                    lo_part(out, flat(tps, t.s)[:, 0:T].rearrange("p (a t) -> p a t", a=5), hi, t.free)
                                else:
                                    lo_part(ptl[:, 5 * TL:], tps[:, t.s, 0, 0:TC], pth[:, 5 * TL:], t.free)

                            softmax(0)
                            for qt in range(1, 5):
                                softmax(qt)
                                turned(qt - 1)
                            turned(4)
                            t = tile()
                            rows = slice(j * VD, (j + 1) * VD)
                            kk = bass.ds(i * 2 + (2 + pair), 1)
                            lo_part(xl[rows, kk, :].rearrange("p a t -> p (a t)"), flat(tps, t.s)[rows, 0:T],
                                    xh[rows, kk, :].rearrange("p a t -> p (a t)"), t.free)

                with due.loop("gate", KT) as i:
                    gates = [slots.tile() for _ in range(3)]
                    y = yc[:, bass.ds(i, 1), :].rearrange("p a t -> p (a t)")
                    for b in range(3):
                        t = tile()
                        dve.wait_ge(gates[b].free, gates[b].free_at)
                        dve.tensor_tensor(halves(y if b == 0 else prod[:, :]), halves(sgm[:, b, :]), tile2(t), ALU.mult)\
                            .then_inc(t.free, 1)
                        dve.wait_ge(t.free, t.free_at)
                        if b:
                            own(dve.tensor_tensor(y, y, prod[:, :], ALU.add))
                dve.sem_inc(y_done, 1)
                for k in range(KT):
                    lo_part(nl[:, k, :], yc[:, k, :], nh[:, k, :], n_ready, hi_out)
                with due.loop("out", 2) as i:
                    for k in range(4):
                        t = into_h(5, i * 4 + k)
                dve.wait_ge(t.free, t.free_at)
                dve.sem_inc(h_new, 1)
                ffn(1)
                dve.sem_inc(layer_end, 1)

            sum_squares()
            m = slots.misc()
            dve.wait_ge(rms_out, due(rms_out))
            dve.reciprocal(rr[:, :], rs[:, :]).then_inc(m.free, 1)
            dve.wait_ge(m.free, m.free_at)
            fg = cst("final_g")
            for k in range(KT):
                dve.scalar_tensor_tensor(out=h[:, k, :], in0=h[:, k, :], scalar=fg[:, k:k + 1], in1=rr[:, :],
                                         op0=ALU.mult, op1=ALU.mult).then_inc(y_ready, 1)


def transform_tables():
    def odd(n, scale=1.0):
        a = np.pi * np.outer(np.arange(n), np.arange(n) + 0.5) / n
        return np.cos(a) * scale, np.sin(a) * scale

    def whole(n, scale):
        a = 2 * np.pi * (np.outer(np.arange(n), np.arange(n)) % n) / n
        return np.cos(a) * scale, np.sin(a) * scale

    def panel(m):
        return m.reshape(4, P, 512).transpose(1, 0, 2).reshape(P, PANEL)

    c, s = odd(TL)
    fc, fs = whole(TL, (TL * 64) ** -0.5)
    tables = np.stack([panel(m) for m in (c, s, c.T / TL, s.T / TL, fc, -fs)])
    cc, cs = odd(TC)
    c64, s64 = whole(64, 1.0)
    z = np.zeros((64, 64))
    bd = [np.block([[m, z], [z, m]]) for m in (c64, s64)]
    gc, gs = whole(TC, (TC * 64) ** -0.5)
    small = np.concatenate([cc, cs, cc.T / TC, cs.T / TC] + bd + [gc, -gs], axis=1)
    return tables.astype(np.float32), small.astype(np.float32)


def filter_features(n):
    t = np.arange(n, dtype=np.float32)
    tn = t / np.float32(n - 1)
    w = np.float32(2.0 * math.pi) * t / np.float32(n)
    bands = np.linspace(1e-4, NB - 1, NB, dtype=np.float32)
    a = (w[:, None] * bands[None, :]).astype(np.float32)
    f = np.concatenate([tn[:, None], np.cos(a), -np.sin(a)], axis=1)
    deltas = np.linspace(math.log(1e-2) / 1.5, math.log(1e-2) / 0.3, HYW, dtype=np.float32)
    return f.astype(np.float32), np.exp(-tn[:, None] * np.abs(deltas)[None, :]).astype(np.float32)


def constants():
    cst = np.zeros((P, NCST), np.float32)

    def put(name, a):
        cst[:a.shape[0], CST[name][0]:CST[name][0] + a.shape[1]] = a

    (f1, d1), (f2, d2) = filter_features(TL), filter_features(TC)
    put("decay", np.concatenate([d1[t * P:(t + 1) * P] for t in range(4)] + [d2], axis=1))
    n_freq = ROPE // 4
    inv = (10000.0 ** (-np.arange(n_freq, dtype=np.float32) / n_freq)).astype(np.float32)
    tok = np.arange(TL)
    ang = [(tok // GRID_W)[:, None] * inv[None], (tok % GRID_W)[:, None] * inv[None]]
    cos = np.concatenate([np.cos(a) for a in ang for _ in range(2)], axis=1)
    sin = np.concatenate([sg * np.sin(a) for a in ang for sg in (-1, 1)], axis=1)
    rope = np.zeros((P, TL), np.float32)
    rope[NOPE:QK], rope[QK:] = cos.T, sin.T
    put("rope", rope)
    put("ident", np.eye(P, dtype=np.float32))
    put("ones", np.ones((P, P), np.float32))
    put("sel", np.array([[1, 0], [0, 1], [1, 0], [0, 1]], np.float32))
    put("eps", np.full((P, 1), EPS, np.float32))
    feats = np.zeros((P, T), np.float32)
    feats[:17, :TL], feats[:17, TL:] = f1.T, f2.T
    return cst, feats


def blocks(w):
    k, m = w.shape
    return w.reshape(k // P, P, m // P, P).transpose(0, 2, 1, 3)


def as_panel(bs):
    return np.concatenate(bs, axis=1)


def feature_major(a):
    return np.ascontiguousarray(a.T.reshape(-1, P, a.shape[0]).transpose(1, 0, 2))


def lay_out(inp):
    f = np.float32
    swap = np.concatenate([np.arange(8, 16), np.arange(8), np.arange(24, 32), np.arange(16, 24)])
    w_ada = inp["w_ada"].reshape(DEPTH, KT, P, 36, 256).transpose(0, 3, 2, 1, 4).reshape(DEPTH * 36, P, PANEL)
    up = inp["w_ffn_up"].reshape(DEPTH, 2, KT, P, 2, HT, P)
    w_up = up.transpose(0, 1, 5, 3, 4, 2, 6).reshape(DEPTH * 2 * HT, P, PANEL)
    down, at = [], 0
    for n in CHUNKS:
        d = inp["w_ffn_down"][:, :, at * P:(at + n) * P].reshape(DEPTH, 2, n, P, 4, 2, P)
        down.append(d.transpose(0, 1, 4, 3, 5, 2, 6).reshape(DEPTH, 2, 4, P, 2 * n * P))
        at += n
    w_down8 = np.stack(down[:2], axis=2).reshape(DEPTH * 2 * 8, P, PANEL)
    w_down6 = down[2].reshape(DEPTH * 2 * 4, P, 2 * 6 * P)
    w_mix, w_qkv, w_gate, w_out, par = [], [], [], [], []
    for l in range(DEPTH):
        w = inp["w_in"][l]
        zero = np.zeros((D, NOPE), f)
        kr = w[:, 1152:1184]
        cols = [w[:, 1184:1440], w[:, 0:768], w[:, 768:1152], np.concatenate([zero, kr, kr[:, swap]], axis=1)]
        b = blocks(np.concatenate(cols, axis=1))
        w_mix += [as_panel([b[k, m] for m in (2 * i, 2 * i + 1) for k in range(KT)]) for i in range(6)]
        qb, kvb = inp["w_qb"][l].reshape(2, P, HEADS, QK), inp["w_kvb"][l].reshape(P, HEADS, NOPE + VD)
        for i in range(4):
            hs = (2 * i, 2 * i + 1)
            bs = [np.concatenate([qb[k, :, hh], qb[k, :, hh, NOPE:][:, swap]], axis=1) for hh in hs for k in range(2)]
            bs += [np.concatenate([kvb[:, hh, :NOPE], np.zeros((P, P - NOPE), f)], axis=1) for hh in hs]
            bs += [np.concatenate([kvb[:, hh, NOPE:] for hh in hs], axis=1)]
            w_qkv.append(as_panel(bs))
        g = blocks(w[:, 1440:])
        ys = [blocks(inp[n][l]) for n in ("w_hy_out", "w_mla_o", "w_fnet")]
        for m in range(KT):
            w_gate.append(as_panel([g[k, b_ * KT + m] for b_ in range(2) for k in range(KT)]))
            w_gate.append(as_panel([g[k, 2 * KT + m] for k in range(KT)] + [y[k, m] for y in ys for k in range(y.shape[0])]))
        wo = blocks(inp["w_out"][l])
        w_out += [as_panel([wo[k, m] for m in (2 * i, 2 * i + 1) for k in range(KT)]) for i in range(4)]
        p = np.zeros((P, NPAR), f)

        def put(name, a, row=0):
            p[row:row + a.shape[0], PAR[name][0]:PAR[name][0] + a.shape[1]] = a

        put("b_ada", np.repeat(inp["b_ada"][l].reshape(72, P).T, 2, axis=1))
        put("norm_g", np.repeat(inp["norm_g"][l].reshape(24, P).T, 2, axis=1))
        cw = np.concatenate([inp["hy_conv_w"][l], inp["hy_conv_b"][l][None]], axis=0)
        put("conv", cw.reshape(4, 6, P).transpose(2, 1, 0).reshape(P, 24))
        put("skip", inp["hy_skip"][l].reshape(4, P).T)
        put("q_g", inp["q_norm_g"][l].reshape(2, P).T)
        put("kv_g", inp["kv_norm_g"][l].reshape(1, P).T)
        put("b1", inp["hy_filt_b1"][l][:, None])
        put("b2", inp["hy_filt_b2"][l][:, None])
        put("w1", inp["hy_filt_w1"][l])
        put("w2", inp["hy_filt_w2"][l])
        put("ckv", inp["cache_ckv"][0, l].T)
        put("krope", inp["cache_krope"][0, l].T, NOPE)
        w3 = inp["hy_filt_w3"][l].reshape(FHID, 2, 2, HYW)
        put("w3", w3.transpose(0, 2, 1, 3).reshape(FHID, 4 * HYW))
        par.append(p)
    x = np.concatenate([inp["x_sample"][0], inp["x_prompt"][0]], axis=0)
    cv = np.stack([inp["c"][0], inp["c_ctx"]], axis=0)
    tables, small = transform_tables()
    cst, feats = constants()
    for k in range(KT):
        cst[:, CST["final_g"][0] + k] = inp["final_g"][k * P:(k + 1) * P]
    out = dict(x=feature_major(x), w_ada=w_ada, w_up=w_up, w_down8=w_down8, w_down6=w_down6, w_mix=np.stack(w_mix),
               w_qkv=np.stack(w_qkv), w_gate=np.stack(w_gate), w_out=np.stack(w_out), tables=tables, small=small, cst=cst,
               cvec=feature_major(cv), feats=feats, par=np.stack(par))
    return {k: np.ascontiguousarray(v, dtype=f) for k, v in out.items()}


OUTS = [("y", (P, KT, T)), ("ckv", (DEPTH, P, TC)), ("krope", (DEPTH, ROPE, TC))]


def build(nc, arrays, per_pass):
    a = {n: nc.dram_tensor(f"in_{n}", v.shape, F32, kind="ExternalInput").ap() for n, v in arrays.items()}
    o = {n: nc.dram_tensor(f"out_{n}", s, F32, kind="ExternalOutput").ap() for n, s in OUTS}
    program(nc, per_pass, a["x"], a["w_ada"], a["w_up"], (a["w_down8"], a["w_down6"]), a["w_mix"], a["w_qkv"], a["w_gate"],
            a["w_out"], a["tables"], a["small"], a["cst"], a["cvec"], a["feats"], a["par"], o["y"], o["ckv"], o["krope"])


def kernel(**inputs):
    import concourse.bacc as _bacc
    from concourse.bass_utils import run_bass_kernel_spmd as _run

    arrays = lay_out({k: np.asarray(v) for k, v in inputs.items()})
    per_pass = {}
    for _ in range(2):
        nc = _bacc.Bacc("TRN2", target_bir_lowering=False, num_devices=1)
        build(nc, arrays, per_pass)
    r = _run(nc, [{f"in_{n}": v for n, v in arrays.items()}], core_ids=[0]).results[0]
    y = r["out_y"].transpose(1, 0, 2).reshape(D, T).T
    ckv, krope = r["out_ckv"].transpose(0, 2, 1), r["out_krope"].transpose(0, 2, 1)
    return (np.ascontiguousarray(y[None, TL:]), np.ascontiguousarray(y[None, :TL]), np.ascontiguousarray(ckv[None]),
            np.ascontiguousarray(krope[None]))
```

```python
import math
from contextlib import ExitStack, contextmanager

import numpy as np
import concourse.bass as bass
import concourse.mybir as mybir

F32 = mybir.dt.float32
F32R = mybir.dt.float32r
ALU = mybir.AluOpType
ACT = mybir.ActivationFunctionType
AX = mybir.AxisListType

P = 128
D = 1024
KT = D // P
TL, TC = 512, 128
T = TL + TC
TH = T // 2
DEPTH = 2
PAST = 128
HYW = 256
FW = 256
NB = 8
FHID = 64
HEADS = 8
NOPE, ROPE, VD = 64, 32, 64
QK = NOPE + ROPE
KEYS = T + PAST
DFF = 2816
HT = DFF // P
CHUNKS = [8, 8, 6]
EPS = 1e-6
PANEL = 2048
FQ = TL // P
GRID_W = 64

PAR = {}
_at = 0
for _n, _w in [("b_ada", 144), ("norm_g", 48), ("conv", 24), ("skip", 4), ("q_g", 2), ("kv_g", 1), ("b1", 1), ("b2", 1),
               ("w1", FHID), ("w2", 2 * FHID), ("ckv", PAST), ("w3", 4 * HYW)]:
    PAR[_n] = (_at, _at + _w)
    _at += _w
NPAR = _at
PAR["krope"] = PAR["w2"]
CST = {}
_at = 0
for _n, _w in [("decay", 5 * HYW), ("rope", TL), ("ident", P), ("ones", P), ("sel", 2), ("eps", 1), ("final_g", KT)]:
    CST[_n] = (_at, _at + _w)
    _at += _w
NCST = _at
SM_C, SM_S, SM_CI, SM_SI, SM_BD, SM_FC, SM_FS, NSM = 0, 128, 256, 384, 512, 768, 896, 1024

SEGMENTS = [(0, 0, TH, 0, TH, 0), (1, 0, TL - TH, TH, TL, 0), (1, TL - TH, TH, TL, T, 1)]
GROUPS = [(0, 0, TL), (1, TL, T)]
FFN_PANELS = sum(c + 4 for c in CHUNKS)
LAYER_PANELS = 36 + 2 * FFN_PANELS + 6 + 2 + 8 + 4 + 16 + 4


def head_order(heads=4, ada_at=((0, 2), (0, 3), (0, 4), (2, 2), (2, 3), (2, 4))):
    order = [("Q", 0), ("K", 0), ("QS", 0), ("V", 0)]
    tiles = [(h, qt) for h in range(heads) for qt in range(5)]
    held, n_ada = None, 0
    for n, (h, qt) in enumerate(tiles):
        order.append(("S", n))
        if n >= 1:
            order.append(("N", n - 1))
        if held is not None:
            order.append(("B", held))
            held = None
        if n >= 2:
            order.append(("T", n - 2))
            if tiles[n - 2][1] == 4:
                g = tiles[n - 2][0]
                order.append(("P", g))
                if g % 2 and g + 1 < heads:
                    order.append(("V", (g + 1) // 2))
        if qt == 1 and h + 1 < heads:
            order += [("Q", h + 1), ("K", h + 1), ("QS", h + 1)]
        if (h, qt) in ada_at:
            order.append(("A", n_ada))
            held, n_ada = n_ada, n_ada + 1
    n = len(tiles) - 1
    return order + [("N", n), ("T", n - 1), ("T", n), ("P", heads - 1)]


HEAD_ORDER = head_order()
ADA_FIRST, ADA_UP, ADA_HEADS = 8, 16, 12
MIX_ORDER = [("mlp", 0), ("channels", 0), ("mlp", 1), ("taps", 0), ("norms", 0), ("tokens", 0), ("combine", 0),
             ("turn", 0), ("taps", 1), ("norms", 1), ("forward", 0), ("combine", 1), ("inverse", 0),
             ("turn", 1), ("forward", 1), ("inverse", 1)]


class Due:

    entered = None

    def __init__(self, engine, eng, per_pass, start):
        self.engine, self.eng, self.per_pass, self.n, self.loops = engine, eng, per_pass, dict(start), []

    def __call__(self, sem, k=1):
        name = sem.name
        self.n[name] = self.n.get(name, 0) + k
        value = self.n[name]
        for key, reg in self.loops:
            step = self.per_pass.get(key, {}).get(name, 0)
            if step:
                value = reg * step + value
        return value

    def now(self, sem):
        return self(sem, 0)

    @contextmanager
    def loop(self, label, count):
        key, before = (self.engine, label), dict(self.n)
        self.eng.sem_inc(self.entered, 1)
        with self.eng.Fori(0, count) as reg:
            self.loops.append((key, reg))
            yield reg
            self.loops.pop()
        step = {s: v - before.get(s, 0) for s, v in self.n.items()}
        self.per_pass[key] = step
        for s, v in step.items():
            self.n[s] += (count - 1) * v


def program(nc, per_pass, x, w_ada, w_up, w_down, w_mix, w_qkv, w_gate, w_out, tables, small, cst_in, cvec, feats, par,
            y_out, ckv_out, krope_out):
    ctx = ExitStack()
    with ctx:
        def sem(name):
            return ctx.enter_context(nc.semaphore(name))

        base = (nc.sbuf_base + 63) // 64 * 64

        def place(at, *specs):
            out = []
            for name, shape, dt in specs:
                out.append(nc.alloc_sbuf_tensor_at(name, shape, dt, offset=at))
                at += 4 * int(np.prod(shape[1:]))
                at = (at + 31) // 32 * 32
            return out, at

        (h, raw, whi, wlo), at = place(base, ("h", [P, KT, T], F32), ("raw", [P, 2, PANEL], F32),
                                       ("whi", [P, 2, PANEL], F32R), ("wlo", [P, 2, PANEL], F32R))
        (smh, sml, cs_t, pr, ada, gm), at = place(
            at, ("small_hi", [P, NSM], F32R), ("small_lo", [P, NSM], F32R), ("constants", [P, NCST], F32),
            ("params", [P, NPAR], F32), ("ada_t", [P, 72, 2], F32), ("norm_scale", [P, 24, 2], F32))
        (stat, csr), at = place(at, ("softmax_stats", [P, 16], F32), ("c_split", [P, 4 * KT + P], F32R))
        X0 = at
        (xh, xl), at = place(X0, ("x_hi", [P, 8, T], F32R), ("x_lo", [P, 8, T], F32R))
        N0 = at
        (nh, nl), at = place(N0, ("n_hi", [P, KT, T], F32R), ("n_lo", [P, KT, T], F32R))
        W0 = at
        (sg, hf, acc, sq, rs, rr, tn), end1 = place(
            W0, ("gate_act", [P, 2, T], F32), ("hidden", [P, 2, T], F32), ("sq_sum", [P, T], F32),
            ("squares", [P, T], F32), ("rms", [P, T], F32), ("inv_rms", [P, T], F32), ("scaled", [P, 2, T], F32))
        (csil, cvt), _ = place(W0, ("c_silu", [P, KT, 2], F32), ("c_raw", [P, KT, 2], F32))
        R0 = (nc.sbuf_usable_end - 4 * TL) // 64 * 64
        (row,), _ = place(R0, ("ada_rows", [P, 2, 256], F32))
        (krt,), _ = place(R0, ("rope_tmp", [P, TL], F32))
        (smraw,), _ = place(N0, ("small_raw", [P, NSM], F32))
        (qa, kvr, krr), A0 = place(W0, ("q_low", [P, 2, T], F32), ("kv_low", [P, T], F32), ("k_rope_h2", [P, T], F32))
        (qnh, qnl), _ = place(W0, ("qn_hi", [P, 2, T], F32R), ("qn_lo", [P, 2, T], F32R))
        (hyx,), wt = place(A0, ("hyena_x", [P, 6, T], F32))
        UP = T + 4
        (upad, ft), end2 = place(wt, ("conv_pad", [P, 2, UP], F32), ("features", [P, T], F32))
        (mz, mz2, mk, mr), _ = place(N0, ("sin_h", [P, T], F32), ("sin_z", [P, T], F32), ("sin_k", [P, T], F32),
                                     ("sin_r", [P, T], F32))
        (reb, hbb, pp, yf, ab, inv), end3 = place(
            wt, ("re_part", [P, 2 * HYW], F32), ("im_part", [P, HYW], F32), ("products", [P, 2, HYW], F32),
            ("y_freq", [P, 2 * HYW], F32), ("abs_filter", [P, 2 * HYW], F32), ("inv_l1", [P, 2, HYW], F32))
        XT = 4 * T
        (fnh,), _ = place(X0, ("fnet_in_hi", [P, 2, T], F32R))
        (fah, ), _ = place(X0 + 2 * XT, ("fnet_mid_hi", [P, 5, 512], F32R))
        (fnl,), _ = place(X0 + 8 * XT, ("fnet_in_lo", [P, 2, T], F32R))
        (fal, ), _ = place(X0 + 10 * XT, ("fnet_mid_lo", [P, 5, 512], F32R))
        (tmh, tml, hd), _ = place(N0, ("tok_hi", [P, 5, 3 * HYW], F32R), ("tok_lo", [P, 5, 3 * HYW], F32R),
                                  ("taps", [P, 5, 2 * HYW], F32))
        (yh,), _ = place(X0 + 2 * XT, ("spec_hi", [P, 10, HYW], F32R))
        (yl,), _ = place(X0 + 10 * XT, ("spec_lo", [P, 10, HYW], F32R))
        NPT = 5 * TL + TC
        (pth, ptl, qh, ql, qf, kh1, kl1), _ = place(
            N0, ("probs_t_hi", [P, NPT], F32R), ("probs_t_lo", [P, NPT], F32R), ("q_hi", [P, 2, T], F32R),
            ("q_lo", [P, 2, T], F32R), ("q_f32", [P, T], F32), ("k_hi1", [P, KEYS], F32R), ("k_lo1", [P, KEYS], F32R))
        (asq, ars, art), _ = place(N0, ("att_sq", [P, 3, T], F32), ("att_rms", [P, 2, T], F32), ("att_scaled", [P, 3, T], F32))
        (kh, kl, vh, vl, pm, ckh, ckl), _ = place(
            A0, ("k_hi", [P, KEYS], F32R), ("k_lo", [P, KEYS], F32R), ("v_hi", [P, KEYS], F32R), ("v_lo", [P, KEYS], F32R),
            ("probs", [P, 2, T], F32), ("ckv_hi", [P, KEYS], F32R), ("ckv_lo", [P, KEYS], F32R))
        (kro,), _ = place(A0 + 4 * 4 * KEYS, ("k_roped", [P, T], F32))
        khs, kls = (kh, kh1), (kl, kl1)
        assert end1 <= R0 and A0 + 16 * KEYS + 8 * T + 8 * KEYS <= R0
        (yc, sgm, prod), _ = place(W0, ("mixed", [P, KT, T], F32), ("branch_gate", [P, 3, T], F32), ("branch", [P, T], F32))

        tps = ctx.enter_context(nc.psum_tensor("tile_psum", [P, 2, 2, 512], F32))
        mps = ctx.enter_context(nc.psum_tensor("misc_psum", [P, 2, 2, 512], F32))

        def flat(ps, s):
            return ps[:, s].rearrange("p a b -> p (a b)")

        def halves(ap):
            return ap.rearrange("p (a b) -> p a b", a=2)

        def cst(name):
            return cs_t[:, CST[name][0]:CST[name][1]]

        def prm(name, a=0, b=None):
            lo, hi = PAR[name]
            return pr[:, lo + a:(hi if b is None else lo + b)]

        csr4 = csr[:, 0:4 * KT].rearrange("p (k c) -> p k c", c=4)
        ident, ones, eps, sel = cst("ident"), cst("ones"), cst("eps"), cst("sel")

        def probs(n):
            return prm("w3", 0, T) if n % 3 == 2 else pm[:, n % 3, :]

        def smat(ap, at, n=P):
            return ap[:, at:at + n]

        loaded = [sem(f"panel_loaded{s}") for s in range(2)]
        hi_ready = sem("panel_hi_ready")
        lo_ready = sem("panel_lo_ready")
        tile_done = [sem(f"tile_done{s}") for s in range(2)]
        tile_free = [sem(f"tile_free{s}") for s in range(2)]
        misc_done = [sem(f"misc_done{s}") for s in range(2)]
        misc_free = [sem(f"misc_free{s}") for s in range(2)]
        dve_own = sem("dve_own")
        consts_in, small_in, par_in = sem("constants_in"), sem("small_in"), sem("params_in")
        x_in, c_in, feat_in = sem("x_in"), sem("c_in"), sem("features_in")
        small_hi, small_split = sem("small_hi"), sem("small_split")
        c_clear, silu_out, c_hi, c_split = sem("c_split_clear"), sem("silu_c_out"), sem("c_hi"), sem("c_split_ready")
        sin_in, sin_out = sem("sin_in"), sem("sin_out")
        rows_out, layer_end = sem("ada_rows_out"), sem("layer_end")
        sq_out, sq_used, sum_ready = sem("squares_out"), sem("squares_used"), sem("sq_sum_ready")
        rms_out, t_ready, hi_out, n_ready = sem("rms_out"), sem("scaled_ready"), sem("n_hi_out"), sem("n_ready")
        hid_hi, hid_ready = sem("hidden_hi"), sem("hidden_ready")
        spilled, back = sem("n_spilled"), sem("n_back")
        conv_in, conv_used, v_ready = sem("conv_in"), sem("conv_used"), sem("v_ready")
        taps_ready, abs_ready, abs_used, bwd_sum = sem("taps_ready"), sem("abs_ready"), sem("abs_used"), sem("bwd_sum_out")
        filter_ready = sem("filter_split")
        parts_out, parts_used, spec_ready = sem("spectrum_parts"), sem("spectrum_parts_used"), sem("spectrum_ready")
        op_hi, z_new, z_split, y_done = sem("operand_hi"), sem("z_new"), sem("z_split"), sem("y_done")
        asq_ready, low_ready, low_hi, low_split = sem("low_squares"), sem("low_scaled"), sem("low_hi"), sem("low_split")
        krope_ready, q_copy, q_roped, q_split = sem("k_roped_ready"), sem("q_copied"), sem("q_roped_ready"), sem("q_split")
        prob_in, prob_ready = sem("neg_max_ready"), sem("probs_ready")
        y_ready, stored = sem("y_ready"), sem("outputs_stored")
        Due.entered = sem("loop_entered")
        credit = {lo_ready.name: 2, q_split.name: 1}

        n_keep = [nc.dram_tensor(f"n_keep{i}", [P, KT, T], F32).ap() for i in range(2)]

        class Slot:

            def __init__(self, s, done, free, due):
                self.s, self.done, self.free = s, done, free
                self.done_at = due(done)
                self.reusable_at = due(free)
                self.free_at = self.reusable_at + 1

        class Slots:

            def __init__(self, due):
                self.due, self.tiles, self.miscs = due, 0, 0

            def tile(self):
                s, self.tiles = self.tiles % 2, self.tiles + 1
                return Slot(s, tile_done[s], tile_free[s], self.due)

            def misc(self):
                s, self.miscs = self.miscs % 2, self.miscs + 1
                return Slot(s, misc_done[s], misc_free[s], self.due)

        block = ctx.enter_context(nc.Block())

        @block.sync
        def _(sp):
            due = Due("sp", sp, per_pass, {})
            slot = [0]

            def load(src, cols):
                s = slot[0] % 2
                slot[0] += 1
                sp.wait_ge(lo_ready, due(lo_ready))
                sp.dma_start(raw[:, s, 0:cols], src).then_inc(loaded[s], 16)

            def pairs(label, src, first, count, cols=PANEL):
                with due.loop(label, count // 2) as i:
                    for k in range(2):
                        load(src(i, first + k), cols)

            sp.dma_start(cs_t[:, :], cst_in).then_inc(consts_in, 16)
            sp.dma_start(smraw[:, :], small).then_inc(small_in, 16)
            sp.dma_start(h[:, :, :], x).then_inc(x_in, 16)
            with due.loop("layer", DEPTH) as l:
                def ada_panel(n):
                    load(w_ada[bass.ds(l * 36 + n, 1)].rearrange("a p n -> (a p) n"), PANEL)

                with due.loop("ada", ADA_FIRST // 2) as i:
                    for k in range(2):
                        ada_panel(i * 2 + k)

                def ffn(f):
                    at = 0
                    for c, n in enumerate(CHUNKS):
                        with due.loop(f"up{f}{c}", n // 2) as i:
                            for k in range(2):
                                if f == 0 and c < 2:
                                    ada_panel(i * 2 + (ADA_FIRST + c * ADA_UP // 2 + k))
                                load(w_up[bass.ds((l * 2 + f) * HT + i * 2 + (at + k), 1)].rearrange("a p n -> (a p) n"), PANEL)
                        wd = w_down[0] if n == 8 else w_down[1]
                        base_row = (l * 2 + f) * 8 + 4 * c if n == 8 else (l * 2 + f) * 4
                        pairs(f"down{f}{c}", lambda i, k: wd[bass.ds(base_row + i * 2 + k, 1)]
                              .rearrange("a p n -> (a p) n"), 0, 4, 2 * n * P)
                        at += n

                ffn(0)
                pairs("mix", lambda i, k: w_mix[bass.ds(l * 6 + i * 2 + k, 1)].rearrange("a p n -> (a p) n"), 0, 6)
                for t in (4, 5) + (0, 1, 2, 3) * 2:
                    load(tables[t], PANEL)
                with due.loop("heads", 2) as i:
                    for what, n in HEAD_ORDER:
                        if what == "A":
                            ada_panel(i * (ADA_HEADS // 2) + (ADA_FIRST + ADA_UP + n))
                        if what == "Q" and n % 2 == 0:
                            load(w_qkv[bass.ds(l * 4 + i * 2 + n // 2, 1)].rearrange("a p n -> (a p) n"), 7 * P)
                pairs("gate", lambda i, k: w_gate[bass.ds(l * 16 + i * 2 + k, 1)].rearrange("a p n -> (a p) n"), 0, 16)
                pairs("out", lambda i, k: w_out[bass.ds(l * 4 + i * 2 + k, 1)].rearrange("a p n -> (a p) n"), 0, 4)
                ffn(1)
            for k in range(2):
                load(tables[0][:, 0:P], P)
            sp.wait_ge(y_ready, due(y_ready, 8))
            sp.dma_start(y_out, h[:, :, :]).then_inc(stored, 16)
            sp.wait_ge(stored, 16 + DEPTH * 32)

        @block.gpsimd
        def _(pool):
            due = Due("pool", pool, per_pass, {})
            with due.loop("panels", DEPTH * LAYER_PANELS // 2 + 1):
                for s in range(2):
                    pool.wait_ge(hi_ready, due(hi_ready))
                    pool.tensor_tensor(wlo[:, s, :], raw[:, s, :], whi[:, s, :].bitcast(F32), ALU.subtract)\
                        .then_inc(lo_ready, 1)

        @block.tensor
        def _(pe):
            due = Due("pe", pe, per_pass, credit)
            slots = Slots(due)
            at = [0]

            def panel():
                s = at[0] % 2
                at[0] += 1
                pe.wait_ge(lo_ready, due(lo_ready))
                return s

            def blk(s, b, n=P):
                return whi[:, s, b * P:b * P + n], wlo[:, s, b * P:b * P + n]

            def mm3(outs, w, xs, first, last):
                for n, (a, b) in enumerate(((0, 0), (0, 1), (1, 0))):
                    for o, x_ in zip(outs, xs):
                        ins = pe.matmul(o, w[a], x_[b], start=first and n == 0, stop=last and n == 2)
                return ins

            def tile():
                return taken(slots.tile()).s

            def taken(slot):
                pe.wait_ge(slot.free, slot.reusable_at)
                return slot

            def misc():
                return taken(slots.misc()).s

            def all_read(frees):
                for f in frees:
                    pe.wait_ge(f, due.now(f) + 1)

            def xs_of(hi, lo, k):
                return [(hi[:, k, j * TH:(j + 1) * TH], lo[:, k, j * TH:(j + 1) * TH]) for j in range(2)]

            def gemm(s, b0, hi, lo, k0, n, each=None):
                t = tile()
                for k in range(n):
                    if each is not None:
                        pe.wait_ge(each[0], each[1] + (k + 1))
                    ins = mm3([tps[:, t, j, 0:TH] for j in range(2)], blk(s, b0 + k), xs_of(hi, lo, k0 + k),
                              k == 0, k == n - 1)
                ins.then_inc(tile_done[t], 1)

            def column_sums(ready, rhs, n=1):
                m = misc()
                pe.wait_ge(ready, due(ready))
                for k in range(n):
                    for j in range(2):
                        ins = pe.matmul(mps[:, m, j, 0:TH], ones, rhs[k][:, j * TH:(j + 1) * TH],
                                        start=k == 0, stop=k == n - 1)
                ins.then_inc(misc_done[m], 1)

            def coming(sem, n):
                now = due.now(sem)
                due(sem, n)
                return sem, now

            def ada_a():
                s = panel()
                m = misc()
                for kt in range(KT):
                    for n, w in enumerate((whi, wlo)):
                        ins = pe.matmul(mps[:, m, 0, 0:256], csr[:, 4 * kt:4 * kt + P], w[:, s, kt * 256:(kt + 1) * 256],
                                        start=kt == 0 and n == 0, stop=kt == KT - 1 and n == 1)
                ins.then_inc(misc_done[m], 1)

            def ada_b(k):
                m = misc()
                pe.wait_ge(rows_out, due(rows_out))
                for j in range(2):
                    ins = pe.matmul(mps[:, m, 0, 2 * j:2 * j + 2], row[0:4, k, j * P:(j + 1) * P], sel[0:4, :],
                                    start=True, stop=True)
                ins.then_inc(misc_done[m], 1)

            def ffn(f):
                column_sums(sum_ready, [acc])
                n_coming = coming(n_ready, KT)
                for c, n in enumerate(CHUNKS):
                    with_ada = f == 0 and c < 2
                    with due.loop(f"up{f}{c}", n // 2):
                        for k in range(2):
                            if with_ada:
                                ada_a()
                            s = panel()
                            gemm(s, 0, nh, nl, 0, KT, n_coming if c == 0 and k == 0 else None)
                            gemm(s, KT, nh, nl, 0, KT)
                            if with_ada:
                                ada_b(k)
                    hid_coming = coming(hid_ready, n)
                    with due.loop(f"down{f}{c}", 2):
                        for k in range(2):
                            s = panel()
                            gemm(s, 0, xh, xl, 0, n, hid_coming if k == 0 else None)
                            gemm(s, n, xh, xl, 0, n)

            def transposes(src, tiles):
                m = misc()
                for c in range(2):
                    ins = pe.transpose(mps[:, m, 0, c * P:(c + 1) * P], src[:, 4 + c, tiles * P:(tiles + 1) * P], ident)
                ins.then_inc(misc_done[m], 1)

            pe.wait_ge(consts_in, due(consts_in, 16))
            pe.wait_ge(small_split, due(small_split))
            with due.loop("layer", DEPTH):
                def filter_mlp(w, src, kk, mm=FHID):
                    m = misc()
                    for j in range(2):
                        ins = pe.matmul(mps[0:mm, m, j, 0:TH], w[0:kk, :], src[0:kk, j * TH:(j + 1) * TH],
                                        start=True, stop=True)
                    ins.then_inc(misc_done[m], 1)

                pe.wait_ge(c_split, due(c_split))
                with due.loop("ada", ADA_FIRST // 2):
                    ada_a()
                    ada_a()
                    ada_b(0)
                    ada_b(1)
                ffn(0)

                column_sums(sum_ready, [acc])
                n_coming = coming(n_ready, KT)
                with due.loop("mix", 3):
                    for k in range(2):
                        s = panel()
                        gemm(s, 0, nh, nl, 0, KT, n_coming if k == 0 else None)
                        gemm(s, KT, nh, nl, 0, KT)

                def mlp(n):
                    if n == 0:
                        pe.wait_ge(feat_in, due(feat_in, 16))
                        pe.wait_ge(par_in, due(par_in, 16))
                        filter_mlp(prm("w1"), ft, 17)
                    else:
                        pe.wait_ge(sin_out, due(sin_out))
                        filter_mlp(prm("w2"), mz, FHID, P)

                def channels(_):
                    bdm = [(smat(smh, SM_BD, 256), smat(sml, SM_BD, 256))]
                    all_read(tile_free)
                    for t in range(5):
                        m = misc()
                        for c in range(2):
                            tk = slice(t * P, (t + 1) * P)
                            ins = mm3([mps[:, m, 0, c * 256:(c + 1) * 256]], (fnh[:, c, tk], fnl[:, c, tk]), bdm, True, True)
                        ins.then_inc(misc_done[m], 1)

                def tokens(_):
                    sc, ss = panel(), panel()
                    all_read(misc_free)
                    for c in range(2):
                        t = tile()
                        for part, s in ((0, sc), (1, ss)):
                            lo_c = c * 256 + part * P
                            for tt in range(4):
                                w = (fah[:, tt, lo_c:lo_c + P], fal[:, tt, lo_c:lo_c + P])
                                mm3([tps[:, t, 0, :]], w, [blk(s, 4 * tt, 512)], part == 0 and tt == 0, part == 1 and tt == 3)
                            at_ = SM_FC if part == 0 else SM_FS
                            w = (fah[:, 4, lo_c:lo_c + P], fal[:, 4, lo_c:lo_c + P])
                            ins = mm3([tps[:, t, 1, 0:TC]], w, [(smat(smh, at_), smat(sml, at_))], part == 0, part == 1)
                        ins.then_inc(tile_done[t], 1)

                def taps(o):
                    if o == 0:
                        pe.wait_ge(sin_out, due(sin_out))
                    for t in range(5):
                        m = misc()
                        pe.matmul(mps[:, m, 0, :], krr[0:FHID, t * P:(t + 1) * P],
                                  prm("w3", o * 512, (o + 1) * 512)[0:FHID, :], start=True, stop=True)\
                            .then_inc(misc_done[m], 1)

                def norms(o):
                    for ts in (range(4), range(4, 5)):
                        m = misc()
                        for t in ts:
                            pe.wait_ge(abs_ready, due(abs_ready))
                            pe.matmul(mps[:, m, 0, :], ones, (ab if t % 2 == 0 else yf)[:, :], start=t == ts[0], stop=t == ts[-1])\
                                .then_inc(misc_done[m] if t == ts[-1] else abs_used, 1)

                def turn(o):
                    pe.wait_ge(v_ready, due(v_ready, 2))
                    for t in range(5):
                        transposes(hyx, t)

                def forward(o):
                    sc, ss = panel(), panel()
                    all_read(misc_free)
                    pe.wait_ge(filter_ready, due(filter_ready))
                    for f in range(5):
                        m = misc()
                        for part, (s, col, sm) in enumerate(((sc, 0, SM_C), (ss, HYW, SM_S))):
                            out = [mps[:, m, part, :]]
                            if f < 4:
                                for t in range(4):
                                    w = (whi[:, s, t * 512 + f * P:t * 512 + (f + 1) * P],
                                         wlo[:, s, t * 512 + f * P:t * 512 + (f + 1) * P])
                                    ins = mm3(out, w, [(tmh[:, t, col:col + 512], tml[:, t, col:col + 512])], t == 0, t == 3)
                            else:
                                ins = mm3(out, (smat(smh, sm), smat(sml, sm)),
                                          [(tmh[:, 4, col:col + 512], tml[:, 4, col:col + 512])], True, True)
                        ins.then_inc(misc_done[m], 1)

                def inverse(o):
                    sc, ss = panel(), panel()
                    pe.wait_ge(spec_ready, due(spec_ready, 5))
                    for c in range(2):
                        t = tile()
                        cc = slice(c * P, (c + 1) * P)
                        for part, s in ((0, sc), (1, ss)):
                            for f in range(4):
                                w = (yh[:, 2 * f + part, cc], yl[:, 2 * f + part, cc])
                                mm3([tps[:, t, 0, :]], w, [blk(s, 4 * f, 512)], part == 0 and f == 0, part == 1 and f == 3)
                            w = (yh[:, 8 + part, cc], yl[:, 8 + part, cc])
                            sm = SM_CI if part == 0 else SM_SI
                            ins = mm3([tps[:, t, 1, 0:TC]], w, [(smat(smh, sm), smat(sml, sm))], part == 0, part == 1)
                        ins.then_inc(tile_done[t], 1)

                steps = dict(mlp=mlp, channels=channels, tokens=tokens, taps=taps, norms=norms, turn=turn,
                             forward=forward, inverse=inverse)
                for what, o in MIX_ORDER:
                    if what in steps:
                        steps[what](o)

                column_sums(asq_ready, [asq[:, k, :] for k in range(2)], 2)
                column_sums(asq_ready, [asq[:, 2, :]])
                pe.wait_ge(low_split, due(low_split, 4))
                with due.loop("heads", 2):
                    s = [None, None]
                    keys, vals, turned = [None] * 4, None, [None, None]
                    for what, n in HEAD_ORDER:
                        h_, qt = n // 5, n % 5
                        if what == "Q":
                            if n % 2 == 0:
                                s[n // 2] = panel()
                            t = tile()
                            for k in range(2):
                                ins = mm3([tps[:, t, i, 0:TH] for i in range(2)], blk(s[n // 2], 2 * (n % 2) + k),
                                          xs_of(qnh, qnl, k), k == 0, k == 1)
                            ins.then_inc(tile_done[t], 1)
                        elif what == "K":
                            keys[n] = m = taken(slots.misc())
                            ks = [slice(0, KEYS // 2), slice(KEYS // 2, KEYS)]
                            mm3([mps[:, m.s, i, 0:KEYS // 2] for i in range(2)], blk(s[n // 2], 4 + n % 2),
                                [(ckh[:, i], ckl[:, i]) for i in ks], True, True).then_inc(m.done, 1)
                        elif what == "V":
                            vals = m = taken(slots.misc())
                            for kt in range(6):
                                kk = slice(kt * P, (kt + 1) * P)
                                ins = mm3([mps[:, m.s, kt // 3, (kt % 3) * P:(kt % 3 + 1) * P]], (ckh[:, kk], ckl[:, kk]),
                                          [blk(s[n], 6)], True, True)
                            ins.then_inc(m.done, 1)
                        elif what == "S":
                            if qt == 0:
                                pe.wait_ge(keys[h_].free, keys[h_].free_at)
                                pe.wait_ge(q_split, due(q_split))
                            m = misc()
                            kh_, kl_ = khs[h_ % 2], kls[h_ % 2]
                            w = (qh[0:QK, h_ % 2, qt * P:(qt + 1) * P], ql[0:QK, h_ % 2, qt * P:(qt + 1) * P])
                            if qt < 4:
                                mm3([mps[:, m, 0, :]], w, [(kh_[0:QK, 0:TL], kl_[0:QK, 0:TL])], True, True)
                                ins = mm3([mps[:, m, 1, 0:P]], w, [(kh_[0:QK, T:KEYS], kl_[0:QK, T:KEYS])], True, True)
                            else:
                                ins = mm3([mps[:, m, 0, 0:P]], w, [(kh_[0:QK, TL:T], kl_[0:QK, TL:T])], True, True)
                            ins.then_inc(misc_done[m], 1)
                        elif what == "T":
                            t = taken(slots.tile())
                            turned[t.s] = t
                            pe.wait_ge(prob_ready, due(prob_ready))
                            for kt in range(5 if qt < 4 else 1):
                                ins = pe.transpose(flat(tps, t.s)[:, kt * P:(kt + 1) * P], probs(n)[:, kt * P:(kt + 1) * P], ident)
                            ins.then_inc(t.done, 1)
                        elif what == "P":
                            for t in turned + [vals]:
                                pe.wait_ge(t.free, t.free_at)
                            t = tile()
                            for kt in range(5):
                                vt = kt if kt < 4 else 5
                                kk = slice(vt * P, (vt + 1) * P)
                                mm3([tps[:, t, 0, :]], (vh[:, kk], vl[:, kk]),
                                    [(pth[:, kt * TL:(kt + 1) * TL], ptl[:, kt * TL:(kt + 1) * TL])], kt == 0, kt == 4)
                            mm3([tps[:, t, 1, 0:TC]], (vh[:, TL:T], vl[:, TL:T]), [(pth[:, 5 * TL:], ptl[:, 5 * TL:])], True, True)\
                                .then_inc(tile_done[t], 1)
                        elif what == "A":
                            ada_a()
                        elif what == "B":
                            ada_b(n % 2)

                all_read(tile_free)
                pe.wait_ge(z_split, due(z_split, 2))
                pe.wait_ge(back, due(back, 32))
                with due.loop("gate", KT):
                    s = panel()
                    gemm(s, 0, nh, nl, 0, KT)
                    gemm(s, KT, nh, nl, 0, KT)
                    s = panel()
                    gemm(s, 0, nh, nl, 0, KT)
                    gemm(s, 8, xh, xl, 0, 2)
                    gemm(s, 10, xh, xl, 2, 4)
                    gemm(s, 14, xh, xl, 6, 2)
                n_coming = coming(n_ready, KT)
                with due.loop("out", 2):
                    for k in range(2):
                        s = panel()
                        gemm(s, 0, nh, nl, 0, KT, n_coming if k == 0 else None)
                        gemm(s, KT, nh, nl, 0, KT)
                ffn(1)
            column_sums(sum_ready, [acc])


        @block.scalar
        def _(act):
            due = Due("act", act, per_pass, {})
            slots = Slots(due)
            at = [0]

            def round_panel():
                s = at[0] % 2
                at[0] += 1
                act.wait_ge(loaded[s], due(loaded[s], 16))
                act.activation(whi[:, s, :], raw[:, s, :], ACT.Copy).then_inc(hi_ready, 1)

            def seen(slot):
                act.wait_ge(slot.done, slot.done_at)
                return slot

            def tile():
                return seen(slots.tile())

            def misc():
                return seen(slots.misc())

            def tile2(t, g=False):
                return tps[:, t.s, :, 0:TH]

            def square(m, t=None):
                if t is not None:
                    act.wait_ge(t.free, t.free_at)
                src = h[:, bass.ds(m, 1), :].rearrange("p a t -> p (a t)")
                act.activation(sq[:, :], src, ACT.Square).then_inc(sq_out, 1)

            def root(out, width, m, ready):
                act.activation(halves(out), mps[:, m.s, :, 0:TH], ACT.Sqrt, bias=eps, scale=1.0 / width).then_inc(ready, 1)

            def norm(i):
                root(rs[:, :], D, misc(), rms_out)
                for k in range(KT):
                    act.wait_ge(t_ready, due(t_ready))
                    for g, (_, a, b) in enumerate(GROUPS):
                        ins = act.activation(nh[:, k, a:b], tn[:, k % 2, a:b], ACT.Identity, bias=ada[:, 24 * i + k, g:g + 1])
                    ins.then_inc(hi_out, 1)
                due(n_ready, KT)

            def ada_a(k):
                m = misc()
                act.activation(row[0:4, k, :], mps[0:4, m.s, 0, 0:256], ACT.Copy).then_inc(rows_out, 1)
                round_panel()
                act.wait_ge(rows_out, due(rows_out))
                act.sem_inc(m.free, 1)

            def into_h(label, last):
                with due.loop(label, 2) as i:
                    for k in range(2):
                        t = [slots.tile(), tile()]
                        round_panel()
                        if last:
                            for j in range(2):
                                square(i * 4 + (2 * k + j), t[j])

            def ffn(f):
                norm(2 * f)
                for c, n in enumerate(CHUNKS):
                    with_ada = f == 0 and c < 2
                    with due.loop(f"up{f}{c}", n // 2) as i:
                        for k in range(2):
                            if with_ada:
                                ada_a(k)
                            t = tile()
                            act.activation(halves(sg[:, k, :]), tile2(t), ACT.Silu).then_inc(t.free, 1)
                            t = tile()
                            round_panel()
                            act.wait_ge(t.free, t.free_at)
                            act.activation(xh[:, bass.ds(i * 2 + k, 1), :].rearrange("p a t -> p (a t)"), hf[:, k, :], ACT.Copy)\
                                .then_inc(hid_hi, 1)
                            if with_ada:
                                slots.misc()
                    into_h(f"down{f}{c}", c == 2)

            def split_hi(out, src, ready=op_hi):
                act.activation(out, src, ACT.Copy).then_inc(ready, 1)

            act.wait_ge(small_in, due(small_in, 16))
            split_hi(smh[:, :], smraw[:, :], small_hi)
            act.wait_ge(consts_in, due(consts_in, 16))
            round_panel()
            round_panel()
            act.wait_ge(x_in, due(x_in, 16))
            for k in range(KT):
                if k:
                    act.wait_ge(sq_used, due(sq_used))
                square(k)
            with due.loop("layer", DEPTH) as l:
                act.wait_ge(layer_end, due(layer_end))
                act.dma_start(pr[:, :], par[bass.ds(l, 1)].rearrange("a p n -> (a p) n")).then_inc(par_in, 16)
                act.dma_start(cvt[:, :, :], cvec).then_inc(c_in, 16)
                act.wait_ge(c_in, due(c_in, 16))
                act.activation(csil[:, :, :], cvt[:, :, :], ACT.Silu).then_inc(silu_out, 1)
                act.wait_ge(silu_out, due(silu_out))
                act.wait_ge(c_clear, due(c_clear))
                act.activation(csr4[:, :, 0:2], csil[:, :, :], ACT.Copy).then_inc(c_hi, 1)
                with due.loop("ada", ADA_FIRST // 2):
                    for k in range(2):
                        ada_a(k)
                    slots.misc()
                    slots.misc()
                ffn(0)

                norm(1)
                act.wait_ge(n_ready, due.now(n_ready))
                act.dma_start(n_keep[0], nh[:, :, :].bitcast(F32)).then_inc(spilled, 16)
                act.dma_start(n_keep[1], nl[:, :, :].bitcast(F32)).then_inc(spilled, 16)
                act.dma_start(ft[:, :], feats).then_inc(feat_in, 16)
                for c in range(2):
                    t = tile()
                    split_hi(halves(fnh[:, c, :]), tile2(t))
                round_panel()
                for c in range(6):
                    t = tile()
                    if c >= 2:
                        act.wait_ge(conv_used, due(conv_used))
                    for bank, c0, c1, t0, t1, g in SEGMENTS:
                        ins = act.activation(upad[:, c % 2, t0 + 1 + 2 * g:t1 + 1 + 2 * g], tps[:, t.s, bank, c0:c1], ACT.Copy)
                        ins.then_inc(t.free if g else conv_in, 1)
                    if c % 2:
                        round_panel()
                due(conv_used, 2)
                for c in range(2):
                    t = tile()
                    act.activation(halves(qa[:, c, :]), tile2(t), ACT.Copy).then_inc(t.free, 1)
                round_panel()
                t = tile()
                act.activation(halves(kvr[:, :]), tile2(t), ACT.Copy).then_inc(t.free, 1)
                t = tile()
                act.activation(halves(krr[FHID:P, :]), tps[FHID:P, t.s, :, 0:TH], ACT.Copy).then_inc(t.free, 1)
                round_panel()
                act.wait_ge(t.free, t.free_at)
                act.dma_start(krope_out[bass.ds(l, 1)].rearrange("a p n -> (a p) n"), krr[FHID:FHID + ROPE, TL:T]).then_inc(stored, 16)

                act.wait_ge(spilled, due(spilled, 32))

                def mlp(n):
                    slots.misc()
                    act.wait_ge(sin_in, due(sin_in))
                    act.activation((mz if n == 0 else krr)[0:FHID, :], mr[0:FHID, :], ACT.Sin).then_inc(sin_out, 1)

                def channels(_):
                    for t in range(5):
                        m = misc()
                        split_hi(fah[:, t, :], mps[:, m.s, 0, :])

                def tokens(_):
                    for c in range(2):
                        t = tile()
                        split_hi(xh[:, 6 + c, :], flat(tps, t.s)[:, 0:T])
                    round_panel()
                    round_panel()

                def taps(o):
                    for t in range(5):
                        slots.misc()

                def norms(o):
                    for t in range(5):
                        act.wait_ge(taps_ready, due(taps_ready))
                        if t in (2, 3):
                            act.wait_ge(abs_used, due(abs_used))
                        if t == 4:
                            act.wait_ge(abs_used, due(abs_used))
                            m = misc()
                            split_hi(inv[:, 0, :], mps[:, m.s, 0, HYW:2 * HYW], bwd_sum)
                        act.activation((ab if t % 2 == 0 else yf)[:, :], hd[:, t, :], ACT.Abs).then_inc(abs_ready, 1)
                    m = misc()
                    split_hi(inv[:, 1, :], mps[:, m.s, 0, HYW:2 * HYW], bwd_sum)

                def turn(o):
                    for t in range(5):
                        m = misc()
                        split_hi(tmh[:, t, HYW:2 * HYW], mps[:, m.s, 0, 0:HYW])

                def forward(o):
                    for f in range(5):
                        m = misc()
                        act.wait_ge(parts_used, due(parts_used))
                        act.activation(reb[:, :], mps[:, m.s, 0, :], ACT.Copy)
                        act.activation(hbb[:, :], mps[:, m.s, 1, HYW:2 * HYW], ACT.Copy).then_inc(parts_out, 1)
                    round_panel()
                    round_panel()

                def inverse(o):
                    slots.tile()
                    tile()
                    round_panel()
                    round_panel()

                steps = dict(mlp=mlp, channels=channels, tokens=tokens, taps=taps, norms=norms, turn=turn,
                             forward=forward, inverse=inverse)
                for what, o in MIX_ORDER:
                    if what in steps:
                        steps[what](o)
                for c in range(2):
                    act.wait_ge(z_new, due(z_new))
                    split_hi(xh[:, c, :], hyx[:, 4 + c, :])

                for k in range(2):
                    ins = act.activation(asq[:, k, :], qa[:, k, :], ACT.Square)
                ins.then_inc(asq_ready, 1)
                act.activation(asq[:, 2, :], kvr[:, :], ACT.Square).then_inc(asq_ready, 1)
                m = misc()
                root(ars[:, 0, :], 2 * P, m, rms_out)
                m = misc()
                root(ars[:, 1, :], P, m, rms_out)
                act.wait_ge(low_ready, due(low_ready))
                split_hi(ckh[:, 0:T], art[:, 2, :], low_hi)
                split_hi(ckh[:, T:KEYS], prm("ckv"), low_hi)
                act.dma_start(ckv_out[bass.ds(l, 1)].rearrange("a p n -> (a p) n"), art[:, 2, TL:T]).then_inc(stored, 16)
                act.wait_ge(krope_ready, due(krope_ready))
                R = slice(NOPE, QK)
                for k_ in khs:
                    split_hi(k_[R, 0:TL], kro[R, 0:TL], low_hi)
                    split_hi(k_[R, TL:T], krr[R, TL:T], low_hi)
                    split_hi(k_[R, T:KEYS], prm("krope")[R, :], low_hi)
                act.wait_ge(low_ready, due(low_ready, 3))
                for k in range(2):
                    split_hi(qnh[:, k, :], art[:, k, :], low_hi)
                act.wait_ge(stored, due(stored, 32))
                with due.loop("heads", 2) as i:
                    for what, n in HEAD_ORDER:
                        h_, qt = n // 5, n % 5
                        if what == "Q":
                            t = tile()
                            act.wait_ge(q_split, due(q_split))
                            act.activation(halves(qf[0:NOPE, :]), tps[0:NOPE, t.s, :, 0:TH], ACT.Copy)
                            act.activation(qf[R, TL:T], tps[R, t.s, 1, TL - TH:TH], ACT.Copy).then_inc(q_copy, 1)
                        elif what == "K":
                            m = misc()
                            split_hi(halves(khs[n % 2][0:NOPE, :]), mps[0:NOPE, m.s, :, 0:KEYS // 2])
                            if n % 2:
                                round_panel()
                        elif what == "QS":
                            act.wait_ge(q_roped, due(q_roped))
                            split_hi(qh[0:QK, n % 2, :], qf[0:QK, :])
                        elif what == "V":
                            m = misc()
                            split_hi(halves(vh[:, :]), mps[:, m.s, :, 0:KEYS // 2])
                        elif what == "S":
                            m = misc()
                            w, c = (TL + PAST if qt < 4 else TC), n % 3
                            act.wait_ge(prob_in, due(prob_in))
                            act.activation(probs(n)[:, 0:w], flat(mps, m.s)[:, 0:w], ACT.Exp, bias=stat[:, 3 + c:4 + c],
                                           scale=QK ** -0.5, accum_out=stat[:, 6 + c:7 + c]).then_inc(m.free, 1)
                        elif what == "T":
                            t = tile()
                            if qt < 4:
                                split_hi(pth[:, 0:5 * TL].rearrange("p (a t) -> p a t", a=5)[:, :, qt * P:(qt + 1) * P],
                                         flat(tps, t.s)[:, 0:T].rearrange("p (a t) -> p a t", a=5))
                            else:
                                split_hi(pth[:, 5 * TL:], tps[:, t.s, 0, 0:TC])
                        elif what == "P":
                            t = tile()
                            rows = slice((n % 2) * VD, (n % 2 + 1) * VD)
                            split_hi(xh[rows, bass.ds(i * 2 + (2 + n // 2), 1), :].rearrange("p a t -> p (a t)"), flat(tps, t.s)[rows, 0:T])
                        elif what == "A":
                            ada_a(n % 2)
                        elif what == "B":
                            slots.misc()
                act.wait_ge(t.free, t.free_at)
                act.dma_start(nh[:, :, :].bitcast(F32), n_keep[0]).then_inc(back, 16)
                act.dma_start(nl[:, :, :].bitcast(F32), n_keep[1]).then_inc(back, 16)

                with due.loop("gate", KT):
                    for b in range(3):
                        t = tile()
                        act.activation(halves(sgm[:, b, :]), tile2(t), ACT.Sigmoid).then_inc(t.free, 1)
                        if b == 1:
                            round_panel()
                    slots.tile()
                    slots.tile()
                    tile()
                    round_panel()
                act.wait_ge(y_done, due(y_done))
                for k in range(KT):
                    split_hi(nh[:, k, :], yc[:, k, :], hi_out)
                due(n_ready, KT)
                into_h("out", True)
                ffn(1)
            root(rs[:, :], D, misc(), rms_out)

        @block.vector
        def _(dve):
            due = Due("dve", dve, per_pass, {})
            slots = Slots(due)

            def own(ins):
                ins.then_inc(dve_own, 1)
                dve.wait_ge(dve_own, due(dve_own))

            def seen(slot):
                dve.wait_ge(slot.done, slot.done_at)
                return slot

            def tile():
                return seen(slots.tile())

            def misc():
                return seen(slots.misc())

            def tile2(t):
                return tps[:, t.s, :, 0:TH]

            def lo_part(out, src, hi, ready, after=None):
                after = op_hi if after is None else after
                dve.wait_ge(after, due(after))
                dve.tensor_tensor(out, src, hi.bitcast(F32), ALU.subtract).then_inc(ready, 1)

            def add_square():
                dve.wait_ge(sq_out, due(sq_out))
                dve.tensor_tensor(acc[:, :], acc[:, :], sq[:, :], ALU.add).then_inc(sq_used, 1)
                dve.wait_ge(sq_used, due(sq_used))

            def inv_rms():
                m = slots.misc()
                dve.wait_ge(rms_out, due(rms_out))
                dve.reciprocal(rr[:, :], rs[:, :]).then_inc(m.free, 1)
                dve.wait_ge(m.free, m.free_at)

            def norm(i):
                inv_rms()

                def scaled(k):
                    for g, (_, a, b) in enumerate(GROUPS):
                        ins = dve.scalar_tensor_tensor(out=tn[:, k % 2, a:b], in0=h[:, k, a:b], scalar=gm[:, 8 * i + k, g:g + 1],
                                                       in1=rr[:, a:b], op0=ALU.mult, op1=ALU.mult)
                    ins.then_inc(t_ready, 1)

                scaled(0)
                for k in range(KT):
                    if k + 1 < KT:
                        if k:
                            dve.wait_ge(n_ready, due(n_ready))
                        scaled(k + 1)
                    dve.wait_ge(t_ready, due(t_ready))
                    dve.wait_ge(hi_out, due(hi_out))
                    for g, (_, a, b) in enumerate(GROUPS):
                        ins = dve.scalar_tensor_tensor(out=nl[:, k, a:b], in0=tn[:, k % 2, a:b], scalar=ada[:, 24 * i + k, g:g + 1],
                                                       in1=nh[:, k, a:b].bitcast(F32), op0=ALU.add, op1=ALU.subtract)
                    ins.then_inc(n_ready, 1)
                due(n_ready, 2)

            def modulation(i):
                sc = slice(24 * i + 8, 24 * i + 16)
                ng = prm("norm_g").rearrange("p (a b) -> p a b", b=2)
                own(dve.scalar_tensor_tensor(out=gm[:, 8 * i:8 * i + 8, :], in0=ada[:, sc, :], scalar=1.0,
                                             in1=ng[:, 8 * i:8 * i + 8, :], op0=ALU.add, op1=ALU.mult))

            def half_gate(i):
                gs = slice(24 * i + 16, 24 * i + 24)
                own(dve.tensor_scalar(ada[:, gs, :], ada[:, gs, :], 0.5, None, ALU.mult))

            def ada_b(n):
                m = misc()
                at_ = bass.ds(n * 2, 2)
                bada = prm("b_ada").rearrange("p (a b) -> p a b", b=2)
                dve.tensor_tensor(ada[:, at_, :], mps[:, m.s, 0, 0:4].rearrange("p (a b) -> p a b", b=2),
                                  bada[:, at_, :], ALU.add).then_inc(m.free, 1)
                return m

            def into_h(label, section, last):
                if last:
                    own(dve.memset(acc[:, :], 0.0))
                with due.loop(label, 2) as i:
                    for k in range(4):
                        m, t = i * 4 + k, tile()
                        for bank, c0, c1, t0, t1, g in SEGMENTS:
                            hs = h[:, bass.ds(m, 1), t0:t1].rearrange("p a t -> p (a t)")
                            gate = ada[:, bass.ds(m + 8 * section, 1), g:g + 1].rearrange("p a t -> p (a t)")
                            ins = dve.scalar_tensor_tensor(out=hs, in0=tps[:, t.s, bank, c0:c1], scalar=gate, in1=hs,
                                                           op0=ALU.mult, op1=ALU.add)
                        ins.then_inc(t.free, 1)
                        if last:
                            add_square()
                dve.wait_ge(t.free, t.free_at)
                if last:
                    dve.sem_inc(sum_ready, 1)

            def ffn(f):
                norm(2 * f)
                for c, n in enumerate(CHUNKS):
                    with_ada = f == 0 and c < 2
                    with due.loop(f"up{f}{c}", n // 2) as i:
                        for k in range(2):
                            if with_ada:
                                slots.misc()
                            tg = slots.tile()
                            t = tile()
                            dve.wait_ge(tg.free, tg.free_at)
                            dve.tensor_tensor(halves(hf[:, k, :]), halves(sg[:, k, :]), tile2(t), ALU.mult).then_inc(t.free, 1)
                            dve.wait_ge(t.free, t.free_at)
                            kk = bass.ds(i * 2 + k, 1)
                            lo_part(xl[:, kk, :].rearrange("p a t -> p (a t)"), hf[:, k, :],
                                    xh[:, kk, :].rearrange("p a t -> p (a t)"), hid_ready, hid_hi)
                            if with_ada:
                                m = ada_b(i * 2 + (ADA_FIRST + c * ADA_UP // 2 + k))
                    if with_ada:
                        dve.wait_ge(m.free, m.free_at)
                        (half_gate, modulation)[c](c)
                    into_h(f"down{f}{c}", 2 if f == 0 else 8, c == 2)

            dve.sem_inc(lo_ready, 2)
            for f in tile_free + misc_free + [layer_end, parts_used, q_split]:
                dve.sem_inc(f, 1)
            dve.wait_ge(small_hi, due(small_hi))
            dve.tensor_tensor(sml[:, :], smraw[:, :], smh[:, :].bitcast(F32), ALU.subtract).then_inc(small_split, 1)
            dve.wait_ge(x_in, due(x_in, 16))
            dve.wait_ge(consts_in, due(consts_in, 16))
            own(dve.memset(acc[:, :], 0.0))
            for k in range(KT):
                add_square()
            dve.sem_inc(sum_ready, 1)
            with due.loop("layer", DEPTH):
                dve.memset(csr[:, :].bitcast(F32), 0.0).then_inc(c_clear, 1)
                dve.wait_ge(c_hi, due(c_hi))
                dve.tensor_tensor(csr4[:, :, 2:4], csil[:, :, :], csr4[:, :, 0:2].bitcast(F32), ALU.subtract).then_inc(c_split, 1)
                dve.wait_ge(par_in, due(par_in, 16))
                with due.loop("ada", ADA_FIRST // 2) as i:
                    slots.misc()
                    slots.misc()
                    for k in range(2):
                        m = ada_b(i * 2 + k)
                dve.wait_ge(m.free, m.free_at)
                modulation(0)
                ffn(0)

                norm(1)
                for c in range(2):
                    t = tile()
                    lo_part(halves(fnl[:, c, :]), tile2(t), halves(fnh[:, c, :]), t.free)
                for c in (0, UP - 1, TL + 1, TL + 2):
                    ins = dve.memset(upad[:, :, c:c + 1], 0.0)
                own(ins)
                for c in range(6):
                    t = slots.tile()
                    dve.wait_ge(conv_in, due(conv_in, 2))
                    dve.wait_ge(t.free, t.free_at)
                    w = prm("conv", 4 * c, 4 * c + 4)
                    for tap, shift in ((1, 1), (0, 0), (2, 2)):
                        for g, a, b in GROUPS:
                            gg = 0 if a == 0 else 1
                            src = upad[:, c % 2, a + shift + 2 * gg:b + shift + 2 * gg]
                            if tap == 1:
                                ins = dve.tensor_scalar(hyx[:, c, a:b], src, w[:, 1:2], w[:, 3:4], ALU.mult, ALU.add)
                            else:
                                ins = dve.scalar_tensor_tensor(out=hyx[:, c, a:b], in0=src, scalar=w[:, tap:tap + 1],
                                                               in1=hyx[:, c, a:b], op0=ALU.mult, op1=ALU.add)
                        if tap != 2:
                            own(ins)
                    ins.then_inc(conv_used, 1)
                    dve.wait_ge(conv_used, due(conv_used))
                for _ in range(4):
                    t = slots.tile()
                dve.sem_inc(v_ready, 1)
                dve.sem_inc(v_ready, 1)

                dve.wait_ge(spilled, due(spilled, 32))
                decay = cst("decay")

                def mlp(n):
                    m, bias = misc(), prm(("b1", "b2")[n])
                    magic, c1 = 1.5 * 2 ** 23, 6.28125
                    F = slice(0, FHID)
                    dve.tensor_scalar(halves(mz2[F, :]), mps[F, m.s, :, 0:TH], bias[F, :], None, ALU.add).then_inc(m.free, 1)
                    dve.wait_ge(m.free, m.free_at)
                    own(dve.tensor_scalar(mk[F, :], mz2[F, :], 1 / (2 * math.pi), magic, ALU.mult, ALU.add))
                    own(dve.tensor_scalar(mk[F, :], mk[F, :], magic, None, ALU.subtract))
                    own(dve.scalar_tensor_tensor(out=mr[F, :], in0=mk[F, :], scalar=-c1, in1=mz2[F, :], op0=ALU.mult, op1=ALU.add))
                    own(dve.scalar_tensor_tensor(out=mr[F, :], in0=mk[F, :], scalar=-(2 * math.pi - c1), in1=mr[F, :],
                                                 op0=ALU.mult, op1=ALU.add))
                    dve.tensor_scalar(mr[F, :], mr[F, :], 3.1415925, -3.1415925, ALU.min, ALU.max).then_inc(sin_in, 1)

                def channels(_):
                    for t in range(5):
                        m = misc()
                        lo_part(fal[:, t, :], mps[:, m.s, 0, :], fah[:, t, :], m.free)

                def tokens(_):
                    for c in range(2):
                        t = tile()
                        lo_part(xl[:, 6 + c, :], flat(tps, t.s)[:, 0:T], xh[:, 6 + c, :], t.free)

                def taps(o):
                    for t in range(5):
                        m = misc()
                        dc = decay[:, t * HYW:(t + 1) * HYW]
                        dve.tensor_tensor(hd[:, t, 0:HYW], mps[:, m.s, 0, 0:HYW], dc, ALU.mult)
                        dve.tensor_tensor(hd[:, t, HYW:], mps[:, m.s, 0, HYW:], dc, ALU.mult).then_inc(m.free, 1)
                        dve.wait_ge(m.free, m.free_at)
                        if t in (0, 4):
                            own(dve.memset(hd[0:1, t, HYW:], 0.0))
                        dve.sem_inc(taps_ready, 1)

                def norms(o):
                    for g in range(2):
                        m = misc()
                        dve.wait_ge(bwd_sum, due(bwd_sum))
                        dve.tensor_tensor(inv[:, g, :], mps[:, m.s, 0, 0:HYW], inv[:, g, :], ALU.add).then_inc(m.free, 1)
                        dve.wait_ge(m.free, m.free_at)
                        own(dve.tensor_scalar(inv[:, g, :], inv[:, g, :], EPS, None, ALU.add))
                        own(dve.reciprocal(inv[:, g, :], inv[:, g, :]))

                def combine(o):
                    for t in range(5):
                        dve.tensor_tensor(pp[:, 0, :], hd[:, t, 0:HYW], hd[:, t, HYW:], ALU.add)
                        own(dve.tensor_tensor(pp[:, 1, :], hd[:, t, 0:HYW], hd[:, t, HYW:], ALU.subtract))
                        iv = inv[:, t // 4, :]
                        dve.tensor_tensor(pp[:, 0, :], pp[:, 0, :], iv, ALU.mult)
                        own(dve.tensor_tensor(pp[:, 1, :], pp[:, 1, :], iv, ALU.mult))
                        hi2 = tmh[:, t, :].rearrange("p (a c) -> p a c", a=3)[:, 0:3:2, :]
                        lo2 = tml[:, t, :].rearrange("p (a c) -> p a c", a=3)[:, 0:3:2, :]
                        own(dve.tensor_copy(hi2, pp[:, :, :]))
                        own(dve.tensor_tensor(lo2, pp[:, :, :], hi2.bitcast(F32), ALU.subtract))
                    dve.sem_inc(filter_ready, 1)

                def turn(o):
                    for t in range(5):
                        m = misc()
                        lo_part(tml[:, t, HYW:2 * HYW], mps[:, m.s, 0, 0:HYW], tmh[:, t, HYW:2 * HYW], m.free)

                def forward(o):
                    for f in range(5):
                        m = misc()
                        dve.wait_ge(parts_out, due(parts_out))
                        ha, ur, us = reb[:, 0:HYW], reb[:, HYW:], mps[:, m.s, 1, 0:HYW]
                        dve.tensor_tensor(pp[:, 0, :], ur, ha, ALU.mult)
                        own(dve.tensor_tensor(pp[:, 1, :], us, hbb[:, :], ALU.mult))
                        own(dve.tensor_tensor(yf[:, 0:HYW], pp[:, 0, :], pp[:, 1, :], ALU.subtract))
                        dve.tensor_tensor(pp[:, 0, :], ur, hbb[:, :], ALU.mult)
                        dve.tensor_tensor(pp[:, 1, :], us, ha, ALU.mult).then_inc(m.free, 1)
                        dve.wait_ge(m.free, m.free_at)
                        dve.tensor_tensor(yf[:, HYW:], pp[:, 0, :], pp[:, 1, :], ALU.add).then_inc(parts_used, 1)
                        dve.wait_ge(parts_used, due(parts_used) + 1)
                        ysl = slice(2 * f, 2 * f + 2)
                        own(dve.tensor_copy(yh[:, ysl, :].rearrange("p a c -> p (a c)"), yf[:, :]))
                        dve.tensor_tensor(yl[:, ysl, :].rearrange("p a c -> p (a c)"), yf[:, :],
                                          yh[:, ysl, :].rearrange("p a c -> p (a c)").bitcast(F32), ALU.subtract)\
                            .then_inc(spec_ready, 1)

                def inverse(o):
                    for c in range(2):
                        t = tile()
                        v = hyx[:, 4 + c, :]
                        dve.scalar_tensor_tensor(out=v, in0=v, scalar=prm("skip", 2 * o + c, 2 * o + c + 1),
                                                 in1=flat(tps, t.s)[:, 0:T], op0=ALU.mult, op1=ALU.add).then_inc(t.free, 1)
                        dve.wait_ge(t.free, t.free_at)
                        dve.tensor_tensor(v, v, hyx[:, 2 * o + c, :], ALU.mult).then_inc(v_ready if o == 0 else z_new, 1)
                    if o == 0:
                        dve.wait_ge(v_ready, due(v_ready, 4))

                steps = dict(mlp=mlp, channels=channels, tokens=tokens, taps=taps, norms=norms, combine=combine,
                             turn=turn, forward=forward, inverse=inverse)
                for what, o in MIX_ORDER:
                    steps[what](o)
                for c in range(2):
                    dve.wait_ge(z_new, due(z_new))
                    lo_part(xl[:, c, :], hyx[:, 4 + c, :], xh[:, c, :], z_split)

                for k in range(2):
                    m = slots.misc()
                    dve.wait_ge(rms_out, due(rms_out))
                    dve.reciprocal(ars[:, k, :], ars[:, k, :]).then_inc(m.free, 1)
                    dve.wait_ge(m.free, m.free_at)
                for k, (src, g) in ((2, (kvr[:, :], prm("kv_g"))), (0, (qa[:, 0, :], prm("q_g", 0, 1))),
                                    (1, (qa[:, 1, :], prm("q_g", 1, 2)))):
                    own(dve.tensor_tensor(art[:, k, :], src, ars[:, 1 if k == 2 else 0, :], ALU.mult))
                    dve.tensor_scalar(art[:, k, :], art[:, k, :], g, None, ALU.mult).then_inc(low_ready, 1)
                    dve.wait_ge(low_ready, due(low_ready))
                R, R2 = slice(NOPE, QK), slice(QK, P)
                rope = cst("rope")
                dve.tensor_tensor(krt[R, :], krr[R2, 0:TL], rope[R2, :], ALU.mult)
                own(dve.tensor_tensor(kro[R, 0:TL], krr[R, 0:TL], rope[R, :], ALU.mult))
                dve.tensor_tensor(kro[R, 0:TL], kro[R, 0:TL], krt[R, :], ALU.add).then_inc(krope_ready, 1)
                dve.wait_ge(krope_ready, due(krope_ready))
                dve.wait_ge(low_hi, due(low_hi, 8))
                for k_h, k_l in zip(khs, kls):
                    for a, b, src in ((0, TL, kro[R, 0:TL]), (TL, T, krr[R, TL:T]), (T, KEYS, prm("krope")[R, :])):
                        dve.tensor_tensor(k_l[R, a:b], src, k_h[R, a:b].bitcast(F32), ALU.subtract)
                dve.tensor_tensor(ckl[:, 0:T], art[:, 2, :], ckh[:, 0:T].bitcast(F32), ALU.subtract).then_inc(low_split, 1)
                dve.tensor_tensor(ckl[:, T:KEYS], prm("ckv"), ckh[:, T:KEYS].bitcast(F32), ALU.subtract).then_inc(low_split, 1)
                dve.wait_ge(low_split, due(low_split, 2))
                dve.sem_inc(low_ready, 1)
                due(low_ready)
                due(low_split, 2)
                dve.wait_ge(stored, due(stored, 32))
                for k in range(2):
                    dve.wait_ge(low_hi, due(low_hi))
                    dve.tensor_tensor(qnl[:, k, :], art[:, k, :], qnh[:, k, :].bitcast(F32), ALU.subtract).then_inc(low_split, 1)
                with due.loop("heads", 2) as i:
                    scored = {}
                    for what, n in HEAD_ORDER:
                        h_, qt, c = n // 5, n % 5, n % 3
                        if what == "Q":
                            t = tile()
                            dve.wait_ge(q_copy, due(q_copy))
                            for bank, c0, c1, t0, t1, g in SEGMENTS[:2]:
                                dve.tensor_tensor(krt[R, t0:t1], tps[R2, t.s, bank, c0:c1], rope[R2, t0:t1], ALU.mult)
                            for bank, c0, c1, t0, t1, g in SEGMENTS[:2]:
                                ins = dve.tensor_tensor(qf[R, t0:t1], tps[R, t.s, bank, c0:c1], rope[R, t0:t1], ALU.mult)
                            ins.then_inc(t.free, 1)
                            dve.wait_ge(t.free, t.free_at)
                            dve.tensor_tensor(qf[R, 0:TL], qf[R, 0:TL], krt[R, :], ALU.add).then_inc(q_roped, 1)
                            dve.wait_ge(q_roped, due(q_roped))
                        elif what == "K":
                            m = misc()
                            lo_part(halves(kls[n % 2][0:NOPE, :]), mps[0:NOPE, m.s, :, 0:KEYS // 2],
                                    halves(khs[n % 2][0:NOPE, :]), m.free)
                        elif what == "QS":
                            lo_part(ql[0:QK, n % 2, :], qf[0:QK, :], qh[0:QK, n % 2, :], q_split)
                        elif what == "V":
                            m = misc()
                            lo_part(halves(vl[:, :]), mps[:, m.s, :, 0:KEYS // 2], halves(vh[:, :]), m.free)
                        elif what == "S":
                            scored[n] = m = misc()
                            w = TL + PAST if qt < 4 else TC
                            own(dve.tensor_reduce(stat[:, c:c + 1], flat(mps, m.s)[:, 0:w], AX.X, ALU.max))
                            dve.tensor_scalar(stat[:, 3 + c:4 + c], stat[:, c:c + 1], -QK ** -0.5, None, ALU.mult)\
                                .then_inc(prob_in, 1)
                        elif what == "N":
                            m = scored[n]
                            w = TL + PAST if qt < 4 else TC
                            dve.wait_ge(m.free, m.free_at)
                            own(dve.reciprocal(stat[:, c:c + 1], stat[:, 6 + c:7 + c]))
                            p = probs(n)[:, 0:w]
                            dve.tensor_scalar(p, p, stat[:, c:c + 1], None, ALU.mult).then_inc(prob_ready, 1)
                        elif what == "T":
                            t = tile()
                            if qt < 4:
                                out, hi = [x_[:, 0:5 * TL].rearrange("p (a t) -> p a t", a=5)[:, :, qt * P:(qt + 1) * P]
                                           for x_ in (ptl, pth)]
                                lo_part(out, flat(tps, t.s)[:, 0:T].rearrange("p (a t) -> p a t", a=5), hi, t.free)
                            else:
                                lo_part(ptl[:, 5 * TL:], tps[:, t.s, 0, 0:TC], pth[:, 5 * TL:], t.free)
                        elif what == "P":
                            t = tile()
                            rows = slice((n % 2) * VD, (n % 2 + 1) * VD)
                            kk = bass.ds(i * 2 + (2 + n // 2), 1)
                            lo_part(xl[rows, kk, :].rearrange("p a t -> p (a t)"), flat(tps, t.s)[rows, 0:T],
                                    xh[rows, kk, :].rearrange("p a t -> p (a t)"), t.free)
                        elif what == "A":
                            slots.misc()
                        elif what == "B":
                            m_ada = ada_b(i * (ADA_HEADS // 2) + (ADA_FIRST + ADA_UP + n))
                dve.wait_ge(m_ada.free, m_ada.free_at)
                modulation(2)
                half_gate(2)

                with due.loop("gate", KT) as i:
                    gates = [slots.tile() for _ in range(3)]
                    y = yc[:, bass.ds(i, 1), :].rearrange("p a t -> p (a t)")
                    for b in range(3):
                        t = tile()
                        dve.wait_ge(gates[b].free, gates[b].free_at)
                        dve.tensor_tensor(halves(y if b == 0 else prod[:, :]), halves(sgm[:, b, :]), tile2(t), ALU.mult)\
                            .then_inc(t.free, 1)
                        dve.wait_ge(t.free, t.free_at)
                        if b:
                            own(dve.tensor_tensor(y, y, prod[:, :], ALU.add))
                dve.sem_inc(y_done, 1)
                for k in range(KT):
                    lo_part(nl[:, k, :], yc[:, k, :], nh[:, k, :], n_ready, hi_out)
                dve.wait_ge(n_ready, due(n_ready, KT))
                into_h("out", 5, True)
                ffn(1)
                dve.sem_inc(layer_end, 1)

            inv_rms()
            fg = cst("final_g")
            for k in range(KT):
                dve.scalar_tensor_tensor(out=h[:, k, :], in0=h[:, k, :], scalar=fg[:, k:k + 1], in1=rr[:, :],
                                         op0=ALU.mult, op1=ALU.mult).then_inc(y_ready, 1)


def transform_tables():
    def odd(n, scale=1.0):
        a = np.pi * np.outer(np.arange(n), np.arange(n) + 0.5) / n
        return np.cos(a) * scale, np.sin(a) * scale

    def whole(n, scale):
        a = 2 * np.pi * (np.outer(np.arange(n), np.arange(n)) % n) / n
        return np.cos(a) * scale, np.sin(a) * scale

    def panel(m):
        return m.reshape(4, P, 512).transpose(1, 0, 2).reshape(P, PANEL)

    c, s = odd(TL)
    fc, fs = whole(TL, (TL * 64) ** -0.5)
    tables = np.stack([panel(m) for m in (c, s, c.T / TL, s.T / TL, fc, -fs)])
    cc, cs = odd(TC)
    c64, s64 = whole(64, 1.0)
    z = np.zeros((64, 64))
    bd = [np.block([[m, z], [z, m]]) for m in (c64, s64)]
    gc, gs = whole(TC, (TC * 64) ** -0.5)
    small = np.concatenate([cc, cs, cc.T / TC, cs.T / TC] + bd + [gc, -gs], axis=1)
    return tables.astype(np.float32), small.astype(np.float32)


def filter_features(n):
    t = np.arange(n, dtype=np.float32)
    tn = t / np.float32(n - 1)
    w = np.float32(2.0 * math.pi) * t / np.float32(n)
    bands = np.linspace(1e-4, NB - 1, NB, dtype=np.float32)
    a = (w[:, None] * bands[None, :]).astype(np.float32)
    f = np.concatenate([tn[:, None], np.cos(a), -np.sin(a)], axis=1)
    deltas = np.linspace(math.log(1e-2) / 1.5, math.log(1e-2) / 0.3, HYW, dtype=np.float32)
    return f.astype(np.float32), np.exp(-tn[:, None] * np.abs(deltas)[None, :]).astype(np.float32)


def constants():
    cst = np.zeros((P, NCST), np.float32)

    def put(name, a):
        cst[:a.shape[0], CST[name][0]:CST[name][0] + a.shape[1]] = a

    (f1, d1), (f2, d2) = filter_features(TL), filter_features(TC)
    put("decay", np.concatenate([d1[t * P:(t + 1) * P] for t in range(4)] + [d2], axis=1))
    n_freq = ROPE // 4
    inv = (10000.0 ** (-np.arange(n_freq, dtype=np.float32) / n_freq)).astype(np.float32)
    tok = np.arange(TL)
    ang = [(tok // GRID_W)[:, None] * inv[None], (tok % GRID_W)[:, None] * inv[None]]
    cos = np.concatenate([np.cos(a) for a in ang for _ in range(2)], axis=1)
    sin = np.concatenate([sg * np.sin(a) for a in ang for sg in (-1, 1)], axis=1)
    rope = np.zeros((P, TL), np.float32)
    rope[NOPE:QK], rope[QK:] = cos.T, sin.T
    put("rope", rope)
    put("ident", np.eye(P, dtype=np.float32))
    put("ones", np.ones((P, P), np.float32))
    put("sel", np.array([[1, 0], [0, 1], [1, 0], [0, 1]], np.float32))
    put("eps", np.full((P, 1), EPS, np.float32))
    feats = np.zeros((P, T), np.float32)
    feats[:17, :TL], feats[:17, TL:] = f1.T, f2.T
    return cst, feats


def blocks(w):
    k, m = w.shape
    return w.reshape(k // P, P, m // P, P).transpose(0, 2, 1, 3)


def as_panel(bs):
    return np.concatenate(bs, axis=1)


def feature_major(a):
    return np.ascontiguousarray(a.T.reshape(-1, P, a.shape[0]).transpose(1, 0, 2))


def lay_out(inp):
    f = np.float32
    swap = np.concatenate([np.arange(8, 16), np.arange(8), np.arange(24, 32), np.arange(16, 24)])
    w_ada = inp["w_ada"].reshape(DEPTH, KT, P, 36, 256).transpose(0, 3, 2, 1, 4).reshape(DEPTH * 36, P, PANEL)
    up = inp["w_ffn_up"].reshape(DEPTH, 2, KT, P, 2, HT, P)
    w_up = up.transpose(0, 1, 5, 3, 4, 2, 6).reshape(DEPTH * 2 * HT, P, PANEL)
    down, at = [], 0
    for n in CHUNKS:
        d = inp["w_ffn_down"][:, :, at * P:(at + n) * P].reshape(DEPTH, 2, n, P, 4, 2, P)
        down.append(d.transpose(0, 1, 4, 3, 5, 2, 6).reshape(DEPTH, 2, 4, P, 2 * n * P))
        at += n
    w_down8 = np.stack(down[:2], axis=2).reshape(DEPTH * 2 * 8, P, PANEL)
    w_down6 = down[2].reshape(DEPTH * 2 * 4, P, 2 * 6 * P)
    w_mix, w_qkv, w_gate, w_out, par = [], [], [], [], []
    for l in range(DEPTH):
        w = inp["w_in"][l]
        zero = np.zeros((D, NOPE), f)
        kr = w[:, 1152:1184]
        cols = [w[:, 1184:1440], w[:, 0:768], w[:, 768:1152], np.concatenate([zero, kr, kr[:, swap]], axis=1)]
        b = blocks(np.concatenate(cols, axis=1))
        w_mix += [as_panel([b[k, m] for m in (2 * i, 2 * i + 1) for k in range(KT)]) for i in range(6)]
        qb, kvb = inp["w_qb"][l].reshape(2, P, HEADS, QK), inp["w_kvb"][l].reshape(P, HEADS, NOPE + VD)
        for i in range(4):
            hs = (2 * i, 2 * i + 1)
            bs = [np.concatenate([qb[k, :, hh], qb[k, :, hh, NOPE:][:, swap]], axis=1) for hh in hs for k in range(2)]
            bs += [np.concatenate([kvb[:, hh, :NOPE], np.zeros((P, P - NOPE), f)], axis=1) for hh in hs]
            bs += [np.concatenate([kvb[:, hh, NOPE:] for hh in hs], axis=1)]
            w_qkv.append(as_panel(bs))
        g = blocks(w[:, 1440:])
        ys = [blocks(inp[n][l]) for n in ("w_hy_out", "w_mla_o", "w_fnet")]
        for m in range(KT):
            w_gate.append(as_panel([g[k, b_ * KT + m] for b_ in range(2) for k in range(KT)]))
            w_gate.append(as_panel([g[k, 2 * KT + m] for k in range(KT)] + [y[k, m] for y in ys for k in range(y.shape[0])]))
        wo = blocks(inp["w_out"][l])
        w_out += [as_panel([wo[k, m] for m in (2 * i, 2 * i + 1) for k in range(KT)]) for i in range(4)]
        p = np.zeros((P, NPAR), f)

        def put(name, a, row=0):
            p[row:row + a.shape[0], PAR[name][0]:PAR[name][0] + a.shape[1]] = a

        put("b_ada", np.repeat(inp["b_ada"][l].reshape(72, P).T, 2, axis=1))
        put("norm_g", np.repeat(inp["norm_g"][l].reshape(24, P).T, 2, axis=1))
        cw = np.concatenate([inp["hy_conv_w"][l], inp["hy_conv_b"][l][None]], axis=0)
        put("conv", cw.reshape(4, 6, P).transpose(2, 1, 0).reshape(P, 24))
        put("skip", inp["hy_skip"][l].reshape(4, P).T)
        put("q_g", inp["q_norm_g"][l].reshape(2, P).T)
        put("kv_g", inp["kv_norm_g"][l].reshape(1, P).T)
        put("b1", inp["hy_filt_b1"][l][:, None])
        put("b2", inp["hy_filt_b2"][l][:, None])
        put("w1", inp["hy_filt_w1"][l])
        put("w2", inp["hy_filt_w2"][l])
        put("ckv", inp["cache_ckv"][0, l].T)
        put("krope", inp["cache_krope"][0, l].T, NOPE)
        w3 = inp["hy_filt_w3"][l].reshape(FHID, 2, 2, HYW)
        put("w3", w3.transpose(0, 2, 1, 3).reshape(FHID, 4 * HYW))
        par.append(p)
    x = np.concatenate([inp["x_sample"][0], inp["x_prompt"][0]], axis=0)
    cv = np.stack([inp["c"][0], inp["c_ctx"]], axis=0)
    tables, small = transform_tables()
    cst, feats = constants()
    for k in range(KT):
        cst[:, CST["final_g"][0] + k] = inp["final_g"][k * P:(k + 1) * P]
    out = dict(x=feature_major(x), w_ada=w_ada, w_up=w_up, w_down8=w_down8, w_down6=w_down6, w_mix=np.stack(w_mix),
               w_qkv=np.stack(w_qkv), w_gate=np.stack(w_gate), w_out=np.stack(w_out), tables=tables, small=small, cst=cst,
               cvec=feature_major(cv), feats=feats, par=np.stack(par))
    return {k: np.ascontiguousarray(v, dtype=f) for k, v in out.items()}


OUTS = [("y", (P, KT, T)), ("ckv", (DEPTH, P, TC)), ("krope", (DEPTH, ROPE, TC))]


def build(nc, arrays, per_pass):
    a = {n: nc.dram_tensor(f"in_{n}", v.shape, F32, kind="ExternalInput").ap() for n, v in arrays.items()}
    o = {n: nc.dram_tensor(f"out_{n}", s, F32, kind="ExternalOutput").ap() for n, s in OUTS}
    program(nc, per_pass, a["x"], a["w_ada"], a["w_up"], (a["w_down8"], a["w_down6"]), a["w_mix"], a["w_qkv"], a["w_gate"],
            a["w_out"], a["tables"], a["small"], a["cst"], a["cvec"], a["feats"], a["par"], o["y"], o["ckv"], o["krope"])


def kernel(**inputs):
    import concourse.bacc as _bacc
    from concourse.bass_utils import run_bass_kernel_spmd as _run

    arrays = lay_out({k: np.asarray(v) for k, v in inputs.items()})
    per_pass = {}
    for _ in range(2):
        nc = _bacc.Bacc("TRN2", target_bir_lowering=False, num_devices=1)
        build(nc, arrays, per_pass)
    r = _run(nc, [{f"in_{n}": v for n, v in arrays.items()}], core_ids=[0]).results[0]
    y = r["out_y"].transpose(1, 0, 2).reshape(D, T).T
    ckv, krope = r["out_ckv"].transpose(0, 2, 1), r["out_krope"].transpose(0, 2, 1)
    return (np.ascontiguousarray(y[None, TL:]), np.ascontiguousarray(y[None, :TL]), np.ascontiguousarray(ckv[None]),
            np.ascontiguousarray(krope[None]))
```

```python
import math
from contextlib import ExitStack, contextmanager

import numpy as np
import concourse.bass as bass
import concourse.mybir as mybir

F32 = mybir.dt.float32
F32R = mybir.dt.float32r
ALU = mybir.AluOpType
ACT = mybir.ActivationFunctionType
AX = mybir.AxisListType

P = 128
D = 1024
KT = D // P
TL, TC = 512, 128
T = TL + TC
TH = T // 2
DEPTH = 2
PAST = 128
HYW = 256
NB = 8
FHID = 64
HEADS = 8
NOPE, ROPE, VD = 64, 32, 64
QK = NOPE + ROPE
KEYS = T + PAST
DFF = 2816
HT = DFF // P
CHUNKS = [8, 8, 6]
EPS = 1e-6
PANEL = 2048
GRID_W = 64

PAR = {}
_at = 0
for _n, _w in [("b_ada", 144), ("norm_g", 48), ("conv", 24), ("skip", 4), ("q_g", 2), ("kv_g", 1), ("b1", 1), ("b2", 1),
               ("w1", FHID), ("w2", 2 * FHID), ("ckv", PAST), ("w3", 4 * HYW)]:
    PAR[_n] = (_at, _at + _w)
    _at += _w
NPAR = _at
PAR["krope"] = PAR["w2"]
CST = {}
_at = 0
for _n, _w in [("decay", 5 * HYW), ("rope", TL), ("ident", P), ("ones", P), ("sel", 2), ("eps", 1), ("final_g", KT)]:
    CST[_n] = (_at, _at + _w)
    _at += _w
NCST = _at
SM_C, SM_S, SM_CI, SM_SI, SM_BD, SM_FC, SM_FS, NSM = 0, 128, 256, 384, 512, 768, 896, 1024

SEGMENTS = [(0, 0, TH, 0, TH, 0), (1, 0, TL - TH, TH, TL, 0), (1, TL - TH, TH, TL, T, 1)]
GROUPS = [(0, 0, TL), (1, TL, T)]
FFN_PANELS = sum(c + 4 for c in CHUNKS)


HEAD_ORDER = [(word.rstrip("0123456789"), int(word.lstrip("QKVSNTPAB"))) for word in """
    Q0 K0 QS0 V0 S0 S1 N0 S2 Q1 N1 T0 K1 QS1 S3 N2 T1 A0 S4 N3 B0 T2 A1 S5 N4 T3 B1 T4 S6 N5 N6 S7 P0 T5 Q2 K2 QS2
    S8 N7 T6 T7 S9 N8 S10 N9 T8 S11 N10 T9 S12 P1 V1 N11 T10 Q3 K3 QS3 S13 N12 T11 A2 S14 B2 N13 T12 A3 S15 N14 B3
    T13 S16 N15 T14 S17 N16 P2 T15 S18 N17 T16 S19 N18 T17 N19 T18 T19 P3
    """.split()]

ADA_FIRST, ADA_UP, ADA_HEADS, ADA_BACK = 8, 16, 8, 4
FIRST_A, FIRST_B = DEPTH * ADA_FIRST // 2 - KT // 2, KT // 2 - 1
POOL_COLS = 704
ADA_LATER = ADA_UP + ADA_HEADS + ADA_BACK
REST_PANELS = (CHUNKS[2] + 8) + 6 + 2 + 8 + ADA_HEADS + 4 + ADA_BACK + 16 + 4 + FFN_PANELS
MIX_ORDER = [("mlp", 0), ("channels", 0), ("mlp", 1), ("taps", 0), ("norms", 0), ("combine", 0), ("tokens", 0),
             ("turn", 0), ("taps", 1), ("norms", 1), ("forward", 0), ("combine", 1), ("inverse", 0),
             ("turn", 1), ("squares", 0), ("forward", 1), ("low_rank", 0), ("inverse", 1)]


class Due:

    entered = None

    def __init__(self, engine, eng, per_pass, start):
        self.engine, self.eng, self.per_pass, self.n, self.loops = engine, eng, per_pass, dict(start), []

    def __call__(self, sem, k=1):
        name = sem.name
        self.n[name] = self.n.get(name, 0) + k
        value = self.n[name]
        for key, reg in self.loops:
            step = self.per_pass.get(key, {}).get(name, 0)
            if step:
                value = reg * step + value
        return value

    def now(self, sem):
        return self(sem, 0)

    @contextmanager
    def loop(self, label, count):
        key, before = (self.engine, label), dict(self.n)
        self.eng.sem_inc(self.entered, 1)
        with self.eng.Fori(0, count) as reg:
            self.loops.append((key, reg))
            yield reg
            self.loops.pop()
        step = {s: v - before.get(s, 0) for s, v in self.n.items()}
        self.per_pass[key] = step
        for s, v in step.items():
            self.n[s] += (count - 1) * v


def program(nc, per_pass, x, w_first, w_ada, w_up, w_down, w_mix, w_qkv, w_gate, w_out, tables, small, cst_in, cvec, feats, par,
            y_out, ckv_out, krope_out):
    ctx = ExitStack()
    with ctx:
        def sem(name):
            return ctx.enter_context(nc.semaphore(name))

        base = (nc.sbuf_base + 63) // 64 * 64

        def place(at, *specs):
            out = []
            for name, shape, dt in specs:
                out.append(nc.alloc_sbuf_tensor_at(name, shape, dt, offset=at))
                at += 4 * int(np.prod(shape[1:]))
                at = (at + 31) // 32 * 32
            return out, at

        (h, raw, whi, wlo), at = place(base, ("h", [P, KT, T], F32), ("raw", [P, 2, PANEL], F32),
                                       ("whi", [P, 2, PANEL], F32R), ("wlo", [P, 2, PANEL], F32R))
        (smh, sml, cs_t, pr, ada0, ada, gm), at = place(
            at, ("small_hi", [P, NSM], F32R), ("small_lo", [P, NSM], F32R), ("constants", [P, NCST], F32),
            ("params", [P, NPAR], F32), ("ada_first", [P, DEPTH * 16, 2], F32),
            ("ada_t", [P, 72, 2], F32), ("norm_scale", [P, 24, 2], F32))
        (stat, csr), at = place(at, ("softmax_stats", [P, 16], F32), ("c_split", [P, 4 * KT + P], F32R))
        X0 = at
        (xh, xl), at = place(X0, ("x_hi", [P, 8, T], F32R), ("x_lo", [P, 8, T], F32R))
        N0 = at
        (nh, nl), at = place(N0, ("n_hi", [P, KT, T], F32R), ("n_lo", [P, KT, T], F32R))
        W0 = at
        (sg, hf, acc, sq, rs, rr, tn), end1 = place(
            W0, ("gate_act", [P, 2, T], F32), ("hidden", [P, 2, T], F32), ("sq_sum", [P, T], F32),
            ("squares", [P, T], F32), ("rms", [P, T], F32), ("inv_rms", [P, T], F32), ("scaled", [P, 2, T], F32))
        (csil, cvt), _ = place(W0, ("c_silu", [P, KT, 2], F32), ("c_raw", [P, KT, 2], F32))
        R0 = (nc.sbuf_usable_end - 4 * TL) // 64 * 64
        (row,), _ = place(R0, ("ada_rows", [P, 2, 256], F32))
        (krt,), _ = place(R0, ("rope_tmp", [P, TL], F32))
        (smraw,), _ = place(N0, ("small_raw", [P, NSM], F32))
        (qa, kvr, krr), A0 = place(W0, ("q_low", [P, 2, T], F32), ("kv_low", [P, T], F32), ("k_rope_h2", [P, T], F32))
        (qnh, qnl), _ = place(W0, ("qn_hi", [P, 2, T], F32R), ("qn_lo", [P, 2, T], F32R))
        (hyx,), wt = place(A0, ("hyena_x", [P, 6, T], F32))
        UP = T + 4
        (upad, ft), end2 = place(wt, ("conv_pad", [P, 2, UP], F32), ("features", [P, T], F32))
        (mz, mz2, mk, mr), _ = place(N0, ("sin_h", [P, T], F32), ("sin_z", [P, T], F32), ("sin_k", [P, T], F32),
                                     ("sin_r", [P, T], F32))
        (reb, hbb, pp, yf, ab), end3 = place(
            wt, ("re_part", [P, 2 * HYW], F32), ("im_part", [P, HYW], F32), ("products", [P, 2, HYW], F32),
            ("y_freq", [P, 2 * HYW], F32), ("abs_filter", [P, 2 * HYW], F32))
        (inv,), _ = place(X0, ("inv_l1", [P, 2, HYW], F32))
        XT = 4 * T
        (fnh,), _ = place(X0, ("fnet_in_hi", [P, 2, T], F32R))
        (fah, ), _ = place(X0 + 2 * XT, ("fnet_mid_hi", [P, 5, 512], F32R))
        (fnl,), _ = place(X0 + 8 * XT, ("fnet_in_lo", [P, 2, T], F32R))
        (fal, ), _ = place(X0 + 10 * XT, ("fnet_mid_lo", [P, 5, 512], F32R))
        (tmh, tml, hd), _ = place(N0, ("tok_hi", [P, 5, 3 * HYW], F32R), ("tok_lo", [P, 5, 3 * HYW], F32R),
                                  ("taps", [P, 5, 2 * HYW], F32))
        (yh,), _ = place(X0 + 2 * XT, ("spec_hi", [P, 10, HYW], F32R))
        (yl,), _ = place(X0 + 10 * XT, ("spec_lo", [P, 10, HYW], F32R))
        NPT = 5 * TL + TC
        (pth, ptl, qh, ql, qf, kh1, kl1), _ = place(
            N0, ("probs_t_hi", [P, NPT], F32R), ("probs_t_lo", [P, NPT], F32R), ("q_hi", [P, 2, T], F32R),
            ("q_lo", [P, 2, T], F32R), ("q_f32", [P, T], F32), ("k_hi1", [P, KEYS], F32R), ("k_lo1", [P, KEYS], F32R))
        (asq,), _ = place(N0 + 4 * 2 * 5 * 3 * HYW, ("att_sq", [P, 3, T], F32))
        (ars, art, kro), _ = place(N0, ("att_rms", [P, 2, T], F32), ("att_scaled", [P, 3, T], F32), ("k_roped", [P, T], F32))
        (kh, kl, vh, vl, pm, ckh, ckl), _ = place(
            A0, ("k_hi", [P, KEYS], F32R), ("k_lo", [P, KEYS], F32R), ("v_hi", [P, KEYS], F32R), ("v_lo", [P, KEYS], F32R),
            ("probs", [P, 2, T], F32), ("ckv_hi", [P, KEYS], F32R), ("ckv_lo", [P, KEYS], F32R))
        khs, kls = (kh, kh1), (kl, kl1)
        assert max(end1, end2) <= R0 and end3 <= nc.sbuf_usable_end and A0 + 16 * KEYS + 8 * T + 8 * KEYS <= R0
        (yc, sgm, prod), _ = place(W0, ("mixed", [P, KT, T], F32), ("branch_gate", [P, 3, T], F32), ("branch", [P, T], F32))

        tps = ctx.enter_context(nc.psum_tensor("tile_psum", [P, 2, 2, 512], F32))
        mps = ctx.enter_context(nc.psum_tensor("misc_psum", [P, 2, 2, 512], F32))

        def flat(ps, s):
            return ps[:, s].rearrange("p a b -> p (a b)")

        def halves(ap):
            return ap.rearrange("p (a b) -> p a b", a=2)

        def cst(name):
            return cs_t[:, CST[name][0]:CST[name][1]]

        def prm(name, a=0, b=None):
            lo, hi = PAR[name]
            return pr[:, lo + a:(hi if b is None else lo + b)]

        csr4 = csr[:, 0:4 * KT].rearrange("p (k c) -> p k c", c=4)
        ident, ones, eps, sel = cst("ident"), cst("ones"), cst("eps"), cst("sel")

        def probs(n):
            return prm("w3", 0, T) if n % 3 == 2 else pm[:, n % 3, :]

        def smat(ap, at, n=P):
            return ap[:, at:at + n]

        loaded = [sem(f"panel_loaded{s}") for s in range(2)]
        hi_ready = sem("panel_hi_ready")
        pool_part, dve_part = sem("panel_lo_pool"), sem("panel_lo_dve")
        lo_ready = sem("panel_lo_ready")
        tile_done = [sem(f"tile_done{s}") for s in range(2)]
        tile_free = [sem(f"tile_free{s}") for s in range(2)]
        misc_done = [sem(f"misc_done{s}") for s in range(2)]
        misc_free = [sem(f"misc_free{s}") for s in range(2)]
        dve_own = sem("dve_own")
        consts_in, small_in, par_in = sem("constants_in"), sem("small_in"), sem("params_in")
        x_in, c_in, feat_in = sem("x_in"), sem("c_in"), sem("features_in")
        small_hi, small_split = sem("small_hi"), sem("small_split")
        c_clear, silu_out, c_hi, c_split = sem("c_split_clear"), sem("silu_c_out"), sem("c_hi"), sem("c_split_ready")
        sin_in, sin_out = sem("sin_in"), sem("sin_out")
        rows_out = sem("ada_rows_out")
        sq_out, sq_used, sum_ready = sem("squares_out"), sem("squares_used"), sem("sq_sum_ready")
        rms_out, t_ready, hi_out, n_ready = sem("rms_out"), sem("scaled_ready"), sem("n_hi_out"), sem("n_ready")
        hid_hi, hid_ready = sem("hidden_hi"), sem("hidden_ready")
        spilled = sem("n_spilled")
        back = [sem(f"n_back{half}") for half in range(2)]
        conv_in, conv_used, v_ready = sem("conv_in"), sem("conv_used"), sem("v_ready")
        taps_ready, abs_ready, abs_used, bwd_sum = sem("taps_ready"), sem("abs_ready"), sem("abs_used"), sem("bwd_sum_out")
        filter_ready, table_used = sem("filter_split"), sem("table_used")
        parts_out, parts_used, spec_ready = sem("spectrum_parts"), sem("spectrum_parts_used"), sem("spectrum_ready")
        op_hi, z_new, z_split, y_done = sem("operand_hi"), sem("z_new"), sem("z_split"), sem("y_done")
        asq_ready, low_ready, low_hi, low_split = sem("low_squares"), sem("low_scaled"), sem("low_hi"), sem("low_split")
        krope_ready, q_copy, q_roped, q_split = sem("k_roped_ready"), sem("q_copied"), sem("q_roped_ready"), sem("q_split")
        prob_in, prob_ready = sem("neg_max_ready"), sem("probs_ready")
        y_ready, stored = sem("y_ready"), sem("outputs_stored")
        Due.entered = sem("loop_entered")
        credit = {lo_ready.name: 2, q_split.name: 1}

        n_keep = [nc.dram_tensor(f"n_keep{i}", [P, KT, T], F32).ap() for i in range(2)]

        class Slot:

            def __init__(self, s, done, free, due):
                self.s, self.done, self.free = s, done, free
                self.done_at = due(done)
                self.reusable_at = due(free)
                self.free_at = self.reusable_at + 1

        class Slots:

            def __init__(self, due):
                self.due, self.tiles, self.miscs = due, 0, 0

            def tile(self):
                s, self.tiles = self.tiles % 2, self.tiles + 1
                return Slot(s, tile_done[s], tile_free[s], self.due)

            def misc(self):
                s, self.miscs = self.miscs % 2, self.miscs + 1
                return Slot(s, misc_done[s], misc_free[s], self.due)

        block = ctx.enter_context(nc.Block())

        @block.sync
        def _(sp):
            due = Due("sp", sp, per_pass, {})
            slot = [0]

            def load(src, cols):
                s = slot[0] % 2
                slot[0] += 1
                sp.wait_ge(lo_ready, due(lo_ready))
                sp.dma_start(raw[:, s, 0:cols], src).then_inc(loaded[s], 16)

            def pairs(label, src, first, count, cols=PANEL):
                with due.loop(label, count // 2) as i:
                    for k in range(2):
                        load(src(i, first + k), cols)

            pairs("first", lambda i, k: w_first[bass.ds(i * 2 + k, 1)].rearrange("a p n -> (a p) n"), 0, DEPTH * ADA_FIRST)
            with due.loop("layer", DEPTH) as l:
                def ada_panel(n):
                    load(w_ada[bass.ds(l * ADA_LATER + n, 1)].rearrange("a p n -> (a p) n"), PANEL)

                def ffn(f):
                    at = 0
                    for c, n in enumerate(CHUNKS):
                        with due.loop(f"up{f}{c}", n // 2) as i:
                            for k in range(2):
                                load(w_up[bass.ds((l * 2 + f) * HT + i * 2 + (at + k), 1)].rearrange("a p n -> (a p) n"), PANEL)
                                if f == 0 and c < 2:
                                    ada_panel(i * 2 + (c * ADA_UP // 2 + k))
                        wd = w_down[0] if n == 8 else w_down[1]
                        base_row = (l * 2 + f) * 8 + 4 * c if n == 8 else (l * 2 + f) * 4
                        pairs(f"down{f}{c}", lambda i, k: wd[bass.ds(base_row + i * 2 + k, 1)]
                              .rearrange("a p n -> (a p) n"), 0, 4, 2 * n * P)
                        at += n

                ffn(0)
                pairs("mix", lambda i, k: w_mix[bass.ds(l * 6 + i * 2 + k, 1)].rearrange("a p n -> (a p) n"), 0, 6)
                for t in (4, 5) + (0, 1, 2, 3) * 2:
                    load(tables[t], PANEL)
                with due.loop("heads", 2) as i:
                    for what, n in HEAD_ORDER:
                        if what == "A":
                            ada_panel(i * (ADA_HEADS // 2) + (ADA_UP + n))
                        if what == "Q" and n % 2 == 0:
                            load(w_qkv[bass.ds(l * 4 + i * 2 + n // 2, 1)].rearrange("a p n -> (a p) n"), 7 * P)
                for n in range(ADA_BACK):
                    ada_panel(ADA_UP + ADA_HEADS + n)
                pairs("gate", lambda i, k: w_gate[bass.ds(l * 16 + i * 2 + k, 1)].rearrange("a p n -> (a p) n"), 0, 16)
                pairs("out", lambda i, k: w_out[bass.ds(l * 4 + i * 2 + k, 1)].rearrange("a p n -> (a p) n"), 0, 4)
                ffn(1)
            for k in range(2):
                load(tables[0][:, 0:P], P)
            sp.wait_ge(y_ready, due(y_ready, 8))
            sp.dma_start(y_out, h[:, :, :]).then_inc(stored, 16)
            sp.wait_ge(stored, 16 + DEPTH * 32)

        @block.gpsimd
        def _(pool):
            due = Due("pool", pool, per_pass, {})

            def low_parts(label, passes, order=(0, 1)):
                with due.loop(label, passes):
                    for n, s in enumerate(order):
                        pool.wait_ge(hi_ready, due(hi_ready))
                        pool.tensor_tensor(wlo[:, s, :], raw[:, n % 2, :], whi[:, s, :].bitcast(F32), ALU.subtract)\
                            .then_inc(lo_ready, 1)

            with due.loop("first", DEPTH * ADA_FIRST // 2):
                for s in range(2):
                    pool.wait_ge(hi_ready, due(hi_ready))
                    pool.tensor_tensor(wlo[:, s, 0:POOL_COLS], raw[:, s, 0:POOL_COLS], whi[:, s, 0:POOL_COLS].bitcast(F32),
                                       ALU.subtract).then_inc(pool_part, 1)
                    pool.wait_ge(pool_part, due(pool_part))
                    pool.wait_ge(dve_part, due(dve_part))
                    pool.sem_inc(lo_ready, 1)
            with due.loop("layer", DEPTH):
                low_parts("up00", CHUNKS[0] // 2, (0, 1, 1, 0))
                low_parts("down00", 2)
                low_parts("up01", CHUNKS[1] // 2, (0, 1, 1, 0))
                low_parts("rest", REST_PANELS // 2)
            low_parts("last", 1)

        @block.tensor
        def _(pe):
            due = Due("pe", pe, per_pass, credit)
            slots = Slots(due)
            at = [0]

            def panel_hi(s=None):
                if s is None:
                    s = at[0] % 2
                    at[0] += 1
                pe.wait_ge(hi_ready, due(hi_ready))
                return s, due(lo_ready)

            def panel(s=None):
                s, low_at = panel_hi(s)
                pe.wait_ge(lo_ready, low_at)
                return s

            def blk(s, b, n=P):
                return whi[:, s, b * P:b * P + n], wlo[:, s, b * P:b * P + n]

            def mm3(outs, w, xs, first, last):
                for n, (a, b) in enumerate(((0, 0), (0, 1), (1, 0))):
                    for o, x_ in zip(outs, xs):
                        ins = pe.matmul(o, w[a], x_[b], start=first and n == 0, stop=last and n == 2)
                return ins

            def tile():
                return taken(slots.tile()).s

            def taken(slot):
                pe.wait_ge(slot.free, slot.reusable_at)
                return slot

            def misc():
                return taken(slots.misc()).s

            def all_read(frees):
                for f in frees:
                    pe.wait_ge(f, due.now(f) + 1)

            def xs_of(hi, lo, k):
                return [(hi[:, k, j * TH:(j + 1) * TH], lo[:, k, j * TH:(j + 1) * TH]) for j in range(2)]

            def gemm(s, b0, hi, lo, k0, n, each=None, low_at=None):
                t = tile()
                for k in range(n):
                    if each is not None:
                        pe.wait_ge(*each(k))
                    for b in range(2):
                        for j, x_ in enumerate(xs_of(hi, lo, k0 + k)):
                            pe.matmul(tps[:, t, j, 0:TH], blk(s, b0 + k)[0], x_[b], start=k == 0 and b == 0, stop=False)
                if low_at is not None:
                    pe.wait_ge(lo_ready, low_at)
                for k in range(n):
                    for j, x_ in enumerate(xs_of(hi, lo, k0 + k)):
                        ins = pe.matmul(tps[:, t, j, 0:TH], blk(s, b0 + k)[1], x_[0], start=False, stop=k == n - 1)
                ins.then_inc(tile_done[t], 1)

            def column_sums(ready, rhs, n=1):
                m = misc()
                pe.wait_ge(ready, due(ready))
                for k in range(n):
                    for j in range(2):
                        ins = pe.matmul(mps[:, m, j, 0:TH], ones, rhs[k][:, j * TH:(j + 1) * TH],
                                        start=k == 0, stop=k == n - 1)
                ins.then_inc(misc_done[m], 1)

            def coming(sem, n):
                now = due.now(sem)
                due(sem, n)
                return lambda k: (sem, now + (k + 1))

            def ada_a(s=None):
                s, low_at = panel_hi(s)
                m = misc()
                for n, w in enumerate((whi, wlo)):
                    if n:
                        pe.wait_ge(lo_ready, low_at)
                    for kt in range(KT):
                        ins = pe.matmul(mps[:, m, 0, 0:256], csr[:, 4 * kt:4 * kt + P], w[:, s, kt * 256:(kt + 1) * 256],
                                        start=kt == 0 and n == 0, stop=kt == KT - 1 and n == 1)
                ins.then_inc(misc_done[m], 1)

            def ada_b(k):
                m = misc()
                pe.wait_ge(rows_out, due(rows_out))
                for j in range(2):
                    ins = pe.matmul(mps[:, m, 0, 2 * j:2 * j + 2], row[0:4, k, j * P:(j + 1) * P], sel[0:4, :],
                                    start=True, stop=True)
                ins.then_inc(misc_done[m], 1)

            def ffn(f):
                column_sums(sum_ready, [acc])
                n_coming = coming(n_ready, KT)
                for c, n in enumerate(CHUNKS):
                    with_ada = f == 0 and c < 2
                    with due.loop(f"up{f}{c}", n // 2):
                        for k in range(2):
                            s, low_at = panel_hi(k if with_ada else None)
                            gemm(s, 0, nh, nl, 0, KT, n_coming if c == 0 and k == 0 else None, low_at)
                            if with_ada:
                                ada_a(1 - k)
                            gemm(s, KT, nh, nl, 0, KT)
                            if with_ada:
                                ada_b(k)
                    hid_coming = coming(hid_ready, n)
                    with due.loop(f"down{f}{c}", 2):
                        for k in range(2):
                            s, low_at = panel_hi()
                            gemm(s, 0, xh, xl, 0, n, hid_coming if k == 0 else None, low_at)
                            gemm(s, n, xh, xl, 0, n)

            def transposes(src, tiles):
                m = misc()
                for c in range(2):
                    ins = pe.transpose(mps[:, m, 0, c * P:(c + 1) * P], src[:, 4 + c, tiles * P:(tiles + 1) * P], ident)
                ins.then_inc(misc_done[m], 1)

            pe.wait_ge(consts_in, due(consts_in, 16))

            def ada_pair():
                ada_a()
                ada_a()
                ada_b(0)
                ada_b(1)

            pe.wait_ge(c_split, due(c_split))
            for label, passes in (("first_a", FIRST_A), ("first_b", FIRST_B)):
                with due.loop(label, passes):
                    ada_pair()
            ada_pair()
            pe.wait_ge(small_split, due(small_split))
            with due.loop("layer", DEPTH):
                def filter_mlp(w, src, kk, mm=FHID):
                    m = misc()
                    for j in range(2):
                        ins = pe.matmul(mps[0:mm, m, j, 0:TH], w[0:kk, :], src[0:kk, j * TH:(j + 1) * TH],
                                        start=True, stop=True)
                    ins.then_inc(misc_done[m], 1)

                ffn(0)

                column_sums(sum_ready, [acc])
                n_coming = coming(n_ready, KT)
                with due.loop("mix", 3):
                    for k in range(2):
                        s, low_at = panel_hi()
                        gemm(s, 0, nh, nl, 0, KT, n_coming if k == 0 else None, low_at)
                        gemm(s, KT, nh, nl, 0, KT)

                def mlp(n):
                    if n == 0:
                        pe.wait_ge(feat_in, due(feat_in, 16))
                        pe.wait_ge(par_in, due(par_in, 16))
                        filter_mlp(prm("w1"), ft, 17)
                    else:
                        pe.wait_ge(sin_out, due(sin_out))
                        filter_mlp(prm("w2"), mz, FHID, P)

                def to_channels(w_of, small_at):
                    ts = [tile(), tile()]
                    for part in range(2):
                        s, low_at = panel_hi()
                        for c in range(2):
                            for k in range(4):
                                for n, w in enumerate(w_of(c, part, k)):
                                    pe.matmul(tps[:, ts[c], 0, :], w, blk(s, 4 * k, 512)[0],
                                              start=part == 0 and k == 0 and n == 0, stop=False)
                            mm3([tps[:, ts[c], 1, 0:TC]], w_of(c, part, 4),
                                [(smat(smh, small_at[part]), smat(sml, small_at[part]))], part == 0, part == 1)
                        pe.wait_ge(lo_ready, low_at)
                        for c in range(2):
                            for k in range(4):
                                ins = pe.matmul(tps[:, ts[c], 0, :], w_of(c, part, k)[0], blk(s, 4 * k, 512)[1],
                                                start=False, stop=part == 1 and k == 3)
                            if part == 1:
                                ins.then_inc(tile_done[ts[c]], 1)
                        if part == 0:
                            ins.then_inc(table_used, 1)

                def channels(_):
                    bdm = [(smat(smh, SM_BD, 256), smat(sml, SM_BD, 256))]
                    all_read(tile_free)
                    for t in range(5):
                        m = misc()
                        for c in range(2):
                            tk = slice(t * P, (t + 1) * P)
                            ins = mm3([mps[:, m, 0, c * 256:(c + 1) * 256]], (fnh[:, c, tk], fnl[:, c, tk]), bdm, True, True)
                        ins.then_inc(misc_done[m], 1)

                def tokens(_):
                    all_read(misc_free)
                    to_channels(lambda c, part, t: [x_[:, t, c * 256 + part * P:c * 256 + (part + 1) * P] for x_ in (fah, fal)],
                                (SM_FC, SM_FS))

                def taps(o):
                    if o == 0:
                        pe.wait_ge(sin_out, due(sin_out))
                    for t in range(5):
                        m = misc()
                        pe.matmul(mps[:, m, 0, :], krr[0:FHID, t * P:(t + 1) * P],
                                  prm("w3", o * 512, (o + 1) * 512)[0:FHID, :], start=True, stop=True)\
                            .then_inc(misc_done[m], 1)

                def norms(o):
                    for ts in (range(4), range(4, 5)):
                        m = misc()
                        for t in ts:
                            pe.wait_ge(abs_ready, due(abs_ready))
                            pe.matmul(mps[:, m, 0, :], ones, (ab if t % 2 == 0 else yf)[:, :], start=t == ts[0], stop=t == ts[-1])\
                                .then_inc(misc_done[m] if t == ts[-1] else abs_used, 1)

                def turn(o):
                    pe.wait_ge(v_ready, due(v_ready, 2))
                    for t in range(5):
                        transposes(hyx, t)

                def forward(o):
                    tables_at = [panel_hi(), panel_hi()]
                    all_read(misc_free)
                    pe.wait_ge(filter_ready, due(filter_ready))
                    for f in range(5):
                        m = misc()
                        for part, (col, sm) in enumerate(((0, SM_C), (HYW, SM_S))):
                            out = mps[:, m, part, :]
                            s, low_at = tables_at[part]
                            if f < 4:
                                for b, w in enumerate((whi, wlo)):
                                    if b and f == 0:
                                        pe.wait_ge(lo_ready, low_at)
                                    for t in range(4):
                                        for x_ in (tmh, tml)[:2 - b]:
                                            ins = pe.matmul(out, w[:, s, t * 512 + f * P:t * 512 + (f + 1) * P],
                                                            x_[:, t, col:col + 512], start=b == 0 and t == 0 and x_ is tmh,
                                                            stop=b == 1 and t == 3)
                            else:
                                ins = mm3([out], (smat(smh, sm), smat(sml, sm)),
                                          [(tmh[:, 4, col:col + 512], tml[:, 4, col:col + 512])], True, True)
                        ins.then_inc(misc_done[m], 1)

                def inverse(o):
                    pe.wait_ge(spec_ready, due(spec_ready, 5))
                    to_channels(lambda c, part, f: [x_[:, 2 * f + part, c * P:(c + 1) * P] for x_ in (yh, yl)], (SM_CI, SM_SI))

                def low_rank(_):
                    column_sums(asq_ready, [asq[:, k, :] for k in range(2)], 2)
                    column_sums(asq_ready, [asq[:, 2, :]])

                steps = dict(mlp=mlp, channels=channels, tokens=tokens, taps=taps, norms=norms, turn=turn,
                             forward=forward, inverse=inverse, low_rank=low_rank)
                for what, o in MIX_ORDER:
                    if what in steps:
                        steps[what](o)

                pe.wait_ge(low_split, due(low_split, 4))
                with due.loop("heads", 2):
                    s = [None, None]
                    keys, vals, turned = [None] * 4, None, [None, None]
                    for what, n in HEAD_ORDER:
                        h_, qt = n // 5, n % 5
                        if what == "Q":
                            if n % 2 == 0:
                                s[n // 2] = panel()
                            t = tile()
                            for k in range(2):
                                ins = mm3([tps[:, t, i, 0:TH] for i in range(2)], blk(s[n // 2], 2 * (n % 2) + k),
                                          xs_of(qnh, qnl, k), k == 0, k == 1)
                            ins.then_inc(tile_done[t], 1)
                        elif what == "K":
                            keys[n] = m = taken(slots.misc())
                            ks = [slice(0, KEYS // 2), slice(KEYS // 2, KEYS)]
                            mm3([mps[:, m.s, i, 0:KEYS // 2] for i in range(2)], blk(s[n // 2], 4 + n % 2),
                                [(ckh[:, i], ckl[:, i]) for i in ks], True, True).then_inc(m.done, 1)
                        elif what == "V":
                            vals = m = taken(slots.misc())
                            for kt in range(6):
                                kk = slice(kt * P, (kt + 1) * P)
                                ins = mm3([mps[:, m.s, kt // 3, (kt % 3) * P:(kt % 3 + 1) * P]], (ckh[:, kk], ckl[:, kk]),
                                          [blk(s[n], 6)], True, True)
                            ins.then_inc(m.done, 1)
                        elif what == "S":
                            if qt == 0:
                                pe.wait_ge(keys[h_].free, keys[h_].free_at)
                                pe.wait_ge(q_split, due(q_split))
                            m = misc()
                            kh_, kl_ = khs[h_ % 2], kls[h_ % 2]
                            w = (qh[0:QK, h_ % 2, qt * P:(qt + 1) * P], ql[0:QK, h_ % 2, qt * P:(qt + 1) * P])
                            if qt < 4:
                                mm3([mps[:, m, 0, :]], w, [(kh_[0:QK, 0:TL], kl_[0:QK, 0:TL])], True, True)
                                ins = mm3([mps[:, m, 1, 0:P]], w, [(kh_[0:QK, T:KEYS], kl_[0:QK, T:KEYS])], True, True)
                            else:
                                ins = mm3([mps[:, m, 0, 0:P]], w, [(kh_[0:QK, TL:T], kl_[0:QK, TL:T])], True, True)
                            ins.then_inc(misc_done[m], 1)
                        elif what == "T":
                            t = taken(slots.tile())
                            turned[t.s] = t
                            pe.wait_ge(prob_ready, due(prob_ready))
                            for kt in range(5 if qt < 4 else 1):
                                ins = pe.transpose(flat(tps, t.s)[:, kt * P:(kt + 1) * P], probs(n)[:, kt * P:(kt + 1) * P], ident)
                            ins.then_inc(t.done, 1)
                        elif what == "P":
                            for t in turned + [vals]:
                                pe.wait_ge(t.free, t.free_at)
                            t = tile()
                            for kt in range(5):
                                vt = kt if kt < 4 else 5
                                kk = slice(vt * P, (vt + 1) * P)
                                mm3([tps[:, t, 0, :]], (vh[:, kk], vl[:, kk]),
                                    [(pth[:, kt * TL:(kt + 1) * TL], ptl[:, kt * TL:(kt + 1) * TL])], kt == 0, kt == 4)
                            mm3([tps[:, t, 1, 0:TC]], (vh[:, TL:T], vl[:, TL:T]), [(pth[:, 5 * TL:], ptl[:, 5 * TL:])], True, True)\
                                .then_inc(tile_done[t], 1)
                        elif what == "A":
                            ada_a()
                        elif what == "B":
                            ada_b(n % 2)

                for _ in range(ADA_BACK // 2):
                    ada_pair()
                all_read(tile_free)
                pe.wait_ge(z_split, due(z_split, 2))
                back_at = [due(b, 32) for b in back]
                with due.loop("gate", KT):
                    s, low_at = panel_hi()
                    gemm(s, 0, nh, nl, 0, KT, lambda k: (back[2 * k // KT], back_at[2 * k // KT]), low_at)
                    gemm(s, KT, nh, nl, 0, KT)
                    s, low_at = panel_hi()
                    gemm(s, 0, nh, nl, 0, KT, None, low_at)
                    gemm(s, 8, xh, xl, 0, 2)
                    gemm(s, 10, xh, xl, 2, 4)
                    gemm(s, 14, xh, xl, 6, 2)
                n_coming = coming(n_ready, KT)
                with due.loop("out", 2):
                    for k in range(2):
                        s, low_at = panel_hi()
                        gemm(s, 0, nh, nl, 0, KT, n_coming if k == 0 else None, low_at)
                        gemm(s, KT, nh, nl, 0, KT)
                ffn(1)
            column_sums(sum_ready, [acc])


        @block.scalar
        def _(act):
            due = Due("act", act, per_pass, {})
            slots = Slots(due)
            at = [0]

            def round_panel(s=None):
                r = at[0] % 2
                at[0] += 1
                act.wait_ge(loaded[r], due(loaded[r], 16))
                act.activation(whi[:, r if s is None else s, :], raw[:, r, :], ACT.Copy).then_inc(hi_ready, 1)

            def seen(slot):
                act.wait_ge(slot.done, slot.done_at)
                return slot

            def tile():
                return seen(slots.tile())

            def misc():
                return seen(slots.misc())

            def tile2(t, g=False):
                return tps[:, t.s, :, 0:TH]

            def square(m, t=None):
                if t is not None:
                    act.wait_ge(t.free, t.free_at)
                src = h[:, bass.ds(m, 1), :].rearrange("p a t -> p (a t)")
                act.activation(sq[:, :], src, ACT.Square).then_inc(sq_out, 1)

            def root(out, width, m, ready):
                act.activation(halves(out), mps[:, m.s, :, 0:TH], ACT.Sqrt, bias=eps, scale=1.0 / width).then_inc(ready, 1)

            def norm(i):
                root(rs[:, :], D, misc(), rms_out)
                for k in range(KT):
                    act.wait_ge(t_ready, due(t_ready))
                    for g, (_, a, b) in enumerate(GROUPS):
                        ins = act.activation(nh[:, k, a:b], tn[:, k % 2, a:b], ACT.Identity, bias=ada[:, 24 * i + k, g:g + 1])
                    ins.then_inc(hi_out, 1)
                due(n_ready, KT)

            def ada_a(k, s=None):
                m = misc()
                act.activation(row[0:4, k, :], mps[0:4, m.s, 0, 0:256], ACT.Copy).then_inc(rows_out, 1)
                round_panel(s)
                act.wait_ge(rows_out, due(rows_out))
                act.sem_inc(m.free, 1)

            def into_h(label, last):
                with due.loop(label, 2) as i:
                    for k in range(2):
                        t = [slots.tile(), tile()]
                        round_panel()
                        if last:
                            for j in range(2):
                                square(i * 4 + (2 * k + j), t[j])

            def ffn(f):
                norm(2 * f)
                for c, n in enumerate(CHUNKS):
                    with_ada = f == 0 and c < 2
                    with due.loop(f"up{f}{c}", n // 2) as i:
                        for k in range(2):
                            t = tile()
                            act.activation(halves(sg[:, k, :]), tile2(t), ACT.Silu).then_inc(t.free, 1)
                            if with_ada:
                                ada_a(k, 1 - k)
                            t = tile()
                            round_panel(k if with_ada else None)
                            act.wait_ge(t.free, t.free_at)
                            act.activation(xh[:, bass.ds(i * 2 + k, 1), :].rearrange("p a t -> p (a t)"), hf[:, k, :], ACT.Copy)\
                                .then_inc(hid_hi, 1)
                            if with_ada:
                                slots.misc()
                    into_h(f"down{f}{c}", c == 2)

            def split_hi(out, src, ready=op_hi):
                act.activation(out, src, ACT.Copy).then_inc(ready, 1)

            act.dma_start(cvt[:, :, :], cvec).then_inc(c_in, 16)
            act.dma_start(cs_t[:, :], cst_in).then_inc(consts_in, 16)
            act.dma_start(smraw[:, :], small).then_inc(small_in, 16)
            act.dma_start(h[:, :, :], x).then_inc(x_in, 16)
            act.dma_start(pr[:, :], par[0]).then_inc(par_in, 16)
            act.wait_ge(c_in, due(c_in, 16))
            act.activation(csil[:, :, :], cvt[:, :, :], ACT.Silu).then_inc(silu_out, 1)
            act.wait_ge(silu_out, due(silu_out))
            act.wait_ge(c_clear, due(c_clear))
            act.activation(csr4[:, :, 0:2], csil[:, :, :], ACT.Copy).then_inc(c_hi, 1)
            round_panel()
            round_panel()
            with due.loop("first_a", FIRST_A):
                for k in range(2):
                    ada_a(k)
                for k in range(2):
                    slots.misc()

            def ada_and_squares(i):
                for k in range(2):
                    square(i * 2 + k)
                    ada_a(k)
                    act.wait_ge(sq_used, due(sq_used))
                for k in range(2):
                    slots.misc()

            act.wait_ge(x_in, due(x_in, 16))
            with due.loop("first_b", FIRST_B) as i:
                ada_and_squares(i)
            ada_and_squares(FIRST_B)
            act.wait_ge(small_in, due(small_in, 16))
            split_hi(smh[:, :], smraw[:, :], small_hi)
            act.wait_ge(small_hi, due(small_hi))
            with due.loop("layer", DEPTH) as l:
                ffn(0)

                norm(1)
                act.wait_ge(n_ready, due.now(n_ready))
                act.dma_start(n_keep[0], nh[:, :, :].bitcast(F32)).then_inc(spilled, 16)
                act.dma_start(n_keep[1], nl[:, :, :].bitcast(F32)).then_inc(spilled, 16)
                act.dma_start(ft[:, :], feats).then_inc(feat_in, 16)
                for c in range(2):
                    t = tile()
                    split_hi(halves(fnh[:, c, :]), tile2(t))
                round_panel()
                for c in range(6):
                    t = tile()
                    if c >= 2:
                        act.wait_ge(conv_used, due(conv_used))
                    for bank, c0, c1, t0, t1, g in SEGMENTS:
                        ins = act.activation(upad[:, c % 2, t0 + 1 + 2 * g:t1 + 1 + 2 * g], tps[:, t.s, bank, c0:c1], ACT.Copy)
                        ins.then_inc(t.free if g else conv_in, 1)
                    if c % 2:
                        round_panel()
                due(conv_used, 2)
                for c in range(2):
                    t = tile()
                    act.activation(halves(qa[:, c, :]), tile2(t), ACT.Copy).then_inc(t.free, 1)
                round_panel()
                t = tile()
                act.activation(halves(kvr[:, :]), tile2(t), ACT.Copy).then_inc(t.free, 1)
                t = tile()
                act.activation(halves(krr[FHID:P, :]), tps[FHID:P, t.s, :, 0:TH], ACT.Copy).then_inc(t.free, 1)
                round_panel()
                act.wait_ge(t.free, t.free_at)
                act.dma_start(krope_out[bass.ds(l, 1)].rearrange("a p n -> (a p) n"), krr[FHID:FHID + ROPE, TL:T]).then_inc(stored, 16)

                act.wait_ge(spilled, due(spilled, 32))

                def mlp(n):
                    slots.misc()
                    act.wait_ge(sin_in, due(sin_in))
                    act.activation((mz if n == 0 else krr)[0:FHID, :], mr[0:FHID, :], ACT.Sin).then_inc(sin_out, 1)

                def channels(_):
                    for t in range(5):
                        m = misc()
                        split_hi(fah[:, t, :], mps[:, m.s, 0, :])

                def tokens(_):
                    act.wait_ge(table_used, due(table_used))
                    round_panel()
                    for c in range(2):
                        t = tile()
                        if c:
                            round_panel()
                        split_hi(xh[:, 6 + c, :], flat(tps, t.s)[:, 0:T])

                def taps(o):
                    for t in range(5):
                        slots.misc()

                def norms(o):
                    for t in range(5):
                        act.wait_ge(taps_ready, due(taps_ready))
                        if t in (2, 3):
                            act.wait_ge(abs_used, due(abs_used))
                        if t == 4:
                            act.wait_ge(abs_used, due(abs_used))
                            m = misc()
                            split_hi(inv[:, 0, :], mps[:, m.s, 0, HYW:2 * HYW], bwd_sum)
                        act.activation((ab if t % 2 == 0 else yf)[:, :], hd[:, t, :], ACT.Abs).then_inc(abs_ready, 1)
                    m = misc()
                    split_hi(inv[:, 1, :], mps[:, m.s, 0, HYW:2 * HYW], bwd_sum)

                def turn(o):
                    for t in range(5):
                        m = misc()
                        split_hi(tmh[:, t, HYW:2 * HYW], mps[:, m.s, 0, 0:HYW])

                def forward(o):
                    for f in range(5):
                        m = misc()
                        act.wait_ge(parts_used, due(parts_used))
                        act.activation(reb[:, :], mps[:, m.s, 0, :], ACT.Copy)
                        act.activation(hbb[:, :], mps[:, m.s, 1, HYW:2 * HYW], ACT.Copy).then_inc(parts_out, 1)
                        if f == 3:
                            round_panel()
                            round_panel()

                def squares(_):
                    for k in range(2):
                        ins = act.activation(asq[:, k, :], qa[:, k, :], ACT.Square)
                    ins.then_inc(asq_ready, 1)
                    act.activation(asq[:, 2, :], kvr[:, :], ACT.Square).then_inc(asq_ready, 1)

                def low_rank(_):
                    m = misc()
                    root(ars[:, 0, :], 2 * P, m, rms_out)
                    m = misc()
                    root(ars[:, 1, :], P, m, rms_out)

                R = slice(NOPE, QK)

                def inverse(o):
                    act.wait_ge(table_used, due(table_used))
                    round_panel()
                    if o == 1:
                        act.wait_ge(low_ready, due(low_ready))
                        split_hi(ckh[:, 0:T], art[:, 2, :], low_hi)
                        split_hi(ckh[:, T:KEYS], prm("ckv"), low_hi)
                        act.dma_start(ckv_out[bass.ds(l, 1)].rearrange("a p n -> (a p) n"), art[:, 2, TL:T]).then_inc(stored, 16)
                        act.wait_ge(krope_ready, due(krope_ready))
                        for k_ in khs:
                            split_hi(k_[R, 0:TL], kro[R, 0:TL], low_hi)
                            split_hi(k_[R, TL:T], krr[R, TL:T], low_hi)
                            split_hi(k_[R, T:KEYS], prm("krope")[R, :], low_hi)
                    slots.tile()
                    tile()
                    round_panel()

                steps = dict(mlp=mlp, channels=channels, tokens=tokens, taps=taps, norms=norms, turn=turn,
                             forward=forward, inverse=inverse, squares=squares, low_rank=low_rank)
                for what, o in MIX_ORDER:
                    if what in steps:
                        steps[what](o)
                for c in range(2):
                    act.wait_ge(z_new, due(z_new))
                    split_hi(xh[:, c, :], hyx[:, 4 + c, :])

                act.wait_ge(low_ready, due(low_ready, 3))
                for k in range(2):
                    split_hi(qnh[:, k, :], art[:, k, :], low_hi)
                act.wait_ge(stored, due(stored, 32))
                with due.loop("heads", 2) as i:
                    for what, n in HEAD_ORDER:
                        h_, qt = n // 5, n % 5
                        if what == "Q":
                            t = tile()
                            act.wait_ge(q_split, due(q_split))
                            act.activation(halves(qf[0:NOPE, :]), tps[0:NOPE, t.s, :, 0:TH], ACT.Copy)
                            act.activation(qf[R, TL:T], tps[R, t.s, 1, TL - TH:TH], ACT.Copy).then_inc(q_copy, 1)
                        elif what == "K":
                            m = misc()
                            split_hi(halves(khs[n % 2][0:NOPE, :]), mps[0:NOPE, m.s, :, 0:KEYS // 2])
                            if n % 2:
                                round_panel()
                        elif what == "QS":
                            act.wait_ge(q_roped, due(q_roped))
                            split_hi(qh[0:QK, n % 2, :], qf[0:QK, :])
                        elif what == "V":
                            m = misc()
                            split_hi(halves(vh[:, :]), mps[:, m.s, :, 0:KEYS // 2])
                        elif what == "S":
                            m = misc()
                            w, c = (TL + PAST if qt < 4 else TC), n % 3
                            act.wait_ge(prob_in, due(prob_in))
                            act.activation(probs(n)[:, 0:w], flat(mps, m.s)[:, 0:w], ACT.Exp, bias=stat[:, 3 + c:4 + c],
                                           scale=QK ** -0.5, accum_out=stat[:, 6 + c:7 + c]).then_inc(m.free, 1)
                        elif what == "T":
                            t = tile()
                            if qt < 4:
                                split_hi(pth[:, 0:5 * TL].rearrange("p (a t) -> p a t", a=5)[:, :, qt * P:(qt + 1) * P],
                                         flat(tps, t.s)[:, 0:T].rearrange("p (a t) -> p a t", a=5))
                            else:
                                split_hi(pth[:, 5 * TL:], tps[:, t.s, 0, 0:TC])
                        elif what == "P":
                            t = tile()
                            rows = slice((n % 2) * VD, (n % 2 + 1) * VD)
                            split_hi(xh[rows, bass.ds(i * 2 + (2 + n // 2), 1), :].rearrange("p a t -> p (a t)"), flat(tps, t.s)[rows, 0:T])
                        elif what == "A":
                            ada_a(n % 2)
                        elif what == "B":
                            slots.misc()
                act.wait_ge(t.free, t.free_at)
                for half in range(2):
                    ks = slice(half * KT // 2, (half + 1) * KT // 2)
                    act.dma_start(nh[:, ks, :].bitcast(F32), n_keep[0][:, ks]).then_inc(back[half], 16)
                    act.dma_start(nl[:, ks, :].bitcast(F32), n_keep[1][:, ks]).then_inc(back[half], 16)
                for n in range(ADA_BACK):
                    ada_a(n % 2)
                    if n % 2:
                        slots.misc()
                        slots.misc()

                with due.loop("gate", KT):
                    for b in range(3):
                        t = tile()
                        act.activation(halves(sgm[:, b, :]), tile2(t), ACT.Sigmoid).then_inc(t.free, 1)
                        if b == 1:
                            round_panel()
                    slots.tile()
                    slots.tile()
                    tile()
                    round_panel()
                act.wait_ge(y_done, due(y_done))
                act.dma_start(pr[:, :], par[bass.ds(l + 1, 1)].rearrange("a p n -> (a p) n")).then_inc(par_in, 16)
                for k in range(KT):
                    split_hi(nh[:, k, :], yc[:, k, :], hi_out)
                due(n_ready, KT)
                into_h("out", True)
                ffn(1)
            root(rs[:, :], D, misc(), rms_out)
            act.wait_ge(par_in, 16 * (DEPTH + 1))

        @block.vector
        def _(dve):
            due = Due("dve", dve, per_pass, {})
            slots = Slots(due)

            def own(ins):
                ins.then_inc(dve_own, 1)
                dve.wait_ge(dve_own, due(dve_own))

            def seen(slot):
                dve.wait_ge(slot.done, slot.done_at)
                return slot

            def tile():
                return seen(slots.tile())

            def misc():
                return seen(slots.misc())

            def tile2(t):
                return tps[:, t.s, :, 0:TH]

            def lo_part(out, src, hi, ready, after=None):
                after = op_hi if after is None else after
                dve.wait_ge(after, due(after))
                dve.tensor_tensor(out, src, hi.bitcast(F32), ALU.subtract).then_inc(ready, 1)

            def add_square():
                dve.wait_ge(sq_out, due(sq_out))
                dve.tensor_tensor(acc[:, :], acc[:, :], sq[:, :], ALU.add).then_inc(sq_used, 1)
                dve.wait_ge(sq_used, due(sq_used))

            def inv_rms():
                m = slots.misc()
                dve.wait_ge(rms_out, due(rms_out))
                dve.reciprocal(rr[:, :], rs[:, :]).then_inc(m.free, 1)
                dve.wait_ge(m.free, m.free_at)

            def norm(i):
                inv_rms()

                def scaled(k):
                    for g, (_, a, b) in enumerate(GROUPS):
                        ins = dve.scalar_tensor_tensor(out=tn[:, k % 2, a:b], in0=h[:, k, a:b], scalar=gm[:, 8 * i + k, g:g + 1],
                                                       in1=rr[:, a:b], op0=ALU.mult, op1=ALU.mult)
                    ins.then_inc(t_ready, 1)

                scaled(0)
                for k in range(KT):
                    if k + 1 < KT:
                        if k:
                            dve.wait_ge(n_ready, due(n_ready))
                        scaled(k + 1)
                    dve.wait_ge(t_ready, due(t_ready))
                    dve.wait_ge(hi_out, due(hi_out))
                    for g, (_, a, b) in enumerate(GROUPS):
                        ins = dve.scalar_tensor_tensor(out=nl[:, k, a:b], in0=tn[:, k % 2, a:b], scalar=ada[:, 24 * i + k, g:g + 1],
                                                       in1=nh[:, k, a:b].bitcast(F32), op0=ALU.add, op1=ALU.subtract)
                    ins.then_inc(n_ready, 1)
                due(n_ready, 2)

            b_ada = prm("b_ada").rearrange("p (a b) -> p a b", b=2)

            def modulation(i):
                sc = slice(24 * i + 8, 24 * i + 16)
                ng = prm("norm_g").rearrange("p (a b) -> p a b", b=2)
                own(dve.scalar_tensor_tensor(out=gm[:, 8 * i:8 * i + 8, :], in0=ada[:, sc, :], scalar=1.0,
                                             in1=ng[:, 8 * i:8 * i + 8, :], op0=ALU.add, op1=ALU.mult))

            def half_gate(i):
                gs = slice(24 * i + 16, 24 * i + 24)
                own(dve.tensor_scalar(ada[:, gs, :], ada[:, gs, :], 0.5, None, ALU.mult))

            def ada_b(n):
                m = misc()
                at_ = bass.ds(n * 2, 2)
                dve.tensor_tensor(ada[:, at_, :], mps[:, m.s, 0, 0:4].rearrange("p (a b) -> p a b", b=2),
                                  b_ada[:, at_, :], ALU.add).then_inc(m.free, 1)
                return m

            def into_h(label, section, last):
                if last:
                    own(dve.memset(acc[:, :], 0.0))
                with due.loop(label, 2) as i:
                    for k in range(4):
                        m, t = i * 4 + k, tile()
                        for bank, c0, c1, t0, t1, g in SEGMENTS:
                            hs = h[:, bass.ds(m, 1), t0:t1].rearrange("p a t -> p (a t)")
                            gate = ada[:, bass.ds(m + 8 * section, 1), g:g + 1].rearrange("p a t -> p (a t)")
                            ins = dve.scalar_tensor_tensor(out=hs, in0=tps[:, t.s, bank, c0:c1], scalar=gate, in1=hs,
                                                           op0=ALU.mult, op1=ALU.add)
                        ins.then_inc(t.free, 1)
                        if last:
                            add_square()
                dve.wait_ge(t.free, t.free_at)
                if last:
                    dve.sem_inc(sum_ready, 1)

            def ffn(f):
                norm(2 * f)
                for c, n in enumerate(CHUNKS):
                    with_ada = f == 0 and c < 2
                    with due.loop(f"up{f}{c}", n // 2) as i:
                        for k in range(2):
                            if with_ada:
                                slots.misc()
                            tg = slots.tile()
                            t = tile()
                            dve.wait_ge(tg.free, tg.free_at)
                            dve.tensor_tensor(halves(hf[:, k, :]), halves(sg[:, k, :]), tile2(t), ALU.mult).then_inc(t.free, 1)
                            dve.wait_ge(t.free, t.free_at)
                            kk = bass.ds(i * 2 + k, 1)
                            lo_part(xl[:, kk, :].rearrange("p a t -> p (a t)"), hf[:, k, :],
                                    xh[:, kk, :].rearrange("p a t -> p (a t)"), hid_ready, hid_hi)
                            if with_ada:
                                m = ada_b(i * 2 + (ADA_FIRST + c * ADA_UP // 2 + k))
                    if with_ada:
                        dve.wait_ge(m.free, m.free_at)
                        (half_gate, modulation)[c](c)
                    into_h(f"down{f}{c}", 2 if f == 0 else 8, c == 2)

            dve.sem_inc(lo_ready, 2)
            for f in tile_free + misc_free + [parts_used, q_split]:
                dve.sem_inc(f, 1)
            dve.memset(csr[:, :].bitcast(F32), 0.0).then_inc(c_clear, 1)
            dve.wait_ge(c_hi, due(c_hi))
            dve.tensor_tensor(csr4[:, :, 2:4], csil[:, :, :], csr4[:, :, 0:2].bitcast(F32), ALU.subtract).then_inc(c_split, 1)
            dve.wait_ge(c_split, due(c_split))
            own(dve.memset(acc[:, :], 0.0))

            def low_share(s):
                dve.wait_ge(hi_ready, due(hi_ready))
                dve.tensor_tensor(wlo[:, s, POOL_COLS:], raw[:, s, POOL_COLS:], whi[:, s, POOL_COLS:].bitcast(F32), ALU.subtract)\
                    .then_inc(dve_part, 1)

            def first(i, squares, share):
                for k in range(2):
                    slots.misc()
                    if squares:
                        add_square()
                    if share and k == 0:
                        low_share(0)
                for k in range(2):
                    m = misc()
                    dve.tensor_copy(ada0[:, bass.ds((i * 2 + k) * 2, 2), :], mps[:, m.s, 0, 0:4].rearrange("p (a b) -> p a b", b=2))\
                        .then_inc(m.free, 1)
                if share:
                    low_share(1)
                return m

            for k in range(2):
                low_share(k)
            with due.loop("first_a", FIRST_A) as i:
                first(i, False, True)
            with due.loop("first_b", FIRST_B) as i:
                first(i + FIRST_A, True, True)
            m = first(FIRST_A + FIRST_B, True, False)
            dve.sem_inc(sum_ready, 1)
            dve.wait_ge(small_hi, due(small_hi))
            dve.tensor_tensor(sml[:, :], smraw[:, :], smh[:, :].bitcast(F32), ALU.subtract).then_inc(small_split, 1)
            dve.wait_ge(m.free, m.free_at)
            dve.wait_ge(small_split, due(small_split))
            with due.loop("layer", DEPTH) as l:
                dve.wait_ge(par_in, due(par_in, 16))
                own(dve.tensor_tensor(ada[:, 0:16, :], ada0[:, bass.ds(l * 16, 16), :], b_ada[:, 0:16, :], ALU.add))
                modulation(0)
                ffn(0)

                norm(1)
                for c in range(2):
                    t = tile()
                    lo_part(halves(fnl[:, c, :]), tile2(t), halves(fnh[:, c, :]), t.free)
                for c in (0, UP - 1, TL + 1, TL + 2):
                    ins = dve.memset(upad[:, :, c:c + 1], 0.0)
                own(ins)
                for c in range(6):
                    t = slots.tile()
                    dve.wait_ge(conv_in, due(conv_in, 2))
                    dve.wait_ge(t.free, t.free_at)
                    w = prm("conv", 4 * c, 4 * c + 4)
                    for tap, shift in ((1, 1), (0, 0), (2, 2)):
                        for g, a, b in GROUPS:
                            gg = 0 if a == 0 else 1
                            src = upad[:, c % 2, a + shift + 2 * gg:b + shift + 2 * gg]
                            if tap == 1:
                                ins = dve.tensor_scalar(hyx[:, c, a:b], src, w[:, 1:2], w[:, 3:4], ALU.mult, ALU.add)
                            else:
                                ins = dve.scalar_tensor_tensor(out=hyx[:, c, a:b], in0=src, scalar=w[:, tap:tap + 1],
                                                               in1=hyx[:, c, a:b], op0=ALU.mult, op1=ALU.add)
                        if tap != 2:
                            own(ins)
                    ins.then_inc(conv_used, 1)
                    dve.wait_ge(conv_used, due(conv_used))
                for _ in range(4):
                    t = slots.tile()
                dve.sem_inc(v_ready, 1)
                dve.sem_inc(v_ready, 1)

                dve.wait_ge(spilled, due(spilled, 32))
                decay = cst("decay")

                def mlp(n):
                    m, bias = misc(), prm(("b1", "b2")[n])
                    magic, c1 = 1.5 * 2 ** 23, 6.28125
                    F = slice(0, FHID)
                    dve.tensor_scalar(halves(mz2[F, :]), mps[F, m.s, :, 0:TH], bias[F, :], None, ALU.add).then_inc(m.free, 1)
                    dve.wait_ge(m.free, m.free_at)
                    own(dve.tensor_scalar(mk[F, :], mz2[F, :], 1 / (2 * math.pi), magic, ALU.mult, ALU.add))
                    own(dve.tensor_scalar(mk[F, :], mk[F, :], magic, None, ALU.subtract))
                    own(dve.scalar_tensor_tensor(out=mr[F, :], in0=mk[F, :], scalar=-c1, in1=mz2[F, :], op0=ALU.mult, op1=ALU.add))
                    own(dve.scalar_tensor_tensor(out=mr[F, :], in0=mk[F, :], scalar=-(2 * math.pi - c1), in1=mr[F, :],
                                                 op0=ALU.mult, op1=ALU.add))
                    dve.tensor_scalar(mr[F, :], mr[F, :], 3.1415925, -3.1415925, ALU.min, ALU.max).then_inc(sin_in, 1)

                def channels(_):
                    for t in range(5):
                        m = misc()
                        lo_part(fal[:, t, :], mps[:, m.s, 0, :], fah[:, t, :], m.free)

                def tokens(_):
                    for c in range(2):
                        t = tile()
                        lo_part(xl[:, 6 + c, :], flat(tps, t.s)[:, 0:T], xh[:, 6 + c, :], t.free)

                def taps(o):
                    for t in range(5):
                        m = misc()
                        dc = decay[:, t * HYW:(t + 1) * HYW]
                        dve.tensor_tensor(hd[:, t, 0:HYW], mps[:, m.s, 0, 0:HYW], dc, ALU.mult)
                        dve.tensor_tensor(hd[:, t, HYW:], mps[:, m.s, 0, HYW:], dc, ALU.mult).then_inc(m.free, 1)
                        dve.wait_ge(m.free, m.free_at)
                        if t in (0, 4):
                            own(dve.memset(hd[0:1, t, HYW:], 0.0))
                        dve.sem_inc(taps_ready, 1)

                def norms(o):
                    for g in range(2):
                        m = misc()
                        dve.wait_ge(bwd_sum, due(bwd_sum))
                        dve.tensor_tensor(inv[:, g, :], mps[:, m.s, 0, 0:HYW], inv[:, g, :], ALU.add).then_inc(m.free, 1)
                        dve.wait_ge(m.free, m.free_at)
                        own(dve.tensor_scalar(inv[:, g, :], inv[:, g, :], EPS, None, ALU.add))
                        own(dve.reciprocal(inv[:, g, :], inv[:, g, :]))

                def combine(o):
                    for t in range(5):
                        dve.tensor_tensor(pp[:, 0, :], hd[:, t, 0:HYW], hd[:, t, HYW:], ALU.add)
                        own(dve.tensor_tensor(pp[:, 1, :], hd[:, t, 0:HYW], hd[:, t, HYW:], ALU.subtract))
                        iv = inv[:, t // 4, :]
                        dve.tensor_tensor(pp[:, 0, :], pp[:, 0, :], iv, ALU.mult)
                        own(dve.tensor_tensor(pp[:, 1, :], pp[:, 1, :], iv, ALU.mult))
                        hi2 = tmh[:, t, :].rearrange("p (a c) -> p a c", a=3)[:, 0:3:2, :]
                        lo2 = tml[:, t, :].rearrange("p (a c) -> p a c", a=3)[:, 0:3:2, :]
                        own(dve.tensor_copy(hi2, pp[:, :, :]))
                        own(dve.tensor_tensor(lo2, pp[:, :, :], hi2.bitcast(F32), ALU.subtract))
                    dve.sem_inc(filter_ready, 1)

                def turn(o):
                    for t in range(5):
                        m = misc()
                        lo_part(tml[:, t, HYW:2 * HYW], mps[:, m.s, 0, 0:HYW], tmh[:, t, HYW:2 * HYW], m.free)

                def forward(o):
                    for f in range(5):
                        m = misc()
                        dve.wait_ge(parts_out, due(parts_out))
                        ha, ur, us = reb[:, 0:HYW], reb[:, HYW:], mps[:, m.s, 1, 0:HYW]
                        dve.tensor_tensor(pp[:, 0, :], ur, ha, ALU.mult)
                        own(dve.tensor_tensor(pp[:, 1, :], us, hbb[:, :], ALU.mult))
                        own(dve.tensor_tensor(yf[:, 0:HYW], pp[:, 0, :], pp[:, 1, :], ALU.subtract))
                        dve.tensor_tensor(pp[:, 0, :], ur, hbb[:, :], ALU.mult)
                        dve.tensor_tensor(pp[:, 1, :], us, ha, ALU.mult).then_inc(m.free, 1)
                        dve.wait_ge(m.free, m.free_at)
                        dve.tensor_tensor(yf[:, HYW:], pp[:, 0, :], pp[:, 1, :], ALU.add).then_inc(parts_used, 1)
                        dve.wait_ge(parts_used, due(parts_used) + 1)
                        ysl = slice(2 * f, 2 * f + 2)
                        own(dve.tensor_copy(yh[:, ysl, :].rearrange("p a c -> p (a c)"), yf[:, :]))
                        dve.tensor_tensor(yl[:, ysl, :].rearrange("p a c -> p (a c)"), yf[:, :],
                                          yh[:, ysl, :].rearrange("p a c -> p (a c)").bitcast(F32), ALU.subtract)\
                            .then_inc(spec_ready, 1)
                    due(spec_ready, 5)

                def inverse(o):
                    for c in range(2):
                        t = tile()
                        v = hyx[:, 4 + c, :]
                        dve.scalar_tensor_tensor(out=v, in0=v, scalar=prm("skip", 2 * o + c, 2 * o + c + 1),
                                                 in1=flat(tps, t.s)[:, 0:T], op0=ALU.mult, op1=ALU.add).then_inc(t.free, 1)
                        dve.wait_ge(t.free, t.free_at)
                        dve.tensor_tensor(v, v, hyx[:, 2 * o + c, :], ALU.mult).then_inc(v_ready if o == 0 else z_new, 1)
                    if o == 0:
                        dve.wait_ge(v_ready, due(v_ready, 4))

                R, R2 = slice(NOPE, QK), slice(QK, P)
                rope = cst("rope")

                def low_rank(_):
                    for k in range(2):
                        m = slots.misc()
                        dve.wait_ge(rms_out, due(rms_out))
                        dve.reciprocal(ars[:, k, :], ars[:, k, :]).then_inc(m.free, 1)
                        dve.wait_ge(m.free, m.free_at)
                    for k, (src, g) in ((2, (kvr[:, :], prm("kv_g"))), (0, (qa[:, 0, :], prm("q_g", 0, 1))),
                                        (1, (qa[:, 1, :], prm("q_g", 1, 2)))):
                        own(dve.tensor_tensor(art[:, k, :], src, ars[:, 1 if k == 2 else 0, :], ALU.mult))
                        dve.tensor_scalar(art[:, k, :], art[:, k, :], g, None, ALU.mult).then_inc(low_ready, 1)
                        dve.wait_ge(low_ready, due(low_ready))
                        if k == 2:
                            dve.tensor_tensor(krt[R, :], krr[R2, 0:TL], rope[R2, :], ALU.mult)
                            own(dve.tensor_tensor(kro[R, 0:TL], krr[R, 0:TL], rope[R, :], ALU.mult))
                            dve.tensor_tensor(kro[R, 0:TL], kro[R, 0:TL], krt[R, :], ALU.add).then_inc(krope_ready, 1)
                            dve.wait_ge(krope_ready, due(krope_ready))
                    dve.wait_ge(spec_ready, due.now(spec_ready))
                    dve.wait_ge(low_hi, due(low_hi, 8))
                    dve.tensor_tensor(ckl[:, 0:T], art[:, 2, :], ckh[:, 0:T].bitcast(F32), ALU.subtract).then_inc(low_split, 1)
                    dve.tensor_tensor(ckl[:, T:KEYS], prm("ckv"), ckh[:, T:KEYS].bitcast(F32), ALU.subtract).then_inc(low_split, 1)

                steps = dict(mlp=mlp, channels=channels, tokens=tokens, taps=taps, norms=norms, combine=combine,
                             turn=turn, forward=forward, inverse=inverse, low_rank=low_rank)
                for what, o in MIX_ORDER:
                    if what in steps:
                        steps[what](o)

                dve.wait_ge(z_new, due.now(z_new) + 2)
                for k_h, k_l in zip(khs, kls):
                    for a, b, src in ((0, TL, kro[R, 0:TL]), (TL, T, krr[R, TL:T]), (T, KEYS, prm("krope")[R, :])):
                        ins = dve.tensor_tensor(k_l[R, a:b], src, k_h[R, a:b].bitcast(F32), ALU.subtract)
                own(ins)
                dve.wait_ge(low_split, due(low_split, 2))
                dve.sem_inc(low_ready, 1)
                due(low_ready)
                for c in range(2):
                    dve.wait_ge(z_new, due(z_new))
                    lo_part(xl[:, c, :], hyx[:, 4 + c, :], xh[:, c, :], z_split)
                dve.wait_ge(stored, due(stored, 32))
                for k in range(2):
                    dve.wait_ge(low_hi, due(low_hi))
                    dve.tensor_tensor(qnl[:, k, :], art[:, k, :], qnh[:, k, :].bitcast(F32), ALU.subtract).then_inc(low_split, 1)
                due(low_split, 2)
                with due.loop("heads", 2) as i:
                    scored = {}
                    for what, n in HEAD_ORDER:
                        h_, qt, c = n // 5, n % 5, n % 3
                        if what == "Q":
                            t = tile()
                            dve.wait_ge(q_copy, due(q_copy))
                            for bank, c0, c1, t0, t1, g in SEGMENTS[:2]:
                                dve.tensor_tensor(krt[R, t0:t1], tps[R2, t.s, bank, c0:c1], rope[R2, t0:t1], ALU.mult)
                            for bank, c0, c1, t0, t1, g in SEGMENTS[:2]:
                                ins = dve.tensor_tensor(qf[R, t0:t1], tps[R, t.s, bank, c0:c1], rope[R, t0:t1], ALU.mult)
                            ins.then_inc(t.free, 1)
                            dve.wait_ge(t.free, t.free_at)
                            dve.tensor_tensor(qf[R, 0:TL], qf[R, 0:TL], krt[R, :], ALU.add).then_inc(q_roped, 1)
                            dve.wait_ge(q_roped, due(q_roped))
                        elif what == "K":
                            m = misc()
                            lo_part(halves(kls[n % 2][0:NOPE, :]), mps[0:NOPE, m.s, :, 0:KEYS // 2],
                                    halves(khs[n % 2][0:NOPE, :]), m.free)
                        elif what == "QS":
                            lo_part(ql[0:QK, n % 2, :], qf[0:QK, :], qh[0:QK, n % 2, :], q_split)
                        elif what == "V":
                            m = misc()
                            lo_part(halves(vl[:, :]), mps[:, m.s, :, 0:KEYS // 2], halves(vh[:, :]), m.free)
                        elif what == "S":
                            scored[n] = m = misc()
                            w = TL + PAST if qt < 4 else TC
                            own(dve.tensor_reduce(stat[:, c:c + 1], flat(mps, m.s)[:, 0:w], AX.X, ALU.max))
                            dve.tensor_scalar(stat[:, 3 + c:4 + c], stat[:, c:c + 1], -QK ** -0.5, None, ALU.mult)\
                                .then_inc(prob_in, 1)
                        elif what == "N":
                            m = scored[n]
                            w = TL + PAST if qt < 4 else TC
                            dve.wait_ge(m.free, m.free_at)
                            own(dve.reciprocal(stat[:, c:c + 1], stat[:, 6 + c:7 + c]))
                            p = probs(n)[:, 0:w]
                            dve.tensor_scalar(p, p, stat[:, c:c + 1], None, ALU.mult).then_inc(prob_ready, 1)
                        elif what == "T":
                            t = tile()
                            if qt < 4:
                                out, hi = [x_[:, 0:5 * TL].rearrange("p (a t) -> p a t", a=5)[:, :, qt * P:(qt + 1) * P]
                                           for x_ in (ptl, pth)]
                                lo_part(out, flat(tps, t.s)[:, 0:T].rearrange("p (a t) -> p a t", a=5), hi, t.free)
                            else:
                                lo_part(ptl[:, 5 * TL:], tps[:, t.s, 0, 0:TC], pth[:, 5 * TL:], t.free)
                        elif what == "P":
                            t = tile()
                            rows = slice((n % 2) * VD, (n % 2 + 1) * VD)
                            kk = bass.ds(i * 2 + (2 + n // 2), 1)
                            lo_part(xl[rows, kk, :].rearrange("p a t -> p (a t)"), flat(tps, t.s)[rows, 0:T],
                                    xh[rows, kk, :].rearrange("p a t -> p (a t)"), t.free)
                        elif what == "A":
                            slots.misc()
                        elif what == "B":
                            ada_b(i * (ADA_HEADS // 2) + (ADA_FIRST + ADA_UP + n))
                for n in range(ADA_BACK):
                    slots.misc()
                    if n % 2:
                        for k in (n - 1, n):
                            m = ada_b(ADA_FIRST + ADA_UP + ADA_HEADS + k)
                            dve.wait_ge(m.free, m.free_at)
                modulation(2)
                half_gate(2)

                with due.loop("gate", KT) as i:
                    gates = [slots.tile() for _ in range(3)]
                    y = yc[:, bass.ds(i, 1), :].rearrange("p a t -> p (a t)")
                    for b in range(3):
                        t = tile()
                        dve.wait_ge(gates[b].free, gates[b].free_at)
                        dve.tensor_tensor(halves(y if b == 0 else prod[:, :]), halves(sgm[:, b, :]), tile2(t), ALU.mult)\
                            .then_inc(t.free, 1)
                        dve.wait_ge(t.free, t.free_at)
                        if b:
                            own(dve.tensor_tensor(y, y, prod[:, :], ALU.add))
                dve.sem_inc(y_done, 1)
                for k in range(KT):
                    lo_part(nl[:, k, :], yc[:, k, :], nh[:, k, :], n_ready, hi_out)
                dve.wait_ge(n_ready, due(n_ready, KT))
                into_h("out", 5, True)
                ffn(1)

            inv_rms()
            fg = cst("final_g")
            for k in range(KT):
                dve.scalar_tensor_tensor(out=h[:, k, :], in0=h[:, k, :], scalar=fg[:, k:k + 1], in1=rr[:, :],
                                         op0=ALU.mult, op1=ALU.mult).then_inc(y_ready, 1)


def transform_tables():
    def odd(n, scale=1.0):
        a = np.pi * np.outer(np.arange(n), np.arange(n) + 0.5) / n
        return np.cos(a) * scale, np.sin(a) * scale

    def whole(n, scale):
        a = 2 * np.pi * (np.outer(np.arange(n), np.arange(n)) % n) / n
        return np.cos(a) * scale, np.sin(a) * scale

    def panel(m):
        return m.reshape(4, P, 512).transpose(1, 0, 2).reshape(P, PANEL)

    c, s = odd(TL)
    fc, fs = whole(TL, (TL * 64) ** -0.5)
    tables = np.stack([panel(m) for m in (c, s, c.T / TL, s.T / TL, fc, -fs)])
    cc, cs = odd(TC)
    c64, s64 = whole(64, 1.0)
    z = np.zeros((64, 64))
    bd = [np.block([[m, z], [z, m]]) for m in (c64, s64)]
    gc, gs = whole(TC, (TC * 64) ** -0.5)
    small = np.concatenate([cc, cs, cc.T / TC, cs.T / TC] + bd + [gc, -gs], axis=1)
    return tables.astype(np.float32), small.astype(np.float32)


def filter_features(n):
    t = np.arange(n, dtype=np.float32)
    tn = t / np.float32(n - 1)
    w = np.float32(2.0 * math.pi) * t / np.float32(n)
    bands = np.linspace(1e-4, NB - 1, NB, dtype=np.float32)
    a = (w[:, None] * bands[None, :]).astype(np.float32)
    f = np.concatenate([tn[:, None], np.cos(a), -np.sin(a)], axis=1)
    deltas = np.linspace(math.log(1e-2) / 1.5, math.log(1e-2) / 0.3, HYW, dtype=np.float32)
    return f.astype(np.float32), np.exp(-tn[:, None] * np.abs(deltas)[None, :]).astype(np.float32)


def constants():
    cst = np.zeros((P, NCST), np.float32)

    def put(name, a):
        cst[:a.shape[0], CST[name][0]:CST[name][0] + a.shape[1]] = a

    (f1, d1), (f2, d2) = filter_features(TL), filter_features(TC)
    put("decay", np.concatenate([d1[t * P:(t + 1) * P] for t in range(4)] + [d2], axis=1))
    n_freq = ROPE // 4
    inv = (10000.0 ** (-np.arange(n_freq, dtype=np.float32) / n_freq)).astype(np.float32)
    tok = np.arange(TL)
    ang = [(tok // GRID_W)[:, None] * inv[None], (tok % GRID_W)[:, None] * inv[None]]
    cos = np.concatenate([np.cos(a) for a in ang for _ in range(2)], axis=1)
    sin = np.concatenate([sg * np.sin(a) for a in ang for sg in (-1, 1)], axis=1)
    rope = np.zeros((P, TL), np.float32)
    rope[NOPE:QK], rope[QK:] = cos.T, sin.T
    put("rope", rope)
    put("ident", np.eye(P, dtype=np.float32))
    put("ones", np.ones((P, P), np.float32))
    put("sel", np.array([[1, 0], [0, 1], [1, 0], [0, 1]], np.float32))
    put("eps", np.full((P, 1), EPS, np.float32))
    feats = np.zeros((P, T), np.float32)
    feats[:17, :TL], feats[:17, TL:] = f1.T, f2.T
    return cst, feats


def blocks(w):
    k, m = w.shape
    return w.reshape(k // P, P, m // P, P).transpose(0, 2, 1, 3)


def as_panel(bs):
    return np.concatenate(bs, axis=1)


def feature_major(a):
    return np.ascontiguousarray(a.T.reshape(-1, P, a.shape[0]).transpose(1, 0, 2))


def lay_out(inp):
    f = np.float32
    swap = np.concatenate([np.arange(8, 16), np.arange(8), np.arange(24, 32), np.arange(16, 24)])
    w = inp["w_ada"].reshape(DEPTH, KT, P, 36, 256).transpose(0, 3, 2, 1, 4)
    w_first, w_ada = w[:, :ADA_FIRST].reshape(-1, P, PANEL), w[:, ADA_FIRST:].reshape(-1, P, PANEL)
    up = inp["w_ffn_up"].reshape(DEPTH, 2, KT, P, 2, HT, P)
    w_up = up.transpose(0, 1, 5, 3, 4, 2, 6).reshape(DEPTH * 2 * HT, P, PANEL)
    down, at = [], 0
    for n in CHUNKS:
        d = inp["w_ffn_down"][:, :, at * P:(at + n) * P].reshape(DEPTH, 2, n, P, 4, 2, P)
        down.append(d.transpose(0, 1, 4, 3, 5, 2, 6).reshape(DEPTH, 2, 4, P, 2 * n * P))
        at += n
    w_down8 = np.stack(down[:2], axis=2).reshape(DEPTH * 2 * 8, P, PANEL)
    w_down6 = down[2].reshape(DEPTH * 2 * 4, P, 2 * 6 * P)
    w_mix, w_qkv, w_gate, w_out, par = [], [], [], [], []
    for l in range(DEPTH):
        w = inp["w_in"][l]
        zero = np.zeros((D, NOPE), f)
        kr = w[:, 1152:1184]
        cols = [w[:, 1184:1440], w[:, 0:768], w[:, 768:1152], np.concatenate([zero, kr, kr[:, swap]], axis=1)]
        b = blocks(np.concatenate(cols, axis=1))
        w_mix += [as_panel([b[k, m] for m in (2 * i, 2 * i + 1) for k in range(KT)]) for i in range(6)]
        qb, kvb = inp["w_qb"][l].reshape(2, P, HEADS, QK), inp["w_kvb"][l].reshape(P, HEADS, NOPE + VD)
        for i in range(4):
            hs = (2 * i, 2 * i + 1)
            bs = [np.concatenate([qb[k, :, hh], qb[k, :, hh, NOPE:][:, swap]], axis=1) for hh in hs for k in range(2)]
            bs += [np.concatenate([kvb[:, hh, :NOPE], np.zeros((P, P - NOPE), f)], axis=1) for hh in hs]
            bs += [np.concatenate([kvb[:, hh, NOPE:] for hh in hs], axis=1)]
            w_qkv.append(as_panel(bs))
        g = blocks(w[:, 1440:])
        ys = [blocks(inp[n][l]) for n in ("w_hy_out", "w_mla_o", "w_fnet")]
        for m in range(KT):
            w_gate.append(as_panel([g[k, b_ * KT + m] for b_ in range(2) for k in range(KT)]))
            w_gate.append(as_panel([g[k, 2 * KT + m] for k in range(KT)] + [y[k, m] for y in ys for k in range(y.shape[0])]))
        wo = blocks(inp["w_out"][l])
        w_out += [as_panel([wo[k, m] for m in (2 * i, 2 * i + 1) for k in range(KT)]) for i in range(4)]
        p = np.zeros((P, NPAR), f)

        def put(name, a, row=0):
            p[row:row + a.shape[0], PAR[name][0]:PAR[name][0] + a.shape[1]] = a

        put("b_ada", np.repeat(inp["b_ada"][l].reshape(72, P).T, 2, axis=1))
        put("norm_g", np.repeat(inp["norm_g"][l].reshape(24, P).T, 2, axis=1))
        cw = np.concatenate([inp["hy_conv_w"][l], inp["hy_conv_b"][l][None]], axis=0)
        put("conv", cw.reshape(4, 6, P).transpose(2, 1, 0).reshape(P, 24))
        put("skip", inp["hy_skip"][l].reshape(4, P).T)
        put("q_g", inp["q_norm_g"][l].reshape(2, P).T)
        put("kv_g", inp["kv_norm_g"][l].reshape(1, P).T)
        put("b1", inp["hy_filt_b1"][l][:, None])
        put("b2", inp["hy_filt_b2"][l][:, None])
        put("w1", inp["hy_filt_w1"][l])
        put("w2", inp["hy_filt_w2"][l])
        put("ckv", inp["cache_ckv"][0, l].T)
        put("krope", inp["cache_krope"][0, l].T, NOPE)
        w3 = inp["hy_filt_w3"][l].reshape(FHID, 2, 2, HYW)
        put("w3", w3.transpose(0, 2, 1, 3).reshape(FHID, 4 * HYW))
        par.append(p)
    x = np.concatenate([inp["x_sample"][0], inp["x_prompt"][0]], axis=0)
    cv = np.stack([inp["c"][0], inp["c_ctx"]], axis=0)
    tables, small = transform_tables()
    cst, feats = constants()
    for k in range(KT):
        cst[:, CST["final_g"][0] + k] = inp["final_g"][k * P:(k + 1) * P]
    out = dict(x=feature_major(x), w_first=w_first, w_ada=w_ada, w_up=w_up, w_down8=w_down8, w_down6=w_down6, w_mix=np.stack(w_mix),
               w_qkv=np.stack(w_qkv), w_gate=np.stack(w_gate), w_out=np.stack(w_out), tables=tables, small=small, cst=cst,
               cvec=feature_major(cv), feats=feats, par=np.stack(par + par[:1]))
    return {k: np.ascontiguousarray(v, dtype=f) for k, v in out.items()}


OUTS = [("y", (P, KT, T)), ("ckv", (DEPTH, P, TC)), ("krope", (DEPTH, ROPE, TC))]


def build(nc, arrays, per_pass):
    a = {n: nc.dram_tensor(f"in_{n}", v.shape, F32, kind="ExternalInput").ap() for n, v in arrays.items()}
    o = {n: nc.dram_tensor(f"out_{n}", s, F32, kind="ExternalOutput").ap() for n, s in OUTS}
    program(nc, per_pass, a["x"], a["w_first"], a["w_ada"], a["w_up"], (a["w_down8"], a["w_down6"]), a["w_mix"], a["w_qkv"], a["w_gate"],
            a["w_out"], a["tables"], a["small"], a["cst"], a["cvec"], a["feats"], a["par"], o["y"], o["ckv"], o["krope"])


def kernel(**inputs):
    import concourse.bacc as _bacc
    from concourse.bass_utils import run_bass_kernel_spmd as _run

    arrays = lay_out({k: np.asarray(v) for k, v in inputs.items()})
    per_pass = {}
    for _ in range(2):
        nc = _bacc.Bacc("TRN2", target_bir_lowering=False, num_devices=1)
        build(nc, arrays, per_pass)
    r = _run(nc, [{f"in_{n}": v for n, v in arrays.items()}], core_ids=[0]).results[0]
    y = r["out_y"].transpose(1, 0, 2).reshape(D, T).T
    ckv, krope = r["out_ckv"].transpose(0, 2, 1), r["out_krope"].transpose(0, 2, 1)
    return (np.ascontiguousarray(y[None, TL:]), np.ascontiguousarray(y[None, :TL]), np.ascontiguousarray(ckv[None]),
            np.ascontiguousarray(krope[None]))
```
